# Optimizing a Trainium2 kernel written in Bass

```python
import math
import jax, jax.numpy as jnp
from jax import lax
import numpy as np

D_MODEL = 1024
BATCH = 1
SEQ = 256
DEPTH = 2

HEAD_DIM = 64
HEADS_A = 8
HEADS_B = 8
HEADS_C = 8
WIDTH = HEADS_A * HEAD_DIM
N_BRANCH = 3
ROPE_DIM = HEAD_DIM // 4
ROPE_THETA = 500000.0
MOBA_BLOCK = 256
MOBA_TOPK = 3
MOBA_Q_CHUNK = 32
IDX_HEADS = 8
IDX_DIM = 64
DSA_TOPK_MAX = 256
Q_BLOCK = 128
RMS_EPS = 1e-6

SECTION_SIZES = (
    WIDTH, WIDTH, WIDTH, WIDTH,
    WIDTH, WIDTH, WIDTH, WIDTH,
    WIDTH, WIDTH, WIDTH, WIDTH,
    IDX_HEADS * IDX_DIM, IDX_DIM, IDX_HEADS,
    HEADS_C,
    N_BRANCH * D_MODEL,
)
D_IN = sum(SECTION_SIZES)
SPLIT_POINTS = tuple(int(v) for v in np.cumsum(SECTION_SIZES)[:-1])


def rms_norm(x, gain):
    xf = x.astype(jnp.float32)
    y = xf * lax.rsqrt(jnp.mean(xf * xf, axis=-1, keepdims=True) + RMS_EPS)
    return (y * gain.astype(jnp.float32)).astype(x.dtype)

def rope_partial(t, pos):
    half = ROPE_DIM // 2
    inv_freq = jnp.power(jnp.float32(ROPE_THETA), -jnp.arange(0, ROPE_DIM, 2, dtype=jnp.float32) / ROPE_DIM)
    ang = pos.astype(jnp.float32)[:, None] * inv_freq[None, :]
    cos = jnp.cos(ang)[None, :, None, :]
    sin = jnp.sin(ang)[None, :, None, :]
    tr = t[..., :ROPE_DIM].astype(jnp.float32)
    t1, t2 = tr[..., :half], tr[..., half:]
    rot = jnp.concatenate([t1 * cos - t2 * sin, t2 * cos + t1 * sin], axis=-1).astype(t.dtype)
    return jnp.concatenate([rot, t[..., ROPE_DIM:]], axis=-1)

def moba_attention(q, k, v):
    B, S, H, d = q.shape
    n_blk = -(-S // MOBA_BLOCK)
    pad = n_blk * MOBA_BLOCK - S
    kp = jnp.pad(k, ((0, 0), (0, pad), (0, 0), (0, 0)))
    vp = jnp.pad(v, ((0, 0), (0, pad), (0, 0), (0, 0)))
    kb = kp.reshape(B, n_blk, MOBA_BLOCK, H, d).transpose(0, 3, 1, 2, 4)
    vb = vp.reshape(B, n_blk, MOBA_BLOCK, H, d).transpose(0, 3, 1, 2, 4)
    k_mean = jnp.mean(kb, axis=3)
    qh = q.transpose(0, 2, 1, 3)
    k_sel = min(MOBA_TOPK, n_blk - 1)
    scale = d ** -0.5
    bi = jnp.arange(B)[:, None, None, None]
    hi = jnp.arange(H)[None, :, None, None]

    def chunk(ci):
        start = ci * MOBA_Q_CHUNK
        qc = lax.dynamic_slice_in_dim(qh, start, MOBA_Q_CHUNK, axis=2)
        qpos = start + jnp.arange(MOBA_Q_CHUNK)
        own = start // MOBA_BLOCK
        k_own = lax.dynamic_index_in_dim(kb, own, axis=2, keepdims=False)
        v_own = lax.dynamic_index_in_dim(vb, own, axis=2, keepdims=False)
        kpos_own = own * MOBA_BLOCK + jnp.arange(MOBA_BLOCK)
        s_own = jnp.einsum('bhqd,bhkd->bhqk', qc, k_own).astype(jnp.float32) * scale
        s_own = jnp.where(kpos_own[None, :] <= qpos[:, None], s_own, -jnp.inf)
        if k_sel == 0:
            p = jax.nn.softmax(s_own, axis=-1).astype(v.dtype)
            return jnp.einsum('bhqk,bhkd->bhqd', p, v_own)
        gate = jnp.einsum('bhqd,bhnd->bhqn', qc, k_mean).astype(jnp.float32)
        gate = jnp.where((jnp.arange(n_blk) < own)[None, None, None, :], gate, -jnp.inf)
        gval, gidx = lax.top_k(gate, k_sel)
        ok = gval > -jnp.inf
        k_g = kb[bi, hi, gidx]
        v_g = vb[bi, hi, gidx]
        s_past = jnp.einsum('bhqd,bhqnkd->bhqnk', qc, k_g).astype(jnp.float32) * scale
        s_past = jnp.where(ok[..., None], s_past, -jnp.inf)
        s_past = s_past.reshape(B, H, MOBA_Q_CHUNK, k_sel * MOBA_BLOCK)
        p = jax.nn.softmax(jnp.concatenate([s_past, s_own], axis=-1), axis=-1).astype(v.dtype)
        p_past = p[..., :k_sel * MOBA_BLOCK].reshape(B, H, MOBA_Q_CHUNK, k_sel, MOBA_BLOCK)
        p_own = p[..., k_sel * MOBA_BLOCK:]
        return (jnp.einsum('bhqnk,bhqnkd->bhqd', p_past, v_g)
                + jnp.einsum('bhqk,bhkd->bhqd', p_own, v_own))

    out = lax.map(chunk, jnp.arange(S // MOBA_Q_CHUNK))
    return out.transpose(1, 0, 3, 2, 4).reshape(B, S, H, d)

def dsa_attention(q, k, v, q_idx, k_idx, w_idx):
    B, S, H, d = q.shape
    top = min(DSA_TOPK_MAX, S // 4)
    scale = d ** -0.5
    bi = jnp.arange(B)[:, None, None]
    kpos = jnp.arange(S)

    def chunk(ci):
        start = ci * Q_BLOCK
        qpos = start + jnp.arange(Q_BLOCK)
        qi = lax.dynamic_slice_in_dim(q_idx, start, Q_BLOCK, axis=1)
        wi = lax.dynamic_slice_in_dim(w_idx, start, Q_BLOCK, axis=1)
        rel = jax.nn.relu(jnp.einsum('bqhd,bsd->bqhs', qi, k_idx))
        isc = jnp.einsum('bqh,bqhs->bqs', wi, rel).astype(jnp.float32)
        isc = jnp.where(kpos[None, None, :] <= qpos[None, :, None], isc, -jnp.inf)
        ival, idx = lax.top_k(isc, top)
        ok = ival > -jnp.inf
        k_g = k[bi, idx]
        v_g = v[bi, idx]
        qc = lax.dynamic_slice_in_dim(q, start, Q_BLOCK, axis=1)
        s = jnp.einsum('bqhd,bqkhd->bhqk', qc, k_g).astype(jnp.float32) * scale
        s = jnp.where(ok[:, None], s, -jnp.inf)
        p = jax.nn.softmax(s, axis=-1).astype(v.dtype)
        return jnp.einsum('bhqk,bqkhd->bqhd', p, v_g)

    out = lax.map(chunk, jnp.arange(S // Q_BLOCK))
    return out.transpose(1, 0, 2, 3, 4).reshape(B, S, H, d)

def forgetting_attention(q, k, v, log_f):
    B, S, H, d = q.shape
    scale = d ** -0.5
    csum = jnp.cumsum(log_f, axis=1).transpose(0, 2, 1)
    qh = q.transpose(0, 2, 1, 3)
    kh = k.transpose(0, 2, 1, 3)
    vh = v.transpose(0, 2, 1, 3)
    kpos = jnp.arange(S)

    def chunk(ci):
        start = ci * Q_BLOCK
        qpos = start + jnp.arange(Q_BLOCK)
        qc = lax.dynamic_slice_in_dim(qh, start, Q_BLOCK, axis=2)
        cq = lax.dynamic_slice_in_dim(csum, start, Q_BLOCK, axis=2)
        s = jnp.einsum('bhqd,bhkd->bhqk', qc, kh).astype(jnp.float32) * scale
        s = s + (cq[..., :, None] - csum[:, :, None, :])
        s = jnp.where(kpos[None, :] <= qpos[:, None], s, -jnp.inf)
        p = jax.nn.softmax(s, axis=-1).astype(v.dtype)
        return jnp.einsum('bhqk,bhkd->bhqd', p, vh)

    out = lax.map(chunk, jnp.arange(S // Q_BLOCK))
    return out.transpose(1, 0, 3, 2, 4).reshape(B, S, H, d)

def hybrid_layer(x, gain, w_in, f_bias, w_branch, w_out):
    B, S, _ = x.shape
    pos = jnp.arange(S)
    h = rms_norm(x, gain)
    proj = jnp.einsum('bsd,de->bse', h, w_in)
    (qa, ka, va, ga, qb, kb_, vb_, gb, qc, kc, vc, gc,
     q_idx, k_idx, w_idx, f_logit, merge_logit) = jnp.split(proj, SPLIT_POINTS, axis=-1)

    def heads(t, n):
        return t.reshape(B, S, n, HEAD_DIM)

    oa = moba_attention(rope_partial(heads(qa, HEADS_A), pos), rope_partial(heads(ka, HEADS_A), pos),
                        heads(va, HEADS_A)).reshape(B, S, WIDTH) * jax.nn.silu(ga)
    qi = rope_partial(q_idx.reshape(B, S, IDX_HEADS, IDX_DIM), pos)
    ki = rope_partial(k_idx[:, :, None, :], pos)[:, :, 0, :]
    wi = w_idx * (IDX_HEADS ** -0.5 * IDX_DIM ** -0.5)
    ob = dsa_attention(rope_partial(heads(qb, HEADS_B), pos), rope_partial(heads(kb_, HEADS_B), pos),
                       heads(vb_, HEADS_B), qi, ki, wi).reshape(B, S, WIDTH) * jax.nn.silu(gb)
    log_f = jax.nn.log_sigmoid((f_logit + f_bias).astype(jnp.float32))
    oc = forgetting_attention(heads(qc, HEADS_C), heads(kc, HEADS_C), heads(vc, HEADS_C),
                              log_f).reshape(B, S, WIDTH) * jax.nn.silu(gc)

    y = jnp.einsum('nbsw,nwd->bsnd', jnp.stack([oa, ob, oc], axis=0), w_branch)
    gates = jax.nn.sigmoid(merge_logit).reshape(B, S, N_BRANCH, D_MODEL)
    merged = jnp.sum(gates * y, axis=2)
    return x + jnp.einsum('bsd,de->bse', merged, w_out)

def first_inputs(seed: int = 0) -> dict:
    key = jax.random.key(seed)
    ks = jax.random.split(key, 8)
    x = jax.random.normal(ks[0], (BATCH, SEQ, D_MODEL), jnp.float32)
    norm_gain = 1.0 + 0.05 * jax.random.normal(ks[1], (DEPTH, D_MODEL), jnp.float32)
    w_in = jax.random.normal(ks[2], (DEPTH, D_MODEL, D_IN), jnp.float32) * D_MODEL ** -0.5
    forget_bias = 3.0 + 0.5 * jax.random.normal(ks[3], (DEPTH, HEADS_C), jnp.float32)
    w_branch = jax.random.normal(ks[4], (DEPTH, N_BRANCH, WIDTH, D_MODEL), jnp.float32) * WIDTH ** -0.5
    w_out = jax.random.normal(ks[5], (DEPTH, D_MODEL, D_MODEL), jnp.float32) * (0.5 * D_MODEL ** -0.5)
    final_gain = 1.0 + 0.05 * jax.random.normal(ks[6], (D_MODEL,), jnp.float32)
    return {"x": x, "norm_gain": norm_gain, "w_in": w_in, "forget_bias": forget_bias,
            "w_branch": w_branch, "w_out": w_out, "final_gain": final_gain}

def first_block(x, norm_gain, w_in, forget_bias, w_branch, w_out, final_gain):
    h = x
    for layer in range(DEPTH):
        h = hybrid_layer(h, norm_gain[layer], w_in[layer], forget_bias[layer],
                         w_branch[layer], w_out[layer])
    return rms_norm(h, final_gain)


CTX_LEN = 256
GRID_W = 64
D_FF = 2816
N_MOD = 9
EPS = 1e-6
ROPE_BASE = 10000.0
MLA_HEADS = 8
MLA_NOPE = 64
MLA_ROPE = 32
MLA_V = 64
MLA_Q_LORA = 384
MLA_KV_LORA = 256
CONV_CH = 512
CONV_WIDTH = 31
GQA_HEADS = 8
GQA_KV_HEADS = 2
NA_HEADS = 8
WIN_H = 8
WIN_W = 16

EVEN_KV_COLS = MLA_KV_LORA + MLA_ROPE
EVEN_CONV_OFF = EVEN_KV_COLS + MLA_Q_LORA
EVEN_COLS = EVEN_CONV_OFF + 2 * CONV_CH
GQA_KV_W = GQA_KV_HEADS * HEAD_DIM
GQA_Q_W = GQA_HEADS * HEAD_DIM
NA_W = NA_HEADS * HEAD_DIM
ODD_KV_COLS = 2 * GQA_KV_W + 2 * NA_W
ODD_COLS = ODD_KV_COLS + GQA_Q_W + NA_W
MIX_OUT = MLA_HEADS * MLA_V + CONV_CH


def rms_norm_2(x, g):
    xf = x.astype(jnp.float32)
    y = xf * lax.rsqrt(jnp.mean(xf * xf, axis=-1, keepdims=True) + EPS)
    return (y * g.astype(jnp.float32)).astype(x.dtype)

def layer_norm(x, g, b):
    xf = x.astype(jnp.float32)
    mu = jnp.mean(xf, axis=-1, keepdims=True)
    var = jnp.mean(jnp.square(xf - mu), axis=-1, keepdims=True)
    y = (xf - mu) * lax.rsqrt(var + EPS)
    return (y * g.astype(jnp.float32) + b.astype(jnp.float32)).astype(x.dtype)

def axial_rope_table(n_tokens, dim):
    t = jnp.arange(n_tokens)
    row = (t // GRID_W).astype(jnp.float32)
    col = (t % GRID_W).astype(jnp.float32)
    n_pairs = dim // 4
    inv = ROPE_BASE ** (-jnp.arange(n_pairs, dtype=jnp.float32) / n_pairs)
    ang = jnp.concatenate([row[:, None] * inv, col[:, None] * inv], axis=-1)
    return jnp.cos(ang), jnp.sin(ang)

def apply_rope(x, cos, sin):
    xp = x.reshape(*x.shape[:-1], x.shape[-1] // 2, 2)
    x1, x2 = xp[..., 0], xp[..., 1]
    cs = cos[None, :, None, :].astype(x.dtype)
    sn = sin[None, :, None, :].astype(x.dtype)
    return jnp.stack([x1 * cs - x2 * sn, x1 * sn + x2 * cs], axis=-1).reshape(x.shape)

def _attend(q, k, v):
    scale = q.shape[-1] ** -0.5
    s = jnp.einsum('bqhgd,bkhd->bhgqk', q, k).astype(jnp.float32) * scale
    p = jax.nn.softmax(s, axis=-1).astype(v.dtype)
    return jnp.einsum('bhgqk,bkhd->bqhgd', p, v)

def context_attention(q, k, v):
    B, L, Hk, G, _ = q.shape
    return _attend(q, k, v).reshape(B, L, Hk * G, v.shape[-1])

def latent_attention(q, k, v, k_ctx, v_ctx):
    B, S, Hk, G, d = q.shape
    k_all = jnp.concatenate([k_ctx, k], axis=1)
    v_all = jnp.concatenate([v_ctx, v], axis=1)
    qb = q.reshape(B, S // Q_BLOCK, Q_BLOCK, Hk, G, d).transpose(1, 0, 2, 3, 4, 5)
    o = lax.map(lambda qi: _attend(qi, k_all, v_all), qb)
    return o.transpose(1, 0, 2, 3, 4, 5).reshape(B, S, Hk * G, v.shape[-1])

def neighbourhood_attention(q, k, v, k_ctx, v_ctx, rpb):
    B, S, H, d = q.shape
    rows = S // GRID_W
    kh = min(WIN_H, rows)
    scale = d ** -0.5
    qg = q.reshape(B, rows, GRID_W, H, d).transpose(1, 0, 2, 3, 4)
    kg = k.reshape(B, rows, GRID_W, H, d)
    vg = v.reshape(B, rows, GRID_W, H, d)
    col = jnp.arange(GRID_W)
    cs = jnp.clip(col - WIN_W // 2, 0, GRID_W - WIN_W)
    col_idx = cs[:, None] + jnp.arange(WIN_W)[None, :]
    dc = col_idx - col[:, None] + (WIN_W - 1)
    n_ctx = k_ctx.shape[1]

    def row_block(args):
        r, q_r = args
        rs = jnp.clip(r - kh // 2, 0, rows - kh)
        k_rows = lax.dynamic_slice_in_dim(kg, rs, kh, axis=1)
        v_rows = lax.dynamic_slice_in_dim(vg, rs, kh, axis=1)
        k_nb = k_rows[:, :, col_idx]
        v_nb = v_rows[:, :, col_idx]
        s_nb = jnp.einsum('bqhd,bjqwhd->bhqjw', q_r, k_nb).astype(jnp.float32) * scale
        dr = rs + jnp.arange(kh) - r + (WIN_H - 1)
        bias = rpb[:, dr[None, :, None], dc[:, None, :]]
        s_nb = (s_nb + bias[None].astype(jnp.float32)).reshape(B, H, GRID_W, kh * WIN_W)
        s_ctx = jnp.einsum('bqhd,bkhd->bhqk', q_r, k_ctx).astype(jnp.float32) * scale
        p = jax.nn.softmax(jnp.concatenate([s_ctx, s_nb], axis=-1), axis=-1).astype(v.dtype)
        p_ctx = p[..., :n_ctx]
        p_nb = p[..., n_ctx:].reshape(B, H, GRID_W, kh, WIN_W)
        return (jnp.einsum('bhqk,bkhd->bqhd', p_ctx, v_ctx)
                + jnp.einsum('bhqjw,bjqwhd->bqhd', p_nb, v_nb))

    o = lax.map(row_block, (jnp.arange(rows), qg))
    return o.transpose(1, 0, 2, 3, 4).reshape(B, S, H, d)

def swiglu(h, w_in, w_out):
    g, u = jnp.split(h @ w_in, 2, axis=-1)
    return (jax.nn.silu(g) * u) @ w_out

def conv_module(u, prm):
    u = u + prm["conv_glu_b"]
    a, g = jnp.split(u, 2, axis=-1)
    y = a * jax.nn.sigmoid(g)
    y = lax.conv_general_dilated(
        y, prm["conv_dw_w"][:, None, :].astype(y.dtype), window_strides=(1,),
        padding=[(CONV_WIDTH // 2, CONV_WIDTH // 2)],
        dimension_numbers=("NWC", "WIO", "NWC"), feature_group_count=CONV_CH) + prm["conv_dw_b"]
    y = layer_norm(y, prm["conv_ln_g"], prm["conv_ln_b"])
    return jax.nn.silu(y)

def mla_kv(pp, prm, rope):
    B, L, _ = pp.shape
    ckv = rms_norm_2(pp[..., :MLA_KV_LORA], prm["mla_kv_norm"])
    kvu = (ckv @ prm["mla_w_ukv"]).reshape(B, L, MLA_HEADS, MLA_NOPE + MLA_V)
    k_nope = rms_norm_2(kvu[..., :MLA_NOPE], prm["mla_k_gain"][:MLA_NOPE])
    v = kvu[..., MLA_NOPE:]
    k_rope = rms_norm_2(pp[..., MLA_KV_LORA:EVEN_KV_COLS], prm["mla_k_gain"][MLA_NOPE:])[:, :, None, :]
    if rope is not None:
        k_rope = apply_rope(k_rope, *rope)
    k = jnp.concatenate([k_nope, jnp.broadcast_to(k_rope, (B, L, MLA_HEADS, MLA_ROPE))], axis=-1)
    return k, v

def mla_q(pp, prm, rope):
    B, L, _ = pp.shape
    cq = rms_norm_2(pp[..., EVEN_KV_COLS:EVEN_CONV_OFF], prm["mla_q_norm"])
    q = (cq @ prm["mla_w_uq"]).reshape(B, L, MLA_HEADS, MLA_NOPE + MLA_ROPE)
    q_nope = rms_norm_2(q[..., :MLA_NOPE], prm["mla_q_gain"][:MLA_NOPE])
    q_rope = rms_norm_2(q[..., MLA_NOPE:], prm["mla_q_gain"][MLA_NOPE:])
    if rope is not None:
        q_rope = apply_rope(q_rope, *rope)
    return jnp.concatenate([q_nope, q_rope], axis=-1)[:, :, :, None, :]

def even_mixer(hl, hc, prm, ctx_out, ropes):
    rope_mla, _ = ropes
    B, S, _ = hl.shape
    pl = hl @ prm["w_in"]
    pc = hc @ (prm["w_in"] if ctx_out else prm["w_in"][:, :EVEN_KV_COLS])
    k_l, v_l = mla_kv(pl, prm, rope_mla)
    k_c, v_c = mla_kv(pc, prm, None)
    att_l = latent_attention(mla_q(pl, prm, rope_mla), k_l, v_l, k_c, v_c).reshape(B, S, -1)
    conv_l = conv_module(pl[..., EVEN_CONV_OFF:], prm)
    ol = jnp.concatenate([att_l, conv_l], axis=-1) @ prm["w_out"]
    oc = None
    if ctx_out:
        Bc, Lc, _ = hc.shape
        att_c = context_attention(mla_q(pc, prm, None), k_c, v_c).reshape(Bc, Lc, -1)
        conv_c = conv_module(pc[..., EVEN_CONV_OFF:], prm)
        oc = jnp.concatenate([att_c, conv_c], axis=-1) @ prm["w_out"]
    return ol, oc

def odd_kv(pp, prm, rope):
    B, L, _ = pp.shape
    o1, o2, o3 = GQA_KV_W, 2 * GQA_KV_W, 2 * GQA_KV_W + NA_W
    ck = rms_norm_2(pp[..., :o1].reshape(B, L, GQA_KV_HEADS, HEAD_DIM), prm["gqa_k_gain"])
    if rope is not None:
        ck = apply_rope(ck, *rope)
    cv = pp[..., o1:o2].reshape(B, L, GQA_KV_HEADS, HEAD_DIM)
    nk = rms_norm_2(pp[..., o2:o3].reshape(B, L, NA_HEADS, HEAD_DIM), prm["na_k_gain"])
    nv = pp[..., o3:ODD_KV_COLS].reshape(B, L, NA_HEADS, HEAD_DIM)
    return ck, cv, nk, nv

def odd_q(pp, prm, rope):
    B, L, _ = pp.shape
    cq = rms_norm_2(pp[..., ODD_KV_COLS:ODD_KV_COLS + GQA_Q_W].reshape(B, L, GQA_HEADS, HEAD_DIM), prm["gqa_q_gain"])
    if rope is not None:
        cq = apply_rope(cq, *rope)
    cq = cq.reshape(B, L, GQA_KV_HEADS, GQA_HEADS // GQA_KV_HEADS, HEAD_DIM)
    nq = rms_norm_2(pp[..., ODD_KV_COLS + GQA_Q_W:].reshape(B, L, NA_HEADS, HEAD_DIM), prm["na_q_gain"])
    return cq, nq

def odd_mixer(hl, hc, prm, ctx_out, ropes):
    _, rope_hd = ropes
    B, S, _ = hl.shape
    pl = hl @ prm["w_in"]
    pc = hc @ (prm["w_in"] if ctx_out else prm["w_in"][:, :ODD_KV_COLS])
    ck_l, cv_l, nk_l, nv_l = odd_kv(pl, prm, rope_hd)
    ck_c, cv_c, nk_c, nv_c = odd_kv(pc, prm, None)
    cq_l, nq_l = odd_q(pl, prm, rope_hd)
    gqa_l = latent_attention(cq_l, ck_l, cv_l, ck_c, cv_c).reshape(B, S, -1)
    na_l = neighbourhood_attention(nq_l, nk_l, nv_l, nk_c, nv_c, prm["na_rpb"]).reshape(B, S, -1)
    ol = jnp.concatenate([gqa_l, na_l], axis=-1) @ prm["w_out"]
    oc = None
    if ctx_out:
        Bc, Lc, _ = hc.shape
        cq_c, nq_c = odd_q(pc, prm, None)
        gqa_c = context_attention(cq_c, ck_c, cv_c).reshape(Bc, Lc, -1)
        na_c = context_attention(nq_c[:, :, :, None, :], nk_c, nv_c).reshape(Bc, Lc, -1)
        oc = jnp.concatenate([gqa_c, na_c], axis=-1) @ prm["w_out"]
    return ol, oc

def adaln(cond, prm):
    mod = jax.nn.silu(cond) @ prm["mod_w"] + prm["mod_b"]
    return jnp.split(mod, N_MOD, axis=-1)

def modulate(h, shift, scale):
    return h * (1.0 + scale) + shift

def trunk_layer(xl, xc, c, c_ctx, prm, even, ctx_out, ropes):
    mod_l = adaln(c[:, None, :], prm)
    mod_c = adaln(c_ctx[None, None, :], prm)

    def half_ffn(x, m, name):
        sh, sc, g = m
        h = modulate(rms_norm_2(x, prm[name + "_norm"]), sh, sc)
        return x + 0.5 * g * swiglu(h, prm[name + "_w_in"], prm[name + "_w_out"])

    xl = half_ffn(xl, mod_l[0:3], "ffn1")
    xc = half_ffn(xc, mod_c[0:3], "ffn1")
    hl = modulate(rms_norm_2(xl, prm["mix_norm"]), mod_l[3], mod_l[4])
    hc = modulate(rms_norm_2(xc, prm["mix_norm"]), mod_c[3], mod_c[4])
    mixer = even_mixer if even else odd_mixer
    ol, oc = mixer(hl, hc, prm, ctx_out, ropes)
    xl = xl + mod_l[5] * ol
    xl = half_ffn(xl, mod_l[6:9], "ffn2")
    if ctx_out:
        xc = xc + mod_c[5] * oc
        xc = half_ffn(xc, mod_c[6:9], "ffn2")
    return xl, xc

def _layer_params(key, i):
    ks = iter(jax.random.split(key, 32))

    def nrm(shape, scale):
        return jax.random.normal(next(ks), shape, jnp.float32) * scale

    def gain(n):
        return 1.0 + 0.02 * jax.random.normal(next(ks), (n,), jnp.float32)

    D = D_MODEL
    pre = f"l{i}_"
    p = {}
    p[pre + "mod_w"] = nrm((D, N_MOD * D), 0.5 * D ** -0.5)
    p[pre + "mod_b"] = nrm((N_MOD * D,), 0.02)
    p[pre + "ffn1_norm"] = gain(D)
    p[pre + "ffn1_w_in"] = nrm((D, 2 * D_FF), D ** -0.5)
    p[pre + "ffn1_w_out"] = nrm((D_FF, D), D_FF ** -0.5)
    p[pre + "mix_norm"] = gain(D)
    if i % 2 == 0:
        p[pre + "w_in"] = nrm((D, EVEN_COLS), D ** -0.5)
        p[pre + "mla_q_norm"] = gain(MLA_Q_LORA)
        p[pre + "mla_w_uq"] = nrm((MLA_Q_LORA, MLA_HEADS * (MLA_NOPE + MLA_ROPE)), MLA_Q_LORA ** -0.5)
        p[pre + "mla_kv_norm"] = gain(MLA_KV_LORA)
        p[pre + "mla_w_ukv"] = nrm((MLA_KV_LORA, MLA_HEADS * (MLA_NOPE + MLA_V)), MLA_KV_LORA ** -0.5)
        p[pre + "mla_q_gain"] = gain(MLA_NOPE + MLA_ROPE)
        p[pre + "mla_k_gain"] = gain(MLA_NOPE + MLA_ROPE)
        p[pre + "conv_glu_b"] = nrm((2 * CONV_CH,), 0.02)
        p[pre + "conv_dw_w"] = nrm((CONV_WIDTH, CONV_CH), CONV_WIDTH ** -0.5)
        p[pre + "conv_dw_b"] = nrm((CONV_CH,), 0.02)
        p[pre + "conv_ln_g"] = gain(CONV_CH)
        p[pre + "conv_ln_b"] = nrm((CONV_CH,), 0.02)
    else:
        p[pre + "w_in"] = nrm((D, ODD_COLS), D ** -0.5)
        p[pre + "gqa_q_gain"] = gain(HEAD_DIM)
        p[pre + "gqa_k_gain"] = gain(HEAD_DIM)
        p[pre + "na_q_gain"] = gain(HEAD_DIM)
        p[pre + "na_k_gain"] = gain(HEAD_DIM)
        p[pre + "na_rpb"] = nrm((NA_HEADS, 2 * WIN_H - 1, 2 * WIN_W - 1), 0.1)
    p[pre + "w_out"] = nrm((MIX_OUT, D), MIX_OUT ** -0.5)
    p[pre + "ffn2_norm"] = gain(D)
    p[pre + "ffn2_w_in"] = nrm((D, 2 * D_FF), D ** -0.5)
    p[pre + "ffn2_w_out"] = nrm((D_FF, D), D_FF ** -0.5)
    return p

def second_inputs(seed: int = 0) -> dict:
    key = jax.random.key(seed)
    k_x, k_c, k_ctx, k_cc, k_layers = jax.random.split(key, 5)
    inputs = {
        "x": jax.random.normal(k_x, (BATCH, SEQ, D_MODEL), jnp.float32),
        "c": jax.random.normal(k_c, (BATCH, D_MODEL), jnp.float32),
        "ctx": jax.random.normal(k_ctx, (BATCH, CTX_LEN, D_MODEL), jnp.float32),
        "c_ctx": jax.random.normal(k_cc, (D_MODEL,), jnp.float32),
    }
    layer_keys = jax.random.split(k_layers, DEPTH)
    for i in range(DEPTH):
        inputs.update(_layer_params(layer_keys[i], i))
    return inputs

def second_block(x, c, ctx, c_ctx,
              l0_mod_w, l0_mod_b, l0_ffn1_norm, l0_ffn1_w_in, l0_ffn1_w_out, l0_mix_norm, l0_w_in,
              l0_mla_q_norm, l0_mla_w_uq, l0_mla_kv_norm, l0_mla_w_ukv, l0_mla_q_gain, l0_mla_k_gain,
              l0_conv_glu_b, l0_conv_dw_w, l0_conv_dw_b, l0_conv_ln_g, l0_conv_ln_b,
              l0_w_out, l0_ffn2_norm, l0_ffn2_w_in, l0_ffn2_w_out,
              l1_mod_w, l1_mod_b, l1_ffn1_norm, l1_ffn1_w_in, l1_ffn1_w_out, l1_mix_norm, l1_w_in,
              l1_gqa_q_gain, l1_gqa_k_gain, l1_na_q_gain, l1_na_k_gain, l1_na_rpb,
              l1_w_out, l1_ffn2_norm, l1_ffn2_w_in, l1_ffn2_w_out):
    layers = (
        dict(mod_w=l0_mod_w, mod_b=l0_mod_b, ffn1_norm=l0_ffn1_norm, ffn1_w_in=l0_ffn1_w_in,
             ffn1_w_out=l0_ffn1_w_out, mix_norm=l0_mix_norm, w_in=l0_w_in,
             mla_q_norm=l0_mla_q_norm, mla_w_uq=l0_mla_w_uq, mla_kv_norm=l0_mla_kv_norm,
             mla_w_ukv=l0_mla_w_ukv, mla_q_gain=l0_mla_q_gain, mla_k_gain=l0_mla_k_gain,
             conv_glu_b=l0_conv_glu_b, conv_dw_w=l0_conv_dw_w, conv_dw_b=l0_conv_dw_b,
             conv_ln_g=l0_conv_ln_g, conv_ln_b=l0_conv_ln_b, w_out=l0_w_out,
             ffn2_norm=l0_ffn2_norm, ffn2_w_in=l0_ffn2_w_in, ffn2_w_out=l0_ffn2_w_out),
        dict(mod_w=l1_mod_w, mod_b=l1_mod_b, ffn1_norm=l1_ffn1_norm, ffn1_w_in=l1_ffn1_w_in,
             ffn1_w_out=l1_ffn1_w_out, mix_norm=l1_mix_norm, w_in=l1_w_in,
             gqa_q_gain=l1_gqa_q_gain, gqa_k_gain=l1_gqa_k_gain, na_q_gain=l1_na_q_gain,
             na_k_gain=l1_na_k_gain, na_rpb=l1_na_rpb, w_out=l1_w_out,
             ffn2_norm=l1_ffn2_norm, ffn2_w_in=l1_ffn2_w_in, ffn2_w_out=l1_ffn2_w_out),
    )
    S = x.shape[1]
    ropes = (axial_rope_table(S, MLA_ROPE), axial_rope_table(S, HEAD_DIM))
    xl, xc = x, ctx
    for i in range(DEPTH):
        xl, xc = trunk_layer(xl, xc, c, c_ctx, layers[i], even=(i % 2 == 0),
                             ctx_out=(i < DEPTH - 1), ropes=ropes)
    return xl


def setup_inputs(seed=0):
    out = dict(first_inputs(seed))
    for name, value in second_inputs(seed + 1).items():
        if name != "x":
            out[name + "_2"] = value
    return out


def reference(
    x, norm_gain, w_in, forget_bias, w_branch, w_out, final_gain, c_2, ctx_2, c_ctx_2,
    l0_mod_w_2, l0_mod_b_2, l0_ffn1_norm_2, l0_ffn1_w_in_2, l0_ffn1_w_out_2, l0_mix_norm_2,
    l0_w_in_2, l0_mla_q_norm_2, l0_mla_w_uq_2, l0_mla_kv_norm_2, l0_mla_w_ukv_2,
    l0_mla_q_gain_2, l0_mla_k_gain_2, l0_conv_glu_b_2, l0_conv_dw_w_2, l0_conv_dw_b_2,
    l0_conv_ln_g_2, l0_conv_ln_b_2, l0_w_out_2, l0_ffn2_norm_2, l0_ffn2_w_in_2, l0_ffn2_w_out_2,
    l1_mod_w_2, l1_mod_b_2, l1_ffn1_norm_2, l1_ffn1_w_in_2, l1_ffn1_w_out_2, l1_mix_norm_2,
    l1_w_in_2, l1_gqa_q_gain_2, l1_gqa_k_gain_2, l1_na_q_gain_2, l1_na_k_gain_2, l1_na_rpb_2,
    l1_w_out_2, l1_ffn2_norm_2, l1_ffn2_w_in_2, l1_ffn2_w_out_2,
):
    x = first_block(
        x, norm_gain, w_in, forget_bias, w_branch, w_out, final_gain,
    )
    return second_block(
        x, c_2, ctx_2, c_ctx_2, l0_mod_w_2, l0_mod_b_2, l0_ffn1_norm_2, l0_ffn1_w_in_2,
        l0_ffn1_w_out_2, l0_mix_norm_2, l0_w_in_2, l0_mla_q_norm_2, l0_mla_w_uq_2,
        l0_mla_kv_norm_2, l0_mla_w_ukv_2, l0_mla_q_gain_2, l0_mla_k_gain_2, l0_conv_glu_b_2,
        l0_conv_dw_w_2, l0_conv_dw_b_2, l0_conv_ln_g_2, l0_conv_ln_b_2, l0_w_out_2,
        l0_ffn2_norm_2, l0_ffn2_w_in_2, l0_ffn2_w_out_2, l1_mod_w_2, l1_mod_b_2, l1_ffn1_norm_2,
        l1_ffn1_w_in_2, l1_ffn1_w_out_2, l1_mix_norm_2, l1_w_in_2, l1_gqa_q_gain_2,
        l1_gqa_k_gain_2, l1_na_q_gain_2, l1_na_k_gain_2, l1_na_rpb_2, l1_w_out_2,
        l1_ffn2_norm_2, l1_ffn2_w_in_2, l1_ffn2_w_out_2,
    )


_drawn_inputs = setup_inputs


def setup_inputs(seed=0):
    import zlib

    import numpy as np

    out = dict(_drawn_inputs(seed))
    spreads = {}
    factors = {'norm_gain': 3.953,
     'l0_mod_b_2': 3.499,
     'l0_ffn1_norm_2': 8.0,
     'l0_mix_norm_2': 8.0,
     'l0_mla_q_norm_2': 8.0,
     'l0_mla_w_uq_2': 3.094,
     'l0_mla_kv_norm_2': 8.0,
     'l0_mla_q_gain_2': 8.0,
     'l0_mla_k_gain_2': 8.0,
     'l0_conv_glu_b_2': 28.393,
     'l0_conv_dw_b_2': 27.893,
     'l0_conv_ln_g_2': 36.499,
     'l0_conv_ln_b_2': 41.616,
     'l0_ffn2_norm_2': 8.0,
     'l1_mod_b_2': 4.111,
     'l1_ffn1_norm_2': 8.0,
     'l1_mix_norm_2': 8.0,
     'l1_gqa_q_gain_2': 8.0,
     'l1_gqa_k_gain_2': 21.458,
     'l1_na_q_gain_2': 8.0,
     'l1_na_k_gain_2': 23.554,
     'l1_na_rpb_2': 64.0,
     'l1_ffn2_norm_2': 32.73}
    for name, (base, spread) in spreads.items():
        noise = np.random.default_rng([zlib.crc32(name.encode()), seed]).standard_normal(out[name].shape)
        drawn = base * np.exp(spread * noise) if base else spread * noise
        out[name] = __import__('jax').numpy.asarray(drawn.astype(out[name].dtype))
    for name, factor in factors.items():
        out[name] = (out[name] * factor).astype(out[name].dtype)
    return out
```

```python
from contextlib import ExitStack, contextmanager

import numpy as np

import concourse.bass as bass
from concourse import mybir
from concourse.alu_op_type import AluOpType as ALU

ACT = mybir.ActivationFunctionType
F32 = mybir.dt.float32
AX_X = mybir.AxisListType.X

P = 128
D = 1024
KD = D // P
SEQ = 256
CTX = 256
TOK = SEQ + CTX
QT = SEQ // P
HD = 64
HEADS = 8
WIDTH = HEADS * HD
KW = WIDTH // P
D_FF = 2816
KF = D_FF // P
N_MOD = 9
MT = N_MOD * KD
TAPS = 31
PAD = TAPS // 2
YW = SEQ + 2 * PAD
TOP = 64
EPS = 1e-6
BLOCKED = -1e30
TAKEN = -3e38
SLOTS = 4
SLOT = KF * P
BANKS = 8
ROTATING = 6
BANK = 512



def weight_plan():
    plan = []
    for l in range(2):
        for br in range(3):
            for part in "qkvg":
                plan.append((f"b1.{l}.{part}{br}", 2, KD * 256))
        plan += [(f"b1.{l}.qi", 2, KD * 256), (f"b1.{l}.misc", 1, KD * 144)]
        plan += [("mod0", 18, KD * 256)]
        plan += [(f"b1.{l}.merge", 12, KD * 256), (f"b1.{l}.branch", 6, KW * 512), (f"b1.{l}.out", 4, KD * 256)]
    for l in range(2):
        plan += [(f"b2.{l}.ffn1_in", 22, KD * 256), (f"b2.{l}.ffn1_out", 8, SLOT)]
        if l == 0:
            plan += [("b2.0.in", 7, KD * 256), ("b2.0.uq", 1, 3 * 768), ("b2.0.ukv", 1, 2 * 1024)]
            plan += [("mod1", 36, KD * 256)]
        else:
            plan += [("b2.1.in", 9, KD * 256)]
        plan += [(f"b2.{l}.out", 4, KD * 256)]
        plan += [(f"b2.{l}.ffn2_in", 22, KD * 256), (f"b2.{l}.ffn2_out", 8, SLOT)]
    return plan


LOOPED = {s: (n % SLOTS + SLOTS if n % SLOTS else 0, n // SLOTS - bool(n % SLOTS)) for s, n, _ in weight_plan() if ".ffn" in s}



def columns(items):
    at, out = 0, {}
    for name, n in items:
        out[name] = (at, n)
        at += n
    return out, at


CONST, N_CONST = columns([
    ("ident", P), ("ones", P), ("sum64", P), ("sum32", P), ("rot_half", P), ("rot_pair", P), ("rot_q", P), ("sum96", P),
    ("cos_part", 512), ("sin_part", 512), ("cos64", 256), ("sin64", 256), ("cos32", 256), ("sin32", 256), ("cos96", 256), ("sin96", 256),
    ("causal", 512), ("window", 512), ("upto", 512), ("eps", 1), ("one", 1)])
PARAM, N_PARAM = columns(
    [(f"b1.{l}.gain", KD) for l in range(2)] + [(f"b1.{l}.fbias", 16) for l in range(2)] + [("final", KD)]
    + [(f"b2.{l}.mod_b", 2 * MT) for l in range(2)]
    + [(f"b2.{l}.{n}", 2 * KD) for l in range(2) for n in ("ffn1_norm", "mix_norm", "ffn2_norm")]
    + [("q_norm", 3), ("kv_norm", 2), ("q_gain", 1), ("k_gain", 1),
       ("glu_b", 8), ("dw_w", 4 * TAPS), ("dw_b", 4), ("ln_g", 4), ("ln_b", 4),
       ("gq_gain", 1), ("gk_gain", 1), ("nq_gain", 1), ("nk_gain", 1), ("cond", 2 * KD)])


SEMAPHORES = (
    "attended", "combined", "copied", "exponentiated", "ffn_multiplied", "gated",
    "hidden_written", "mixer_added", "modulation_copied", "modulation_multiplied", "multiplied", "normed",
    "partnered", "probs_ready", "projected", "rooted", "roped", "scales_prepared",
    "shifted", "squared", "summed")


class Book:

    def __init__(self, before=None):
        self.before = before
        self.labels, self.strides, self.turns, self.banks = {}, {}, {}, {}


class Engine:

    def __init__(self, book, sems):
        self.book, self.sems = book, sems
        self.count = {}
        self.loop_name = self.turn = self.last = self.next_label = None
        self.seen = {}

    def step(self, sem, label=None):
        n = self.count[sem.name] = self.count.get(sem.name, 0) + 1
        self.last = (sem.name, n, self.loop_name)
        for name in (label, self.next_label):
            if name is not None:
                assert name not in self.book.labels, name
                self.book.labels[name] = self.last
        self.next_label = None
        if self.loop_name is None:
            return n
        return self.turn * self.stride(self.loop_name, sem.name) + n

    def name_last(self, label):
        self.book.labels[label] = self.last

    def name_next(self, label):
        self.next_label = label

    def stride(self, loop, sem):
        return self.book.before.strides[loop, sem] if self.book.before else 1

    def at(self, label, shift=0, it=None):
        sem, n, loop = self.book.before.labels[label]
        if loop is None:
            return self.sems[sem], n
        stride = self.stride(loop, sem)
        if it is None and loop == self.loop_name:
            return self.sems[sem], self.turn * stride + (n + shift * stride)
        return self.sems[sem], n + (self.book.before.turns[loop] - 1 if it is None else it) * stride

    def new(self, label, shift=0, it=None):
        if self.book.before is None:
            return False
        sem, n, loop = self.book.before.labels[label]
        if self.loop_name is not None:
            return loop == self.loop_name or self.seen.get(sem, 0) < n
        value = self.at(label, shift, it)[1]
        if self.seen.get(sem, 0) >= value:
            return False
        self.seen[sem] = value
        return True

    @contextmanager
    def loop(self, engine, name, turns, first=0):
        before = dict(self.count)
        with engine.Fori(first, turns) as self.turn:
            self.loop_name = name
            yield self.turn
        self.loop_name = None
        self.book.turns[name] = turns
        for sem, n in self.count.items():
            stride = n - before.get(sem, 0)
            self.book.strides[name, sem] = stride
            self.count[sem] = before.get(sem, 0) + stride * (turns - first)

    def bank(self, label):
        return self.book.before.banks[label] if self.book.before else 0


def program(nc, book, weights, d_const, d_param, d_onehot, d_x, d_ctx, d_bias, d_out):
    plan = weight_plan()
    stage_of, start = [], {}
    for s, n, w in plan:
        start.setdefault(s, []).append(len(stage_of))
        stage_of += [s] * n
    width = {s: w for s, _, w in plan}

    with ExitStack() as ctx:
        def sb(name, shape):
            return ctx.enter_context(nc.sbuf_tensor(name, shape, F32))

        wring = sb("wring", [P, SLOTS, SLOT])
        cst = sb("cst", [P, N_CONST])
        prm = sb("prm", [P, N_PARAM])
        x = sb("x", [P, KD, TOK])
        h = sb("h", [P, KD, TOK])
        squares = sb("squares", [P, 4, BANK])
        rs = sb("rs", [P, BANK])
        work = sb("work", [P, 2, BANK])
        probs = sb("probs", [P, 3, BANK])
        probsT = sb("probsT", [P, 2, BANK])
        stat = sb("stat", [P, 4, 8])
        csil = sb("csil", [P, KD, 2])
        mods = sb("mods", [P, 2, MT, 2])
        mscale = sb("mscale", [P, KD, 2])
        ARENA = 21200
        arena = sb("arena", [P, ARENA])
        psum = ctx.enter_context(nc.psum_tensor("psum", [P, BANKS, BANK], F32))
        sems = {n: ctx.enter_context(nc.semaphore(n)) for n in SEMAPHORES}
        (attended, combined, copied, exponentiated, ffn_multiplied, gated,
         hidden_written, mixer_added, modulation_copied, modulation_multiplied, multiplied, normed,
         partnered, probs_ready, projected, rooted, roped, scales_prepared,
         shifted, squared, summed) = sems.values()
        landed = [ctx.enter_context(nc.semaphore(f"weights_landed{i}")) for i in range(SLOTS)]
        s_const = ctx.enter_context(nc.semaphore("constants_landed"))
        s_x = ctx.enter_context(nc.semaphore("x_landed"))
        s_ctx = ctx.enter_context(nc.semaphore("context_landed"))
        s_onehot = ctx.enter_context(nc.semaphore("onehot_landed"))
        s_bias = ctx.enter_context(nc.semaphore("bias_landed"))
        s_out = ctx.enter_context(nc.semaphore("output_written"))

        def C(name):
            at, n = CONST[name]
            return cst[:, at:at + n]

        def R(name, i=0, n=None):
            at, m = PARAM[name]
            return prm[:, at + i:at + (m if n is None else i + n)]

        class Space:

            def __init__(self):
                self.at = 0

            def take(self, *shape):
                n = int(np.prod(shape))
                v = arena[:, self.at:self.at + n]
                self.at += n
                assert self.at <= ARENA, self.at
                if len(shape) == 2:
                    v = v.rearrange("p (a b) -> p a b", a=shape[0])
                if len(shape) == 3:
                    v = v.rearrange("p (a b c) -> p a b c", a=shape[0], b=shape[1])
                return v

        s1 = Space()
        qT = [s1.take(KW, SEQ) for _ in range(3)]
        kT = [s1.take(KW, SEQ) for _ in range(3)]
        vv = [s1.take(QT, WIDTH) for _ in range(3)]
        gg = [s1.take(KW, SEQ) for _ in range(3)]
        qiT = s1.take(KW, SEQ)
        kiT = s1.take(SEQ)
        onehot = s1.take(1024)
        merged = s1.take(KD, SEQ)
        oT = [s1.take(KW, SEQ) for _ in range(3)]
        isc = s1.take(QT, SEQ)
        dsa_mask = s1.take(QT, SEQ)
        wl = s1.take(QT, 16)
        fz = s1.take(4, 16)
        csT = s1.take(SEQ)
        cq = s1.take(QT, 8)
        top8 = s1.take(8)
        gates = arena[:, 0:3 * KD * SEQ].rearrange("p (a b) -> p a b", a=3 * KD)
        assert 3 * KD * SEQ <= 6 * KW * SEQ

        hid = Space().take(KF, TOK)

        s2 = Space()
        m_ckv = s2.take(2, TOK)
        m_cq = s2.take(3, TOK)
        m_q = s2.take(HEADS, TOK)
        m_k = s2.take(HEADS, TOK)
        m_kr = s2.take(TOK)
        m_v = s2.take(4, WIDTH)
        m_ca = s2.take(4, TOK)
        m_y = s2.take(4, 2, YW)
        m_yc = m_ca
        m_o = h

        s3 = Space()
        g_ck = s3.take(TOK)
        g_cv = s3.take(4, P)
        g_nk = s3.take(4, TOK)
        g_nv = s3.take(4, WIDTH)
        g_cq = s3.take(4, SEQ)
        g_nq = s3.take(4, SEQ)
        g_o = h[:, :, 0:SEQ]
        g_bias = s3.take(2 * HEADS, SEQ)

        def flat(v):
            return v.rearrange("p a b -> p (a b)")

        def slot_of(c):
            return wring[:, c % SLOTS, :]

        def used(c):
            s = stage_of[c]
            k = c - max(a for a in start[s] if a <= c)
            if s in LOOPED and k >= LOOPED[s][0]:
                k -= LOOPED[s][0]
                return f"w{c - k + k % SLOTS}", k // SLOTS
            return f"w{c}", None

        def units_of(kind, l=0):
            out = []
            if kind in ("moba", "dsa", "fox"):
                br = ("moba", "dsa", "fox").index(kind)
                for hh in range(HEADS):
                    rows = slice(HD * (hh % 2), HD * (hh % 2) + HD)
                    mms = [(qT[br][rows, hh // 2, P * g:P * g + P], kT[br][rows, hh // 2, :]) for g in range(QT)]
                    out.append(dict(
                        G=QT, K=SEQ, mms=mms, kind=kind, head=hh, scale=HD ** -0.5 if kind != "fox" else 1.0,
                        v=[vv[br][:, t, HD * hh:HD * hh + HD] for t in range(2)], half=hh % 2,
                        cols=(0, SEQ), last=hh % 2 == 1, dst=oT[br][:, hh // 2, :], gate=gg[br][:, hh // 2, :]))
            if kind == "mla_lat":
                for hh in range(HEADS):
                    for q in range(QT):
                        out.append(dict(
                            G=1, K=TOK, kind="none", scale=96 ** -0.5, half=hh % 2, head=hh,
                            mms=[(m_q[0:96, hh, P * q:P * q + P], m_k[0:96, hh, :])],
                            v=[m_v[:, t, HD * hh:HD * hh + HD] for t in range(4)], cols=(P * q, P),
                            last=hh % 2 == 1 and q == 1, dst=m_o[:, hh // 2, 0:SEQ], gate=None))
            if kind == "mla_ctx":
                for hh in range(HEADS):
                    out.append(dict(
                        G=2, K=CTX, kind="none", scale=96 ** -0.5, half=hh % 2, head=hh,
                        mms=[(m_q[0:96, hh, SEQ + P * q:SEQ + P * q + P], m_k[0:96, hh, SEQ:TOK]) for q in range(2)],
                        v=[m_v[:, t, HD * hh:HD * hh + HD] for t in (2, 3)], cols=(0, CTX),
                        last=hh % 2 == 1, dst=m_o[:, hh // 2, SEQ:TOK], gate=None))
            if kind == "gqa":
                for j in range(4):
                    for kv in range(2):
                        rows = slice(HD * kv, HD * kv + HD)
                        for q in range(QT):
                            out.append(dict(
                                G=1, K=TOK, kind="none", scale=HD ** -0.5, half=kv, head=j,
                                mms=[(g_cq[rows, j, P * q:P * q + P], g_ck[rows, :])],
                                v=[g_cv[:, t, HD * kv:HD * kv + HD] for t in range(4)], cols=(P * q, P),
                                last=kv == 1 and q == 1, dst=g_o[:, j, :], gate=None))
            if kind == "na":
                for hh in range(HEADS):
                    rows = slice(HD * (hh % 2), HD * (hh % 2) + HD)
                    for q in range(QT):
                        out.append(dict(
                            G=1, K=TOK, kind="na", scale=1.0, half=hh % 2, head=hh, q=q,
                            mms=[(g_nq[rows, hh // 2, P * q:P * q + P], g_nk[rows, hh // 2, :])],
                            v=[g_nv[:, t, HD * hh:HD * hh + HD] for t in range(4)], cols=(P * q, P),
                            last=hh % 2 == 1 and q == 1, dst=g_o[:, 4 + hh // 2, :], gate=None))
            return out

        MOD_EARLY = 24
        ATT = {}
        for l in range(2):
            ATT[f"b1.{l}.att"] = [u for k in ("moba", "dsa", "fox") for u in units_of(k)]
        ATT["b2.0.att"] = units_of("mla_lat") + units_of("mla_ctx")
        ATT["b2.1.att"] = units_of("gqa") + units_of("na")
        FILL = {"b1.0.att": (0, 0, 18), "b1.1.att": (0, 18, 36), "b2.0.att": (1, MOD_EARLY, 36)}

        def fill_at(nm, t):
            if nm not in FILL:
                return []
            l, a, b = FILL[nm]
            steps = len(ATT[nm]) + 3
            return [(l, c) for c in range(a, b) if (c - a) * steps // (b - a) == t]

        XR = {"b1.0": None, "b1.1": "b1.0.out.x3", "final": "b1.1.out.x3",
              "b2.0.n1": "final.h7", "b2.0.nm": "b2.0.ffn1_out.x3", "b2.0.n2": "b2.0.out.x3",
              "b2.1.n1": "b2.0.ffn2_out.x3", "b2.1.nm": "b2.1.ffn1_out.x3", "b2.1.n2": "b2.1.out.x3"}
        NORM_N = {nm: SEQ if nm in ("b1.0", "b1.1", "final", "b2.1.n2") else TOK for nm in XR}

        def heads_ready(nm, u):
            if nm.startswith("b1"):
                return nm.replace("att", "cs'") if u["kind"] == "fox" else nm.replace("att", "rki'")
            return "b2.0.heads.kr_copied" if nm == "b2.0.att" else "b2.1.heads.nqh.n3"

        def mixed_ready(nm, k):
            if nm == "b2.0":
                return f"b2.0.att.o{16 + 2 * k + 1}" if k < 4 else f"b2.0.conv.o{k - 4}"
            return f"b2.1.att.o{4 * k + 3}"

        def head_norms(nm):
            out = []

            def one(name, tiles, total, mat, count, gains, ready, rope=None):
                out.append(dict(name=f"{nm}.{name}", tiles=tiles, total=total, mat=mat, count=count, gains=gains,
                                ready=ready, rope=rope))
            if nm == "b2.0.lora":
                one("ckv", [m_ckv[:, t, :] for t in range(2)], True, "ones", 256, [R("kv_norm", t, 1) for t in range(2)],
                    ["b2.0.in.e0", "b2.0.in.e1"])
                one("kr", [m_kr], False, "sum32", 32, [R("k_gain")], ["b2.0.in.e2"], ("cos32", "sin32"))
                one("cq", [m_cq[:, t, :] for t in range(3)], True, "ones", 384, [R("q_norm", t, 1) for t in range(3)],
                    ["b2.0.in.e3", "b2.0.in.e4", "b2.0.in.e5"])
            if nm == "b2.0.heads":
                one("q", [m_q[0:96, t, :] for t in range(HEADS)], False, "sum96", 1, [R("q_gain")[0:96, :]] * HEADS,
                    [f"b2.0.uq.{t}'" for t in range(HEADS)], ("cos96", "sin96"))
                one("k", [m_k[0:64, t, :] for t in range(HEADS)], False, "sum96", 1, [R("k_gain")[0:64, :]] * HEADS,
                    [f"b2.0.ukv.{t}'" for t in range(HEADS)])
            if nm == "b2.1.heads":
                one("ck", [g_ck], False, "sum64", 64, [R("gk_gain")], ["b2.1.in.e0"], ("cos64", "sin64"))
                one("nk", [g_nk[:, t, :] for t in range(4)], False, "sum64", 64, [R("nk_gain")] * 4,
                    [f"b2.1.in.e{1 + t}" for t in range(4)])
                one("cqh", [g_cq[:, t, :] for t in range(4)], False, "sum64", 64, [R("gq_gain")] * 4,
                    [f"b2.1.cq.e{t // 2}" for t in range(4)], ("cos64", "sin64"))
                one("nqh", [g_nq[:, t, :] for t in range(4)], False, "sum64", 64, [R("nq_gain")] * 4,
                    [f"b2.1.nq.e{t // 2}" for t in range(4)])
            return out

        block = ctx.enter_context(nc.Block())

        @block.sync
        def _(sp):
            E = Engine(book, sems)
            sp.dma_start(cst[:, :], d_const).then_inc(s_const, 16)
            sp.dma_start(prm[:, :], d_param).then_inc(s_const, 16)
            sp.dma_start(x[:, :, 0:SEQ], d_x).then_inc(s_x, 16)
            sp.dma_start(onehot, d_onehot).then_inc(s_onehot, 16)
            for c, s in enumerate(stage_of):
                first = max(a for a in start[s] if a <= c)
                k = c - first
                w = width[s]
                n_chunks = len(stage_of)
                base = k + sum(n for (s2_, n, _), a in zip(plan, np.cumsum([0] + [n for _, n, _ in plan])[:-1])
                               if s2_ == s and a < first)
                lead, turns = LOOPED.get(s, (n_chunks, 0))
                if k >= lead + SLOTS:
                    if k > lead + SLOTS:
                        continue
                    with E.loop(sp, s, turns, first=1) as it:
                        for u in range(SLOTS):
                            if E.new(f"w{first + lead + u}", shift=-1):
                                sp.wait_ge(*E.at(f"w{first + lead + u}", shift=-1))
                            sp.dma_start(slot_of(first + lead + u)[:, 0:w],
                                         weights[s][bass.ds(it * SLOTS + (lead + u), 1), :, :].rearrange("a p w -> (a p) w"))\
                              .then_inc(landed[(first + lead + u) % SLOTS], 16)
                    continue
                if c >= SLOTS:
                    label, turn = used(c - SLOTS)
                    if E.new(label, it=turn):
                        sp.wait_ge(*E.at(label, it=turn))
                sp.dma_start(slot_of(c)[:, 0:w], weights[s][base, :, :]).then_inc(landed[c % SLOTS], 16)
                if s == "b1.0.q0" and k == 1:
                    sp.dma_start(x[:, :, SEQ:TOK], d_ctx).then_inc(s_ctx, 16)
                if s == "b2.1.in" and k == 8:
                    if E.new("b2.1.ffn1_out.x3"):
                        sp.wait_ge(*E.at("b2.1.ffn1_out.x3"))
                    for r in range(4):
                        for hh in range(HEADS):
                            q, part = divmod(r, 2)
                            sp.dma_start(
                                g_bias[HD * part:HD * part + HD, 2 * hh + q, :].rearrange("c (j k) -> c j k", j=4),
                                d_bias[hh, 7 - r:11 - r, :, :].rearrange("j c k -> c j k")).then_inc(s_bias, 16)
            if E.new("last.h7"):
                sp.wait_ge(*E.at("last.h7"))
            sp.dma_start(d_out, x[:, :, 0:SEQ]).then_inc(s_out, 16)
            sp.wait_ge(s_out, 16)

        @block.tensor
        def _(pe):
            E = Engine(book, sems)
            state = dict(c=0, bank=0, o=0)
            occupant = {}

            def take(label, rotating=BANKS, fixed=None):
                b = state["bank"] % rotating if fixed is None else fixed
                if fixed is None:
                    state["bank"] = (b + 1) % rotating
                if b in occupant:
                    if E.new(occupant[b] + "'"):
                        pe.wait_ge(*E.at(occupant[b] + "'"))
                occupant[b] = label
                book.banks[label] = b
                return psum[:, b, :]

            def next_chunk():
                c = state["c"]
                state["c"] += 1
                pe.wait_ge(landed[c % SLOTS], 16 * (c // SLOTS + 1))
                return c, slot_of(c)

            def product(out, lhsT, rhs, k, n):
                return nc.tensor.matmul(out, lhsT, rhs, start=(k == 0), stop=(k == n - 1))

            def features(nm, c, w, cols, rhs, N, tiles, first=0):
                per = BANK // N
                wv = w[:, 0:len(rhs) * cols].rearrange("p (k n) -> p k n", n=cols)
                for t in range(tiles):
                    if t % per == 0:
                        label = f"{nm}.{first + t // per}"
                        acc = take(label)
                    for k, (r, lab) in enumerate(rhs):
                        if t == 0 and lab:
                            if E.new(lab):
                                pe.wait_ge(*E.at(lab))
                        mm = product(acc[:, N * (t % per):N * (t % per) + N], wv[:, k, P * t:P * t + P], r, k, len(rhs))
                    if t % per == per - 1 or t == tiles - 1:
                        if t == tiles - 1 and c is not None:
                            E.name_next(f"w{c}")
                        mm.then_inc(projected, 1)
                        E.step(projected, label)

            def tokens(nm, c, w, cols, a, b, lhs, ntok, first=0, close=True):
                n = b - a
                per = BANK // n
                wv = w[:, 0:len(lhs) * cols].rearrange("p (k n) -> p k n", n=cols)
                for t in range(ntok):
                    if t % per == 0:
                        label = f"{nm}.{first + t // per}"
                        acc = take(label)
                    for k, (r, lab) in enumerate(lhs):
                        if lab:
                            if E.new(lab):
                                pe.wait_ge(*E.at(lab))
                        mm = product(acc[:, n * (t % per):n * (t % per) + n], r[:, P * t:P * t + P], wv[:, k, a:b], k, len(lhs))
                    if t % per == per - 1 or t == ntok - 1:
                        if t == ntok - 1 and close:
                            E.name_next(f"w{c}")
                        mm.then_inc(projected, 1)
                        E.step(projected, label)

            def normed(nm, N):
                return [(h[:, k, 0:N], f"{nm}.h{k}") for k in range(KD)]

            def norm(nm):
                acc = take(f"{nm}.sum")
                for k in range(KD):
                    if E.new(f"{nm}.sq{k}"):
                        pe.wait_ge(*E.at(f"{nm}.sq{k}"))
                    mm = product(acc[:, 0:NORM_N[nm]], C("ones"), squares[:, k % 4, 0:NORM_N[nm]], k, KD)
                    mm.then_inc(summed, 1)
                    E.step(summed, f"{nm}.c{k}")

            def rotate(nm, view, mat, ready, N):
                acc = take(nm)
                if E.new(ready):
                    pe.wait_ge(*E.at(ready))
                rows = view.shape[0]
                product(acc[0:rows, 0:N], C(mat)[0:rows, 0:rows], view, 0, 1).then_inc(partnered, 1)
                E.step(partnered, nm)

            def attention(nm):
                units = ATT[nm]
                n = len(units)
                for t in range(n + 3):
                    if t < n:
                        u = units[t]
                        if E.new(heads_ready(nm, u)):
                            pe.wait_ge(*E.at(heads_ready(nm, u)))
                        if u["kind"] == "fox":
                            hh = u["head"]
                            acc = take(f"{nm}.B{t}", ROTATING)
                            for g in range(2):
                                out = acc[:, SEQ * g:SEQ * g + SEQ]
                                product(out, onehot[:, P * hh:P * hh + P], csT, 0, 2)
                                mm = product(out, C("ident"), C("causal")[:, SEQ * g:SEQ * g + SEQ], 1, 2)
                            mm.then_inc(attended, 1)
                            E.step(attended, f"{nm}.B{t}")
                        acc = take(f"{nm}.S{t}", ROTATING)
                        for g, (lh, rh) in enumerate(u["mms"]):
                            mm = product(acc[:, g * u["K"]:(g + 1) * u["K"]], lh, rh, 0, 1)
                        mm.then_inc(attended, 1)
                        E.step(attended, f"{nm}.S{t}")
                    for l, c in fill_at(nm, t):
                        modulation(l, c)
                    if 2 <= t < n + 2:
                        v = t - 2
                        acc = take(f"{nm}.T{v}", ROTATING)
                        if E.new(f"{nm}.p{v}"):
                            pe.wait_ge(*E.at(f"{nm}.p{v}"))
                        for b in range(4):
                            mm = nc.tensor.transpose(acc[:, P * b:P * b + P], probs[:, v % 3, P * b:P * b + P], C("ident"))
                        mm.then_inc(attended, 1)
                        E.step(attended, f"{nm}.T{v}")
                    if t >= 3:
                        v = t - 3
                        u = units[v]
                        if v == 0 or units[v - 1]["last"]:
                            state["o"] ^= 1
                            state["acc"] = take(f"{nm}.O{v}", fixed=ROTATING + state["o"])
                            state["ol"] = f"{nm}.O{v}"
                        acc = state["acc"]
                        if E.new(f"{nm}.pT{v}"):
                            pe.wait_ge(*E.at(f"{nm}.pT{v}"))
                        a, w = u["cols"]
                        out = acc[HD * u["half"]:HD * u["half"] + HD, a:a + w]
                        for i, vt in enumerate(u["v"]):
                            if u["G"] == 2:
                                rh = probsT[:, v % 2, :].rearrange("p (g k q) -> p g k q", g=2, k=2)[:, :, i, :]
                                oo = out.rearrange("p (g q) -> p g q", g=2)
                            else:
                                rh, oo = probsT[:, v % 2, P * i:P * i + P], out
                            mm = product(oo, vt, rh, i, len(u["v"]))
                        mm.then_inc(attended, 1)
                        E.step(attended, state["ol"] if u["last"] else None)

            def modulation(l, m):
                c, w = next_chunk()
                if E.new("cond"):
                    pe.wait_ge(*E.at("cond"))
                acc = take(f"mod{l}.{m}", ROTATING)
                wv = w[:, 0:KD * 256].rearrange("p (k n) -> p k n", n=256)
                for t in range(2):
                    for k in range(KD):
                        mm = product(acc[:, 2 * t:2 * t + 2], wv[:, k, P * t:P * t + P], csil[:, k, :], k, KD)
                E.name_next(f"w{c}")
                mm.then_inc(modulation_multiplied, 1)
                E.step(modulation_multiplied, f"mod{l}.{m}")

            def ffn(nm, nn, N):
                rhs = normed(nn, N)
                pre = [(r, None) for r, _ in rhs]

                def pair(c, w, base, i, r):
                    wv = w[:, 0:KD * 256].rearrange("p (k n) -> p k n", n=256)
                    for t in range(2):
                        label = f"{nm}_in.{i}.{t}"
                        if E.loop_name:
                            b = (base + 2 * i + t) % BANKS
                            if E.new(label + "'", shift=-1):
                                pe.wait_ge(*E.at(label + "'", shift=-1))
                            book.banks[label] = b
                            acc = psum[:, b, :]
                        else:
                            acc = take(label)
                        for k in range(KD):
                            if r[k][1]:
                                if E.new(r[k][1]):
                                    pe.wait_ge(*E.at(r[k][1]))
                            mm = product(acc[:, 0:N], wv[:, k, P * t:P * t + P], r[k][0], k, KD)
                        if t == 1:
                            E.name_next(f"w{c}")
                        mm.then_inc(ffn_multiplied, 1)
                        E.step(ffn_multiplied, label)

                lead, turns = LOOPED[f"{nm}_in"]
                for u in range(lead):
                    c, w = next_chunk()
                    pair(c, w, 0, SLOTS + u, rhs)
                first = state["c"]
                base = state["bank"]
                for b in range(BANKS):
                    if b in occupant:
                        if E.new(occupant[b] + "'"):
                            pe.wait_ge(*E.at(occupant[b] + "'"))
                with E.loop(pe, f"{nm}_in", turns) as it:
                    for u in range(SLOTS):
                        c = first + u
                        pe.wait_ge(landed[c % SLOTS], 16 * (c // SLOTS + 1) + it * 16)
                        pair(c, slot_of(c), base, u, pre)
                for u in range(SLOTS):
                    for t in range(2):
                        occupant[(base + 2 * u + t) % BANKS] = f"{nm}_in.{u}.{t}"
                state["c"] += turns * SLOTS
                lead, turns = LOOPED[f"{nm}_out"]
                first = state["c"]
                base = state["bank"]
                for u in range(SLOTS):
                    if (base + u) % BANKS in occupant:
                        if E.new(occupant[(base + u) % BANKS] + "'"):
                            pe.wait_ge(*E.at(occupant[(base + u) % BANKS] + "'"))
                if E.new(f"{nm}_in.hid"):
                    pe.wait_ge(*E.at(f"{nm}_in.hid"))
                with E.loop(pe, f"{nm}_out", turns) as it:
                    for u in range(SLOTS):
                        c = first + u
                        label = f"{nm}_out.{u}"
                        pe.wait_ge(landed[c % SLOTS], 16 * (c // SLOTS + 1) + it * 16)
                        b = (base + u) % BANKS
                        if E.new(f"{nm}_out.x{u}", shift=-1):
                            pe.wait_ge(*E.at(f"{nm}_out.x{u}", shift=-1))
                        book.banks[label] = b
                        wv = slot_of(c).rearrange("p (k n) -> p k n", n=P)
                        for k in range(KF):
                            mm = product(psum[:, b, 0:N], wv[:, k, :], hid[:, k, 0:N], k, KF)
                        E.name_next(f"w{c}")
                        mm.then_inc(ffn_multiplied, 1)
                        E.step(ffn_multiplied, label)
                for u in range(SLOTS):
                    occupant[(base + u) % BANKS] = f"{nm}_out.{u}"
                state["c"] += turns * SLOTS
                state["bank"] = (base + SLOTS) % BANKS

            def head_norm(nm):
                for H in head_norms(nm):
                    T = H["tiles"]
                    N = T[0].shape[-1]
                    if H["total"]:
                        acc = take(f"{H['name']}.sum0")
                    for t in range(len(T)):
                        if not H["total"]:
                            acc = take(f"{H['name']}.sum{t}")
                        if E.new(f"{H['name']}.sq{t}"):
                            pe.wait_ge(*E.at(f"{H['name']}.sq{t}"))
                        rows = T[t].shape[0]
                        mm = product(acc[0:rows, 0:N], C(H["mat"])[0:rows, 0:rows], squares[0:rows, t % 4, 0:N],
                                     t if H["total"] else 0, len(T) if H["total"] else 1)
                        mm.then_inc(summed, 1)
                        E.step(summed, f"{H['name']}.c{t}")
                        if not H["total"]:
                            E.name_last(f"{H['name']}.sum{t}")
                    if H["total"]:
                        E.name_last(f"{H['name']}.sum0")
                    if H["rope"]:
                        for t in range(len(T)):
                            rotate(f"{H['name']}.r{t}", T[t][:, 0:SEQ], "rot_q" if rows == 96 else "rot_pair", f"{H['name']}.n{t}", SEQ)

            pe.wait_ge(s_const, 32)
            for l in range(2):
                nm = f"b1.{l}"
                norm(nm)
                rhs = normed(nm, SEQ)
                for br in range(3):
                    for part in "qkvg":
                        for j in range(2):
                            c, w = next_chunk()
                            if part == "v":
                                tokens(f"{nm}.v{br}{j}", c, w, 256, 0, 256, rhs, QT)
                            else:
                                features(f"{nm}.{part}{br}{j}", c, w, 256, rhs, SEQ, 2)
                    if br < 2:
                        for part, buf in (("q", qT[br]), ("k", kT[br])):
                            for j in range(2):
                                rotate(f"{nm}.r{part}{br}{j}", flat(buf[:, 2 * j:2 * j + 2, :]), "rot_half",
                                       f"{nm}.{part}{br}{j}.0'", 512)
                for j in range(2):
                    c, w = next_chunk()
                    features(f"{nm}.qi{j}", c, w, 256, rhs, SEQ, 2)
                c, w = next_chunk()
                features(f"{nm}.ki", None, w, 144, rhs, SEQ, 1)
                tokens(f"{nm}.wl", c, w, 144, 128, 144, rhs, QT)
                for j in range(2):
                    rotate(f"{nm}.rqi{j}", flat(qiT[:, 2 * j:2 * j + 2, :]), "rot_half", f"{nm}.qi{j}.0'", 512)
                rotate(f"{nm}.rki", kiT, "rot_half", f"{nm}.ki.0'", SEQ)
                for hh in range(HEADS):
                    acc = take(f"{nm}.ix{hh}")
                    rows = slice(HD * (hh % 2), HD * (hh % 2) + HD)
                    if E.new(f"{nm}.rqi{hh // 4}'"):
                        pe.wait_ge(*E.at(f"{nm}.rqi{hh // 4}'"))
                    if E.new(f"{nm}.rki'"):
                        pe.wait_ge(*E.at(f"{nm}.rki'"))
                    for q in range(QT):
                        mm = product(acc[:, SEQ * q:SEQ * q + SEQ], qiT[rows, hh // 2, P * q:P * q + P], kiT[rows, :], 0, 1)
                    mm.then_inc(multiplied, 1)
                    E.step(multiplied, f"{nm}.ix{hh}")
                acc = take(f"{nm}.cs")
                if E.new(f"{nm}.logf"):
                    pe.wait_ge(*E.at(f"{nm}.logf"))
                for t in range(QT):
                    mm = product(acc[0:8, 0:SEQ], fz[:, t, 0:8], C("upto")[:, SEQ * t:SEQ * t + SEQ], t, QT)
                for q in range(QT):
                    for t in range(QT):
                        mm = product(acc[:, SEQ + 8 * q:SEQ + 8 * q + 8],
                                     C("upto")[:, SEQ * t + P * q:SEQ * t + P * q + P], fz[:, t, 0:8], t, QT)
                mm.then_inc(multiplied, 1)
                E.step(multiplied, f"{nm}.cs")
                if l == 0:
                    pe.wait_ge(s_onehot, 16)
                attention(f"{nm}.att")
                for j in range(12):
                    c, w = next_chunk()
                    features(f"{nm}.m{j}", c, w, 256, rhs, SEQ, 2)
                for n in range(3):
                    for j in range(2):
                        c, w = next_chunk()
                        features(f"{nm}.y{n}{j}", c, w, 512, [(oT[n][:, k, :], f"{nm}.att.o{8 * n + 2 * k + 1}") for k in range(KW)],
                                 SEQ, 4)
                for j in range(4):
                    c, w = next_chunk()
                    features(f"{nm}.out{j}", c, w, 256, [(merged[:, k, :], f"{nm}.mg{k // 2}") for k in range(KD)], SEQ, 2)
            norm("final")
            norm("b2.0.n1")
            ffn("b2.0.ffn1", "b2.0.n1", TOK)
            norm("b2.0.nm")
            rhs = normed("b2.0.nm", TOK)
            for j in range(7):
                c, w = next_chunk()
                features("b2.0.in", c, w, 256, rhs, TOK, 2, first=2 * j)
            head_norm("b2.0.lora")
            c, w = next_chunk()
            wv = w[:, 0:3 * 768].rearrange("p (k n) -> p k n", n=768)
            for t in range(HEADS):
                acc = take(f"b2.0.uq.{t}")
                for k in range(3):
                    if E.new(f"b2.0.lora.cq.n{k}"):
                        pe.wait_ge(*E.at(f"b2.0.lora.cq.n{k}"))
                    mm = product(acc[0:96, :], wv[:, k, 96 * t:96 * t + 96], m_cq[:, k, :], k, 3)
                if t == HEADS - 1:
                    E.name_next(f"w{c}")
                mm.then_inc(multiplied, 1)
                E.step(multiplied, f"b2.0.uq.{t}")
            c, w = next_chunk()
            kv = [(m_ckv[:, k, :], f"b2.0.lora.ckv.n{k}") for k in range(2)]
            wv = w[:, 0:2048].rearrange("p (k n) -> p k n", n=1024)
            for t in range(HEADS):
                acc = take(f"b2.0.ukv.{t}")
                for k in range(2):
                    if E.new(kv[k][1]):
                        pe.wait_ge(*E.at(kv[k][1]))
                    mm = product(acc[0:64, :], wv[:, k, HD * t:HD * t + HD], kv[k][0], k, 2)
                mm.then_inc(multiplied, 1)
                E.step(multiplied, f"b2.0.ukv.{t}")
            tokens("b2.0.mv", c, w, 1024, 512, 1024, kv, 4)
            head_norm("b2.0.heads")
            for m in range(MOD_EARLY):
                modulation(1, m)
            for what in ("mean", "var"):
                acc = take(f"b2.0.conv.{what}")
                for t in range(4):
                    if E.new(f"b2.0.conv.{'y' if what == 'mean' else 'sq'}{t}"):
                        pe.wait_ge(*E.at(f"b2.0.conv.{'y' if what == 'mean' else 'sq'}{t}"))
                    mm = product(acc, C("ones"), m_yc[:, t, :] if what == "mean" else squares[:, t, :], t, 4)
                mm.then_inc(multiplied, 1)
                E.step(multiplied, f"b2.0.conv.{what}")
            attention("b2.0.att")
            for j in range(4):
                c, w = next_chunk()
                features(f"b2.0.out", c, w, 256,
                         [(m_o[:, k, :], mixed_ready("b2.0", k)) for k in range(KD)], TOK, 2, first=2 * j)
            norm("b2.0.n2")
            ffn("b2.0.ffn2", "b2.0.n2", TOK)
            norm("b2.1.n1")
            ffn("b2.1.ffn1", "b2.1.n1", TOK)
            norm("b2.1.nm")
            rhs = normed("b2.1.nm", TOK)
            for j in range(2):
                c, w = next_chunk()
                features("b2.1.in", c, w, 256, rhs, TOK, 2, first=2 * j)
            c, w = next_chunk()
            features("b2.1.in", None, w, 256, rhs, TOK, 1, first=4)
            tokens("b2.1.cv", c, w, 256, 128, 256, rhs, 4)
            for j in range(2):
                c, w = next_chunk()
                tokens("b2.1.nv", c, w, 256, 0, 256, rhs, 4, first=2 * j)
            rhs = normed("b2.1.nm", SEQ)
            for part in ("cq", "nq"):
                for j in range(2):
                    c, w = next_chunk()
                    features(f"b2.1.{part}", c, w, 256, rhs, SEQ, 2, first=j)
            head_norm("b2.1.heads")
            attention("b2.1.att")
            for j in range(4):
                c, w = next_chunk()
                features(f"b2.1.out", c, w, 256, [(g_o[:, k, :], mixed_ready("b2.1", k)) for k in range(KD)], SEQ, 2, first=j)
            norm("b2.1.n2")
            ffn("b2.1.ffn2", "b2.1.n2", SEQ)
            assert state["c"] == len(stage_of), (state["c"], len(stage_of))

        @block.scalar
        def _(act):
            E = Engine(book, sems)
            A = nc.scalar.activation

            def bank(label, N=BANK):
                if E.new(label):
                    act.wait_ge(*E.at(label))
                return psum[:, E.bank(label), 0:N]

            def norm(nm):
                N = NORM_N[nm]
                if XR[nm]:
                    if E.new(XR[nm]):
                        act.wait_ge(*E.at(XR[nm]))
                for k in range(KD):
                    if k >= 4:
                        if E.new(f"{nm}.c{k - 4}"):
                            act.wait_ge(*E.at(f"{nm}.c{k - 4}"))
                    A(squares[:, k % 4, 0:N], x[:, k, 0:N], ACT.Square).then_inc(rooted, 1)
                    act.wait_ge(rooted, E.step(rooted, f"{nm}.sq{k}"))
                A(rs[:, 0:N], sum_bank(nm, N), ACT.Sqrt, scale=1.0 / D,
                  bias=C("eps")).then_inc(rooted, 1)
                act.wait_ge(rooted, E.step(rooted, f"{nm}.sum'"))

            def sum_bank(nm, N):
                if E.new(f"{nm}.c7"):
                    act.wait_ge(*E.at(f"{nm}.c7"))
                return psum[:, E.bank(f"{nm}.sum"), 0:N]

            def modulate(nm, l, which, N):
                if E.new(f"{nm}.mscale"):
                    act.wait_ge(*E.at(f"{nm}.mscale"))
                for k in range(KD):
                    if E.new(f"{nm}.t{k}"):
                        act.wait_ge(*E.at(f"{nm}.t{k}"))
                    for g in range(N // SEQ):
                        v = h[:, k, SEQ * g:SEQ * g + SEQ]
                        last = g == N // SEQ - 1
                        A(v, v, ACT.Identity, scale=mscale[:, k, g:g + 1],
                          bias=mods[:, l, 24 * which + k, g:g + 1]).then_inc(shifted, 1)
                        act.wait_ge(shifted, E.step(shifted, f"{nm}.h{k}" if last else None))

            def attention(nm):
                units = ATT[nm]
                n = len(units)
                for t in range(n + 3):
                    if t < n:
                        u = units[t]
                        if u["kind"] == "fox":
                            A(work[:, t % 2, :], bank(f"{nm}.B{t}"), ACT.Copy).then_inc(exponentiated, 1)
                            act.wait_ge(exponentiated, E.step(exponentiated, f"{nm}.B{t}'"))
                        if E.new(f"{nm}.mx{t}"):
                            act.wait_ge(*E.at(f"{nm}.mx{t}"))
                        K = u["K"]
                        src = psum[:, E.bank(f"{nm}.S{t}"), :]
                        for g in range(u["G"]):
                            last = g == u["G"] - 1
                            A(probs[:, t % 3, K * g:K * g + K], src[:, K * g:K * g + K], ACT.Exp,
                              scale=u["scale"], bias=stat[:, t % 4, 2 + g:3 + g],
                              accum_out=stat[:, t % 4, 4 + g:5 + g]).then_inc(exponentiated, 1)
                            act.wait_ge(exponentiated, E.step(exponentiated, f"{nm}.S{t}'" if last else None))
                    for l, c in fill_at(nm, t):
                        modulation(l, c)
                    if 2 <= t < n + 2:
                        v = t - 2
                        A(probsT[:, v % 2, :], bank(f"{nm}.T{v}"), ACT.Copy).then_inc(exponentiated, 1)
                        act.wait_ge(exponentiated, E.step(exponentiated, f"{nm}.T{v}'"))
                        E.name_last(f"{nm}.pT{v}")

            def modulation(l, c):
                lab = f"mod{l}.{c}"
                A(mods[:, l, 2 * c:2 * c + 2, :].rearrange("p a b -> p (a b)"), bank(lab, 4), ACT.Copy).then_inc(modulation_copied, 1)
                act.wait_ge(modulation_copied, E.step(modulation_copied, lab + "'"))

            def ffn(nm, N):
                def pair(i, ring, shift):
                    for t in range(2):
                        if shift is not None and E.new(f"{nm}_in.h{i - shift}.{t}", shift=-1 if E.loop_name else 0):
                            act.wait_ge(*E.at(f"{nm}_in.h{i - shift}.{t}", shift=-1 if E.loop_name else 0))
                        lab = f"{nm}_in.{i}.{t}"
                        A(squares[:, ring * 2 + t, 0:N], bank(lab, N), ACT.Silu).then_inc(gated, 1)
                        act.wait_ge(gated, E.step(gated, lab + "'"))
                lead, turns = LOOPED[f"{nm}_in"]
                for r in range(lead // 2):
                    pair(SLOTS + 2 * r, r % 2, 4 if r >= 2 else None)
                with E.loop(act, f"{nm}_in", turns):
                    for r in range(2):
                        pair(2 * r, (lead // 2 + r) % 2, 0)

            def head_norm(nm):
                for H in head_norms(nm):
                    T = H["tiles"]
                    N = T[0].shape[-1]
                    rows = T[0].shape[0]

                    def square(t):
                        if E.new(H["ready"][t]):
                            act.wait_ge(*E.at(H["ready"][t]))
                        if t >= 4:
                            if E.new(f"{H['name']}.c{t - 4}"):
                                act.wait_ge(*E.at(f"{H['name']}.c{t - 4}"))
                        A(squares[0:rows, t % 4, 0:N], T[t], ACT.Square).then_inc(squared, 1)
                        act.wait_ge(squared, E.step(squared, f"{H['name']}.sq{t}"))

                    def root(t, s):
                        src = psum[0:rows, E.bank(f"{H['name']}.sum{s}"), 0:N]
                        if E.new(f"{H['name']}.sum{s}"):
                            act.wait_ge(*E.at(f"{H['name']}.sum{s}"))
                        A(work[0:rows, t % 2, 0:N], src, ACT.Sqrt, scale=1.0 / H["count"], bias=C("eps")[0:rows, :]).then_inc(rooted, 1)
                        act.wait_ge(rooted, E.step(rooted, f"{H['name']}.sum{s}'"))
                    for t in range(len(T)):
                        square(t)
                    if H["total"]:
                        root(0, 0)
                    else:
                        for t in range(len(T)):
                            if t >= 2:
                                if E.new(f"{H['name']}.n{t - 2}"):
                                    act.wait_ge(*E.at(f"{H['name']}.n{t - 2}"))
                            root(t, t)
                    if E.new(f"{H['name']}.n{len(T) - 1}"):
                        act.wait_ge(*E.at(f"{H['name']}.n{len(T) - 1}"))

            act.wait_ge(s_const, 32)
            act.wait_ge(s_x, 16)
            A(csil[:, :, :].rearrange("p a b -> p (a b)"), R("cond"), ACT.Silu).then_inc(copied, 1)
            act.wait_ge(copied, E.step(copied, "cond"))
            for l in range(2):
                nm = f"b1.{l}"
                norm(nm)
                for br in range(3):
                    for part in "qkvg":
                        for j in range(2):
                            lab = f"{nm}.{part}{br}{j}.0"
                            src = bank(lab)
                            if part == "v":
                                A(vv[br][:, :, 256 * j:256 * j + 256], src.rearrange("p (a b) -> p a b", a=2), ACT.Copy).then_inc(copied, 1)
                                act.wait_ge(copied, E.step(copied, lab + "'"))
                            else:
                                buf = {"q": qT, "k": kT, "g": gg}[part][br]
                                sc = HD ** -0.5 if (part == "q" and br == 2) else 1.0
                                A(flat(buf[:, 2 * j:2 * j + 2, :]), src, ACT.Silu if part == "g" else ACT.Copy,
                                  scale=sc).then_inc(copied, 1)
                                act.wait_ge(copied, E.step(copied, lab + "'"))
                for j in range(2):
                    lab = f"{nm}.qi{j}.0"
                    A(flat(qiT[:, 2 * j:2 * j + 2, :]), bank(lab), ACT.Copy).then_inc(copied, 1)
                    act.wait_ge(copied, E.step(copied, lab + "'"))
                lab = f"{nm}.ki.0"
                A(kiT, bank(lab, SEQ), ACT.Copy).then_inc(copied, 1)
                act.wait_ge(copied, E.step(copied, lab + "'"))
                lab = f"{nm}.wl.0"
                A(flat(wl), bank(lab, 32), ACT.Copy).then_inc(copied, 1)
                act.wait_ge(copied, E.step(copied, lab + "'"))
                if E.new(f"{nm}.z"):
                    act.wait_ge(*E.at(f"{nm}.z"))
                A(fz[:, 2, :], fz[:, 1, :], ACT.Exp, scale=-1.0).then_inc(copied, 1)
                act.wait_ge(copied, E.step(copied))
                A(fz[:, 3, :], fz[:, 2, :], ACT.Ln, bias=C("one")).then_inc(copied, 1)
                act.wait_ge(copied, E.step(copied, f"{nm}.ln"))
                for hh in range(HEADS):
                    if hh >= 2:
                        if E.new(f"{nm}.isc{hh - 2}"):
                            act.wait_ge(*E.at(f"{nm}.isc{hh - 2}"))
                    lab = f"{nm}.ix{hh}"
                    A(work[:, hh % 2, :], bank(lab), ACT.Relu).then_inc(copied, 1)
                    act.wait_ge(copied, E.step(copied, lab + "'"))
                attention(f"{nm}.att")
                for j in range(12):
                    lab = f"{nm}.m{j}.0"
                    A(flat(gates[:, 2 * j:2 * j + 2, :]), bank(lab), ACT.Sigmoid).then_inc(copied, 1)
                    act.wait_ge(copied, E.step(copied, lab + "'"))
            norm("final")
            act.wait_ge(s_ctx, 16)
            norm("b2.0.n1")
            modulate("b2.0.n1", 0, 0, TOK)
            ffn("b2.0.ffn1", TOK)
            norm("b2.0.nm")
            modulate("b2.0.nm", 0, 1, TOK)
            dst = [m_ckv[:, 0, :], m_ckv[:, 1, :], m_kr, m_cq[:, 0, :], m_cq[:, 1, :], m_cq[:, 2, :]]
            for i in range(6):
                lab = f"b2.0.in.{i}"
                A(dst[i], bank(lab), ACT.Copy).then_inc(copied, 1)
                act.wait_ge(copied, E.step(copied, lab + "'"))
                E.name_last(f"b2.0.in.e{i}")
            for i in range(4):
                lab = f"b2.0.in.{6 + i}"
                A(m_ca[:, i, :], bank(lab), ACT.Identity, bias=R("glu_b", i, 1)).then_inc(copied, 1)
                act.wait_ge(copied, E.step(copied, lab + "'"))
            for i in range(4):
                lab = f"b2.0.in.{10 + i}"
                A(squares[:, i, :], bank(lab), ACT.Sigmoid, bias=R("glu_b", 4 + i, 1)).then_inc(copied, 1)
                act.wait_ge(copied, E.step(copied, lab + "'"))
            if E.new("b2.0.conv.glu3"):
                act.wait_ge(*E.at("b2.0.conv.glu3"))
            head_norm("b2.0.lora")
            for i in range(HEADS):
                lab = f"b2.0.uq.{i}"
                A(m_q[0:96, i, :], bank(lab)[0:96, :], ACT.Copy).then_inc(copied, 1)
                act.wait_ge(copied, E.step(copied, lab + "'"))
            for i in range(HEADS):
                lab = f"b2.0.ukv.{i}"
                A(m_k[0:64, i, :], bank(lab)[0:64, :], ACT.Copy).then_inc(copied, 1)
                act.wait_ge(copied, E.step(copied, lab + "'"))
            for i in range(4):
                lab = f"b2.0.mv.{i}"
                A(m_v[:, i, :], bank(lab), ACT.Copy).then_inc(copied, 1)
                act.wait_ge(copied, E.step(copied, lab + "'"))
            head_norm("b2.0.heads")
            for i in range(HEADS):
                A(m_k[64:96, i, :], m_kr[64:96, :], ACT.Copy).then_inc(copied, 1)
                act.wait_ge(copied, E.step(copied, "b2.0.heads.kr_copied" if i == HEADS - 1 else None))
            for c in range(MOD_EARLY):
                modulation(1, c)
            for t in range(4):
                if E.new(f"b2.0.conv.c{t}"):
                    act.wait_ge(*E.at(f"b2.0.conv.c{t}"))
                A(squares[:, t, :], m_yc[:, t, :], ACT.Square).then_inc(copied, 1)
                act.wait_ge(copied, E.step(copied, f"b2.0.conv.sq{t}"))
            A(rs[:, :], bank("b2.0.conv.var"), ACT.Sqrt, scale=1.0 / 512, bias=C("eps")).then_inc(copied, 1)
            act.wait_ge(copied, E.step(copied, "b2.0.conv.var'"))
            for t in range(4):
                if E.new(f"b2.0.conv.n{t}"):
                    act.wait_ge(*E.at(f"b2.0.conv.n{t}"))
                A(m_o[:, 4 + t, :], m_yc[:, t, :], ACT.Silu, scale=R("ln_g", t, 1), bias=R("ln_b", t, 1)).then_inc(copied, 1)
                act.wait_ge(copied, E.step(copied, f"b2.0.conv.o{t}"))
            attention("b2.0.att")
            norm("b2.0.n2")
            modulate("b2.0.n2", 0, 2, TOK)
            ffn("b2.0.ffn2", TOK)
            norm("b2.1.n1")
            modulate("b2.1.n1", 1, 0, TOK)
            ffn("b2.1.ffn1", TOK)
            norm("b2.1.nm")
            modulate("b2.1.nm", 1, 1, TOK)
            dst = [g_ck] + [g_nk[:, t, :] for t in range(4)]
            for i in range(5):
                lab = f"b2.1.in.{i}"
                A(dst[i], bank(lab), ACT.Copy).then_inc(copied, 1)
                act.wait_ge(copied, E.step(copied, lab + "'"))
                E.name_last(f"b2.1.in.e{i}")
            A(flat(g_cv), bank("b2.1.cv.0"), ACT.Copy).then_inc(copied, 1)
            act.wait_ge(copied, E.step(copied, "b2.1.cv.0'"))
            for j in range(2):
                for i in range(2):
                    lab = f"b2.1.nv.{2 * j + i}"
                    A(g_nv[:, 2 * i:2 * i + 2, 256 * j:256 * j + 256],
                      bank(lab).rearrange("p (a b) -> p a b", a=2), ACT.Copy).then_inc(copied, 1)
                    act.wait_ge(copied, E.step(copied, lab + "'"))
            for part, buf in (("cq", g_cq), ("nq", g_nq)):
                for j in range(2):
                    lab = f"b2.1.{part}.{j}"
                    A(flat(buf[:, 2 * j:2 * j + 2, :]), bank(lab), ACT.Copy).then_inc(copied, 1)
                    act.wait_ge(copied, E.step(copied, lab + "'"))
                    E.name_last(f"b2.1.{part}.e{j}")
            head_norm("b2.1.heads")
            attention("b2.1.att")
            norm("b2.1.n2")
            modulate("b2.1.n2", 1, 2, SEQ)
            ffn("b2.1.ffn2", SEQ)

        @block.vector
        def _(dve):
            E = Engine(book, sems)
            V = nc.vector

            def bank(label, N=BANK):
                if E.new(label):
                    dve.wait_ge(*E.at(label))
                return psum[:, E.bank(label), 0:N]

            def norm(nm, gain=None, to=None):
                N = NORM_N[nm]
                if E.new(f"{nm}.sum'"):
                    dve.wait_ge(*E.at(f"{nm}.sum'"))
                V.reciprocal(rs[:, 0:N], rs[:, 0:N]).then_inc(normed, 1)
                dve.wait_ge(normed, E.step(normed))
                for k in range(KD):
                    if gain is not None:
                        out = (x if to == "x" else h)[:, k, 0:N]
                        V.scalar_tensor_tensor(out=out, in0=x[:, k, 0:N], scalar=gain[:, k:k + 1], in1=rs[:, 0:N],
                                               op0=ALU.mult, op1=ALU.mult).then_inc(normed, 1)
                        dve.wait_ge(normed, E.step(normed, f"{nm}.h{k}"))
                    else:
                        V.tensor_tensor(h[:, k, 0:N], x[:, k, 0:N], rs[:, 0:N], ALU.mult).then_inc(normed, 1)
                        dve.wait_ge(normed, E.step(normed, f"{nm}.t{k}"))

            def prepare(nm, l, which, gain):
                a = 24 * which + 8
                V.scalar_tensor_tensor(out=mscale[:, :, :].rearrange("p a b -> p (a b)"),
                                       in0=mods[:, l, a:a + 8, :].rearrange("p a b -> p (a b)"), scalar=1.0,
                                       in1=R(gain), op0=ALU.add, op1=ALU.mult).then_inc(scales_prepared, 1)
                dve.wait_ge(scales_prepared, E.step(scales_prepared, f"{nm}.mscale"))

            def rope(nm, view, cos, sin, lab, N):
                rows = view.shape[0]
                b, cos, sin = bank(lab, N)[0:rows, :], cos[0:rows, :], sin[0:rows, :]
                V.tensor_tensor(b, b, sin, ALU.mult).then_inc(roped, 1)
                dve.wait_ge(roped, E.step(roped))
                V.tensor_tensor(view, view, cos, ALU.mult).then_inc(roped, 1)
                dve.wait_ge(roped, E.step(roped))
                V.tensor_tensor(view, view, b, ALU.add).then_inc(roped, 1)
                dve.wait_ge(roped, E.step(roped, lab + "'"))

            def attention(nm):
                units = ATT[nm]
                n = len(units)
                pair = 0
                for t in range(n + 3):
                    if t < n:
                        u = units[t]
                        G, K = u["G"], u["K"]
                        S = bank(f"{nm}.S{t}", G * K)
                        st = stat[:, t % 4, :]
                        if u["kind"] == "moba":
                            V.tensor_tensor(S, S, C("causal"), ALU.add).then_inc(probs_ready, 1)
                            dve.wait_ge(probs_ready, E.step(probs_ready))
                        if u["kind"] == "dsa":
                            V.tensor_tensor(S, S, flat(dsa_mask), ALU.add).then_inc(probs_ready, 1)
                            dve.wait_ge(probs_ready, E.step(probs_ready))
                        if u["kind"] == "fox":
                            if E.new(f"{nm}.B{t}'"):
                                dve.wait_ge(*E.at(f"{nm}.B{t}'"))
                            for g in range(G):
                                V.scalar_tensor_tensor(
                              out=S[:, K * g:K * g + K], in0=S[:, K * g:K * g + K], scalar=cq[:, g, u["head"]:u["head"] + 1],
                              in1=work[:, t % 2, K * g:K * g + K], op0=ALU.add, op1=ALU.add).then_inc(probs_ready, 1)
                                dve.wait_ge(probs_ready, E.step(probs_ready))
                        if u["kind"] == "na":
                            V.tensor_tensor(S[:, 0:SEQ], S[:, 0:SEQ], g_bias[:, 2 * u["head"] + u["q"], :], ALU.add).then_inc(probs_ready, 1)
                            dve.wait_ge(probs_ready, E.step(probs_ready))
                        V.tensor_reduce(st[:, 0:G], S.rearrange("p (g k) -> p g k", g=G), AX_X, ALU.max).then_inc(probs_ready, 1)
                        dve.wait_ge(probs_ready, E.step(probs_ready))
                        V.tensor_scalar(st[:, 2:2 + G], st[:, 0:G], -u["scale"], None, ALU.mult).then_inc(probs_ready, 1)
                        dve.wait_ge(probs_ready, E.step(probs_ready, f"{nm}.mx{t}"))
                    if 1 <= t <= n:
                        v = t - 1
                        u = units[v]
                        G, K = u["G"], u["K"]
                        st = stat[:, v % 4, :]
                        if E.new(f"{nm}.S{v}'"):
                            dve.wait_ge(*E.at(f"{nm}.S{v}'"))
                        V.reciprocal(st[:, 6:6 + G], st[:, 4:4 + G]).then_inc(probs_ready, 1)
                        dve.wait_ge(probs_ready, E.step(probs_ready))
                        for g in range(G):
                            pv = probs[:, v % 3, K * g:K * g + K]
                            V.tensor_scalar(pv, pv, st[:, 6 + g:7 + g], None, ALU.mult).then_inc(probs_ready, 1)
                            dve.wait_ge(probs_ready, E.step(probs_ready, f"{nm}.p{v}" if g == G - 1 else None))
                    if t >= 3:
                        v = t - 3
                        u = units[v]
                        if v == 0 or units[v - 1]["last"]:
                            state["ol"] = f"{nm}.O{v}"
                        if u["last"]:
                            o = bank(state["ol"], SEQ)
                            if u["gate"] is not None:
                                V.tensor_tensor(u["dst"], o, u["gate"], ALU.mult).then_inc(probs_ready, 1)
                                dve.wait_ge(probs_ready, E.step(probs_ready, state["ol"] + "'"))
                            else:
                                V.tensor_copy(u["dst"], o).then_inc(probs_ready, 1)
                                dve.wait_ge(probs_ready, E.step(probs_ready, state["ol"] + "'"))
                            E.name_last(f"{nm}.o{v}")

            state = {}

            def ffn(nm, l, N, which):
                def pair(i, ring, tile):
                    for t in range(2):
                        if E.new(f"{nm}_in.{i}.{t}'"):
                            dve.wait_ge(*E.at(f"{nm}_in.{i}.{t}'"))
                        lab = f"{nm}_in.{i + 1}.{t}"
                        u = bank(lab, N)
                        dst = hid[:, bass.ds(tile + t, 1), 0:N].rearrange("p a b -> p (a b)")
                        V.tensor_tensor(dst, squares[:, 2 * ring + t, 0:N], u, ALU.mult).then_inc(hidden_written, 1)
                        dve.wait_ge(hidden_written, E.step(hidden_written, lab + "'"))
                        E.name_last(f"{nm}_in.h{i}.{t}")
                lead, turns = LOOPED[f"{nm}_in"]
                for r in range(lead // 2):
                    pair(SLOTS + 2 * r, r % 2, 2 * r)
                with E.loop(dve, f"{nm}_in", turns) as it:
                    for r in range(2):
                        pair(2 * r, (lead // 2 + r) % 2, it * SLOTS + (lead + 2 * r))
                E.name_last(f"{nm}_in.hid")
                a = 24 * which + 16
                V.tensor_scalar(mscale[:, :, :].rearrange("p a b -> p (a b)"),
                                mods[:, l, a:a + 8, :].rearrange("p a b -> p (a b)"), 0.5, None, ALU.mult).then_inc(hidden_written, 1)
                dve.wait_ge(hidden_written, E.step(hidden_written))
                with E.loop(dve, f"{nm}_out", LOOPED[f"{nm}_out"][1]) as it:
                    for u in range(SLOTS):
                        src = bank(f"{nm}_out.{u}", N)
                        for g in range(N // SEQ):
                            k = bass.ds(it * SLOTS + u, 1)
                            xv = x[:, k, SEQ * g:SEQ * g + SEQ].rearrange("p a b -> p (a b)")
                            last = g == N // SEQ - 1
                            V.scalar_tensor_tensor(out=xv, in0=src[:, SEQ * g:SEQ * g + SEQ],
                                                   scalar=mscale[:, k, g:g + 1].rearrange("p a b -> p (a b)"), in1=xv,
                                                   op0=ALU.mult, op1=ALU.add).then_inc(hidden_written, 1)
                            dve.wait_ge(hidden_written, E.step(hidden_written, f"{nm}_out.x{u}" if last else None))
                        E.name_last(f"{nm}_out.{u}'")

            def head_norm(nm):
                for H in head_norms(nm):
                    T = H["tiles"]
                    N = T[0].shape[-1]
                    for t in range(len(T)):
                        if E.new(f"{H['name']}.sum{0 if H['total'] else t}'"):
                            dve.wait_ge(*E.at(f"{H['name']}.sum{0 if H['total'] else t}'"))
                        w = work[0:T[t].shape[0], 0 if H["total"] else t % 2, 0:N]
                        if t == 0 or not H["total"]:
                            V.reciprocal(w, w).then_inc(normed, 1)
                            dve.wait_ge(normed, E.step(normed))
                        V.scalar_tensor_tensor(out=T[t], in0=T[t], scalar=H["gains"][t], in1=w,
                                               op0=ALU.mult, op1=ALU.mult).then_inc(normed, 1)
                        dve.wait_ge(normed, E.step(normed, f"{H['name']}.n{t}"))
                    if H["rope"]:
                        for t in range(len(T)):
                            rope(H["name"], T[t][:, 0:SEQ], C(H["rope"][0]), C(H["rope"][1]), f"{H['name']}.r{t}", SEQ)
                    E.name_last(f"{H['name']}.done")

            dve.wait_ge(s_const, 32)
            for l in range(2):
                nm = f"b1.{l}"
                norm(nm, gain=R(f"{nm}.gain"))
                for br in range(2):
                    for part, buf in (("q", qT[br]), ("k", kT[br])):
                        for j in range(2):
                            rope(nm, flat(buf[:, 2 * j:2 * j + 2, :]), C("cos_part"), C("sin_part"), f"{nm}.r{part}{br}{j}", 512)
                if E.new(f"{nm}.wl.0'"):
                    dve.wait_ge(*E.at(f"{nm}.wl.0'"))
                zz = fz[:, 0, :].rearrange("p (a b) -> p a b", a=2)
                aa = fz[:, 1, :].rearrange("p (a b) -> p a b", a=2)
                V.tensor_tensor(zz, wl[:, :, 8:16], R(f"{nm}.fbias").rearrange("p (a b) -> p a b", a=2), ALU.add).then_inc(combined, 1)
                dve.wait_ge(combined, E.step(combined))
                V.tensor_scalar(fz[:, 1, :], fz[:, 0, :], -1.0, None, ALU.mult).then_inc(combined, 1)
                dve.wait_ge(combined, E.step(combined))
                V.tensor_tensor(aa, aa, zz, ALU.max).then_inc(combined, 1)
                dve.wait_ge(combined, E.step(combined, f"{nm}.z"))
                V.tensor_scalar(wl[:, :, 0:8], wl[:, :, 0:8], float(HEADS ** -0.5 * HD ** -0.5), None, ALU.mult).then_inc(combined, 1)
                dve.wait_ge(combined, E.step(combined))
                if E.new(f"{nm}.ln"):
                    dve.wait_ge(*E.at(f"{nm}.ln"))
                V.tensor_scalar(fz[:, 2, :], fz[:, 0, :], 0.0, None, ALU.min).then_inc(combined, 1)
                dve.wait_ge(combined, E.step(combined))
                V.tensor_tensor(fz[:, 3, :], fz[:, 2, :], fz[:, 3, :], ALU.subtract).then_inc(combined, 1)
                dve.wait_ge(combined, E.step(combined))
                V.tensor_copy(fz[:, 0:2, 0:8], fz[:, 3, :].rearrange("p (a b) -> p a b", a=2)).then_inc(combined, 1)
                dve.wait_ge(combined, E.step(combined, f"{nm}.logf"))
                for j in range(2):
                    rope(nm, flat(qiT[:, 2 * j:2 * j + 2, :]), C("cos_part"), C("sin_part"), f"{nm}.rqi{j}", 512)
                rope(nm, kiT, C("cos_part")[:, 0:SEQ], C("sin_part")[:, 0:SEQ], f"{nm}.rki", SEQ)
                for hh in range(HEADS):
                    if E.new(f"{nm}.ix{hh}'"):
                        dve.wait_ge(*E.at(f"{nm}.ix{hh}'"))
                    for q in range(QT):
                        rl = work[:, hh % 2, SEQ * q:SEQ * q + SEQ]
                        wcol = wl[:, q, hh:hh + 1]
                        last = f"{nm}.isc{hh}" if q == 1 else None
                        if hh == 0:
                            V.tensor_scalar(isc[:, q, :], rl, wcol, None, ALU.mult).then_inc(combined, 1)
                            dve.wait_ge(combined, E.step(combined, last))
                        else:
                            V.scalar_tensor_tensor(out=isc[:, q, :], in0=rl, scalar=wcol, in1=isc[:, q, :],
                                                   op0=ALU.mult, op1=ALU.add).then_inc(combined, 1)
                            dve.wait_ge(combined, E.step(combined, last))
                V.tensor_tensor(flat(isc), flat(isc), C("causal"), ALU.add).then_inc(combined, 1)
                dve.wait_ge(combined, E.step(combined))
                for q in range(QT):
                    for r in range(TOP // 8):
                        V.max(top8, isc[:, q, :]).then_inc(combined, 1)
                        dve.wait_ge(combined, E.step(combined))
                        V.match_replace(isc[:, q, :], top8, isc[:, q, :], TAKEN).then_inc(combined, 1)
                        dve.wait_ge(combined, E.step(combined))
                V.tensor_scalar(flat(dsa_mask), flat(isc), TAKEN / 2, -BLOCKED, ALU.is_le, ALU.mult).then_inc(combined, 1)
                dve.wait_ge(combined, E.step(combined))
                V.scalar_tensor_tensor(out=flat(dsa_mask), in0=flat(dsa_mask), scalar=BLOCKED, in1=C("causal"),
                                       op0=ALU.add, op1=ALU.add).then_inc(combined, 1)
                dve.wait_ge(combined, E.step(combined))
                b = bank(f"{nm}.cs", SEQ + 16)
                V.memset(csT, 0.0).then_inc(combined, 1)
                dve.wait_ge(combined, E.step(combined))
                V.tensor_copy(csT[0:8, :], b[0:8, 0:SEQ]).then_inc(combined, 1)
                dve.wait_ge(combined, E.step(combined))
                V.tensor_copy(flat(cq), b[:, SEQ:SEQ + 16]).then_inc(combined, 1)
                dve.wait_ge(combined, E.step(combined, f"{nm}.cs'"))
                attention(f"{nm}.att")
                for n in range(3):
                    for j in range(2):
                        for i in range(2):
                            lab = f"{nm}.y{n}{j}.{i}"
                            k = 4 * j + 2 * i
                            if E.new(f"{nm}.m{(KD * n + k) // 2}.0'"):
                                dve.wait_ge(*E.at(f"{nm}.m{(KD * n + k) // 2}.0'"))
                            b = bank(lab)
                            mg, gt = flat(merged[:, k:k + 2, :]), flat(gates[:, KD * n + k:KD * n + k + 2, :])
                            if n == 0:
                                V.tensor_tensor(mg, b, gt, ALU.mult).then_inc(combined, 1)
                                dve.wait_ge(combined, E.step(combined, lab + "'"))
                            else:
                                V.tensor_tensor(gt, b, gt, ALU.mult).then_inc(combined, 1)
                                dve.wait_ge(combined, E.step(combined, lab + "'"))
                                V.tensor_tensor(mg, mg, gt, ALU.add).then_inc(combined, 1)
                                dve.wait_ge(combined, E.step(combined, f"{nm}.mg{k // 2}" if n == 2 else None))
                for j in range(4):
                    lab = f"{nm}.out{j}.0"
                    xv = x[:, 2 * j:2 * j + 2, 0:SEQ]
                    V.tensor_tensor(xv, xv, bank(lab).rearrange("p (a b) -> p a b", a=2), ALU.add).then_inc(combined, 1)
                    dve.wait_ge(combined, E.step(combined, lab + "'"))
                E.name_last(f"{nm}.out.x3")
            norm("final", gain=R("final"), to="x")
            if E.new("mod0.35'"):
                dve.wait_ge(*E.at("mod0.35'"))
            md = mods[:, 0, :, :].rearrange("p a b -> p (a b)")
            V.tensor_tensor(md, md, R("b2.0.mod_b"), ALU.add).then_inc(combined, 1)
            dve.wait_ge(combined, E.step(combined))
            prepare("b2.0.n1", 0, 0, "b2.0.ffn1_norm")
            norm("b2.0.n1")
            ffn("b2.0.ffn1", 0, TOK, 0)
            prepare("b2.0.nm", 0, 1, "b2.0.mix_norm")
            norm("b2.0.nm")
            if E.new("b2.0.ffn1_out.3"):
                dve.wait_ge(*E.at("b2.0.ffn1_out.3"))
            V.memset(m_y.rearrange("p a b c -> p (a b c)"), 0.0).then_inc(combined, 1)
            dve.wait_ge(combined, E.step(combined))
            for i in range(4):
                if E.new(f"b2.0.in.{10 + i}'"):
                    dve.wait_ge(*E.at(f"b2.0.in.{10 + i}'"))
                V.tensor_tensor(m_y[:, i, :, PAD:PAD + SEQ], m_ca[:, i, :].rearrange("p (g s) -> p g s", g=2),
                                squares[:, i, :].rearrange("p (g s) -> p g s", g=2), ALU.mult).then_inc(combined, 1)
                dve.wait_ge(combined, E.step(combined, f"b2.0.conv.glu{i}"))
            head_norm("b2.0.lora")
            head_norm("b2.0.heads")
            at, _ = PARAM["dw_w"]
            for i in range(4):
                out = m_yc[:, i, :].rearrange("p (g s) -> p g s", g=2)
                for k in range(TAPS):
                    src = m_y[:, i, :, k:k + SEQ]
                    wk = R("dw_w", TAPS * i + k, 1)
                    if k == 0:
                        V.tensor_scalar(out, src, wk, R("dw_b", i, 1), ALU.mult, ALU.add).then_inc(combined, 1)
                        dve.wait_ge(combined, E.step(combined))
                    else:
                        V.scalar_tensor_tensor(out=out, in0=src, scalar=wk, in1=out, op0=ALU.mult, op1=ALU.add).then_inc(combined, 1)
                        dve.wait_ge(combined, E.step(combined, f"b2.0.conv.y{i}" if k == TAPS - 1 else None))
            b = bank("b2.0.conv.mean")
            V.tensor_scalar(work[:, 0, :], b, -1.0 / 512, None, ALU.mult).then_inc(combined, 1)
            dve.wait_ge(combined, E.step(combined, "b2.0.conv.mean'"))
            for t in range(4):
                V.tensor_tensor(m_yc[:, t, :], m_yc[:, t, :], work[:, 0, :], ALU.add).then_inc(combined, 1)
                dve.wait_ge(combined, E.step(combined, f"b2.0.conv.c{t}"))
            if E.new("b2.0.conv.var'"):
                dve.wait_ge(*E.at("b2.0.conv.var'"))
            V.reciprocal(rs[:, :], rs[:, :]).then_inc(combined, 1)
            dve.wait_ge(combined, E.step(combined))
            for t in range(4):
                V.tensor_tensor(m_yc[:, t, :], m_yc[:, t, :], rs[:, :], ALU.mult).then_inc(combined, 1)
                dve.wait_ge(combined, E.step(combined, f"b2.0.conv.n{t}"))
            attention("b2.0.att")

            def add_mixer(nm, l, groups, per):
                for i in range(KD):
                    b = psum[:, E.bank(f"{nm}.out.{i // per}"), :]
                    if E.new(f"{nm}.out.{i // per}"):
                        dve.wait_ge(*E.at(f"{nm}.out.{i // per}"))
                    off = (i % per) * SEQ if per > 1 else 0
                    for g in range(groups):
                        xv = x[:, i, SEQ * g:SEQ * g + SEQ]
                        lab = f"{nm}.out.{i // per}'" if g == groups - 1 and i % per == per - 1 else None
                        V.scalar_tensor_tensor(out=xv, in0=b[:, off + SEQ * g:off + SEQ * g + SEQ],
                                               scalar=mods[:, l, 40 + i, g:g + 1], in1=xv,
                                               op0=ALU.mult, op1=ALU.add).then_inc(mixer_added, 1)
                        dve.wait_ge(mixer_added, E.step(mixer_added, lab))
                E.name_last(f"{nm}.out.x3")

            add_mixer("b2.0", 0, 2, 1)
            prepare("b2.0.n2", 0, 2, "b2.0.ffn2_norm")
            norm("b2.0.n2")
            ffn("b2.0.ffn2", 0, TOK, 2)
            if E.new("mod1.35'"):
                dve.wait_ge(*E.at("mod1.35'"))
            md = mods[:, 1, :, :].rearrange("p a b -> p (a b)")
            V.tensor_tensor(md, md, R("b2.1.mod_b"), ALU.add).then_inc(combined, 1)
            dve.wait_ge(combined, E.step(combined))
            prepare("b2.1.n1", 1, 0, "b2.1.ffn1_norm")
            norm("b2.1.n1")
            ffn("b2.1.ffn1", 1, TOK, 0)
            prepare("b2.1.nm", 1, 1, "b2.1.mix_norm")
            norm("b2.1.nm")
            V.tensor_scalar(R("nq_gain"), R("nq_gain"), HD ** -0.5, None, ALU.mult).then_inc(combined, 1)
            dve.wait_ge(combined, E.step(combined))
            head_norm("b2.1.heads")
            dve.wait_ge(s_bias, 16 * 4 * HEADS)
            for i in range(2 * HEADS):
                q = i % 2
                V.tensor_tensor(g_bias[:, i, :], g_bias[:, i, :], C("window")[:, SEQ * q:SEQ * q + SEQ], ALU.add).then_inc(combined, 1)
                dve.wait_ge(combined, E.step(combined))
            attention("b2.1.att")
            add_mixer("b2.1", 1, 1, 2)
            prepare("b2.1.n2", 1, 2, "b2.1.ffn2_norm")
            norm("b2.1.n2")
            ffn("b2.1.ffn2", 1, SEQ, 2)
            E.name_last("last.h7")




def chunked(w, cols):
    k, n = w.shape[0] // P, w.shape[1] // cols
    return np.ascontiguousarray(w.reshape(k, P, n, cols).transpose(2, 1, 0, 3)).reshape(n, P, k * cols)


def by_feature(v):
    return v.reshape(-1, P).T


def constants():
    out = {n: np.zeros((P, w), np.float32) for n, (_, w) in CONST.items()}
    i = np.arange(P)
    out["ident"][:] = np.eye(P)
    out["ones"][:] = 1
    out["sum64"][:] = i[:, None] // 64 == i[None, :] // 64
    out["sum32"][:] = i[:, None] // 32 == i[None, :] // 32
    out["sum96"][0:64, 0:64] = 1 / 64
    out["sum96"][64:96, 64:96] = 1 / 32
    for b in (0, HD):
        for j in range(8):
            out["rot_half"][b + j + 8, b + j] = -1
            out["rot_half"][b + j, b + j + 8] = 1
    for j in range(0, P, 2):
        for name in ("rot_pair",) + (("rot_q",) if 64 <= j < 96 else ()):
            out[name][j + 1, j] = -1
            out[name][j, j + 1] = 1
    pos = np.arange(SEQ, dtype=np.float32)
    inv = np.power(np.float32(500000.0), -np.arange(0, 16, 2, dtype=np.float32) / 16).astype(np.float32)
    ang = (pos[:, None] * inv[None, :]).astype(np.float32)
    c, s = np.ones((P, SEQ), np.float32), np.zeros((P, SEQ), np.float32)
    for b in (0, HD):
        c[b:b + 16] = np.concatenate([np.cos(ang), np.cos(ang)], 1).T
        s[b:b + 16] = np.concatenate([np.sin(ang), np.sin(ang)], 1).T
    out["cos_part"][:], out["sin_part"][:] = np.tile(c, (1, 2)), np.tile(s, (1, 2))
    for dim in (64, 32):
        n = dim // 4
        inv = (10000.0 ** (-np.arange(n, dtype=np.float32) / n)).astype(np.float32)
        t = np.arange(SEQ)
        row, col = (t // 64).astype(np.float32), (t % 64).astype(np.float32)
        ang = np.concatenate([row[:, None] * inv, col[:, None] * inv], -1).astype(np.float32)
        out[f"cos{dim}"][:] = np.tile(np.repeat(np.cos(ang).T, 2, 0), (P // dim, 1))
        out[f"sin{dim}"][:] = np.tile(np.repeat(np.sin(ang).T, 2, 0), (P // dim, 1))
    out["cos96"][:] = 1
    out["cos96"][64:96], out["sin96"][64:96] = out["cos32"][64:96], out["sin32"][64:96]
    q = np.arange(QT)[:, None] * P + i[None, :]
    k = np.arange(SEQ)
    causal = np.where(k[None, None, :] <= q[:, :, None], 0, BLOCKED)
    out["causal"][:] = causal.transpose(1, 0, 2).reshape(P, -1)
    cs = np.clip(q % 64 - 8, 0, 48)
    inside = (k % 64 >= cs[:, :, None]) & (k % 64 < cs[:, :, None] + 16)
    out["window"][:] = np.where(inside, 0, BLOCKED).transpose(1, 0, 2).reshape(P, -1)
    out["upto"][:] = (q[:, :, None] <= k[None, None, :]).astype(np.float32).transpose(1, 0, 2).reshape(P, -1)
    out["eps"][:], out["one"][:] = EPS, 1
    return np.concatenate([out[n] for n in CONST], 1)


def lay_out(I):
    W = {}
    for l in range(2):
        w = I["w_in"][l]
        for br in range(3):
            for i, part in enumerate("qkvg"):
                a = WIDTH * (4 * br + i)
                W[f"b1.{l}.{part}{br}"] = chunked(w[:, a:a + WIDTH], 256)
        W[f"b1.{l}.qi"] = chunked(w[:, 6144:6656], 256)
        ki = w[:, 6656:6720]
        W[f"b1.{l}.misc"] = chunked(np.concatenate([ki, ki, w[:, 6720:6736]], 1), 144)
        W[f"b1.{l}.merge"] = chunked(w[:, 6736:], 256)
        W[f"b1.{l}.branch"] = np.concatenate([chunked(I["w_branch"][l, n], 512) for n in range(3)])
        W[f"b1.{l}.out"] = chunked(I["w_out"][l], 256)
        g = lambda n: I[f"l{l}_{n}_2"]
        W[f"mod{l}"] = chunked(g("mod_w"), 256)
        for f in ("ffn1", "ffn2"):
            w2 = chunked(g(f + "_w_in"), 256)
            W[f"b2.{l}.{f}_in"] = np.stack([w2[:11], w2[11:]], 1).reshape(w2.shape)
            W[f"b2.{l}.{f}_out"] = chunked(g(f + "_w_out"), P)
    w = I["l0_w_in_2"]
    W["b2.0.in"] = chunked(np.concatenate([w[:, :256]] + [w[:, 256:288]] * 4 + [w[:, 288:]], 1), 256)
    W["b2.0.uq"] = chunked(I["l0_mla_w_uq_2"], 768)
    u = I["l0_mla_w_ukv_2"].reshape(256, HEADS, 2, HD).transpose(0, 2, 1, 3).reshape(256, 1024)
    W["b2.0.ukv"] = chunked(u, 1024)
    W["b2.0.out"] = chunked(I["l0_w_out_2"], 256)
    w = I["l1_w_in_2"]
    pairs = [j for i in range(4) for j in (i, i + 4)]
    cq = w[:, 1280:1792].reshape(D, HEADS, HD)[:, pairs].reshape(D, WIDTH)
    W["b2.1.in"] = chunked(np.concatenate([w[:, 0:128], w[:, 256:768], w[:, 128:256], w[:, 768:1280], cq, w[:, 1792:]], 1), 256)
    wo = I["l1_w_out_2"]
    wo = np.concatenate([wo[:WIDTH].reshape(HEADS, HD, D)[pairs].reshape(WIDTH, D), wo[WIDTH:]])
    W["b2.1.out"] = chunked(wo, 256)

    prm = {}
    for l in range(2):
        prm[f"b1.{l}.gain"] = by_feature(I["norm_gain"][l])
        prm[f"b1.{l}.fbias"] = np.tile(I["forget_bias"][l], (P, 2))
        prm[f"b2.{l}.mod_b"] = np.repeat(by_feature(I[f"l{l}_mod_b_2"]), 2, 1)
        for n in ("ffn1_norm", "mix_norm", "ffn2_norm"):
            prm[f"b2.{l}.{n}"] = np.repeat(by_feature(I[f"l{l}_{n}_2"]), 2, 1)
    prm["final"] = by_feature(I["final_gain"])
    prm["q_norm"] = by_feature(I["l0_mla_q_norm_2"])
    prm["kv_norm"] = by_feature(I["l0_mla_kv_norm_2"])
    for n in "qk":
        v = I[f"l0_mla_{n}_gain_2"]
        prm[f"{n}_gain"] = np.concatenate([v, v[64:96]])[:, None]
    prm["glu_b"] = by_feature(I["l0_conv_glu_b_2"])
    prm["dw_w"] = I["l0_conv_dw_w_2"].reshape(TAPS, 4, P).transpose(2, 1, 0).reshape(P, 4 * TAPS)
    prm["dw_b"] = by_feature(I["l0_conv_dw_b_2"])
    prm["ln_g"] = by_feature(I["l0_conv_ln_g_2"])
    prm["ln_b"] = by_feature(I["l0_conv_ln_b_2"])
    for n, f in (("gq", "gqa_q"), ("gk", "gqa_k"), ("nq", "na_q"), ("nk", "na_k")):
        prm[f"{n}_gain"] = np.tile(I[f"l1_{f}_gain_2"], 2)[:, None]
    prm["cond"] = np.stack([by_feature(I["c_2"][0]), by_feature(I["c_ctx_2"])], 2).reshape(P, 2 * KD)
    for n, (_, w_) in PARAM.items():
        assert prm[n].shape == (P, w_), (n, prm[n].shape)

    onehot = np.zeros((P, 1024), np.float32)
    for hh in range(HEADS):
        onehot[hh, P * hh:P * hh + P] = -1
    wide = np.pad(I["l1_na_rpb_2"], ((0, 0), (0, 0), (48, 48)))
    bias = np.stack([wide[:, :, 63 - c:127 - c] for c in range(64)], 2)
    small = dict(consts=constants(), params=np.concatenate([prm[n] for n in PARAM], 1), onehot=onehot,
                 x=I["x"][0].T.reshape(KD, P, SEQ).transpose(1, 0, 2), ctx=I["ctx_2"][0].T.reshape(KD, P, CTX).transpose(1, 0, 2),
                 bias=bias)
    return W, {n: np.ascontiguousarray(v, np.float32) for n, v in small.items()}


def build(nc, book, shapes):
    t = {n: nc.dram_tensor("in_" + n, s, F32, kind="ExternalInput").ap() for n, s in shapes.items()}
    out = nc.dram_tensor("outT", (P, KD, SEQ), F32, kind="ExternalOutput").ap()
    weights = {s: t["w_" + s.replace(".", "_")] for s, _, _ in weight_plan()}
    program(nc, book, weights, t["consts"], t["params"], t["onehot"], t["x"], t["ctx"], t["bias"], out)


def kernel(**inputs):
    import concourse.bacc as bacc
    from concourse.bass_utils import run_bass_kernel_spmd

    W, arrays = lay_out({n: np.asarray(v) for n, v in inputs.items()})
    for s, v in W.items():
        arrays["w_" + s.replace(".", "_")] = v
    book = None
    for _ in range(2):
        nc = bacc.Bacc("TRN2", target_bir_lowering=False, num_devices=1)
        book = Book(book)
        build(nc, book, {n: v.shape for n, v in arrays.items()})
    r = run_bass_kernel_spmd(nc, [{"in_" + n: v for n, v in arrays.items()}], core_ids=[0])
    y = np.asarray(r.results[0]["outT"])
    return np.ascontiguousarray(y.transpose(1, 0, 2).reshape(D, SEQ).T)[None]
```

```python
from contextlib import ExitStack, contextmanager

import numpy as np

import concourse.bass as bass
from concourse import mybir
from concourse.alu_op_type import AluOpType as ALU

ACT = mybir.ActivationFunctionType
F32 = mybir.dt.float32
F32R = mybir.dt.float32r
AX_X = mybir.AxisListType.X

P = 128
D = 1024
KD = D // P
SEQ = 256
CTX = 256
TOK = SEQ + CTX
QT = SEQ // P
HD = 64
HEADS = 8
WIDTH = HEADS * HD
KW = WIDTH // P
D_FF = 2816
KF = D_FF // P
KH = KF // 2
N_MOD = 9
MT = N_MOD * KD
TAPS = 31
PAD = TAPS // 2
YW = SEQ + 2 * PAD
TOP = 64
EPS = 1e-6
BLOCKED = -1e30
TAKEN = -3e38
SLOTS = 4
SLOT = KD * 256
BANKS = 8
ROTATING = 6
BANK = 512
PARTS = 4
LAG = 3
PIECES = 2 * KH + KD



UNITS = {"b1.0.att": 24, "b1.1.att": 24, "b2.0.att": 24, "b2.1.att": 32}
DVE_CONV, POOL_CONV = 1, 2
PE_CONV = range(DVE_CONV + POOL_CONV, 4)
MOD_PLACES = [("b1.0.att", 9), ("b1.1", 2), ("b1.1.att", 11), ("b2.0.n1", 2), ("b2.0.nm", 2), ("b2.0.heads", 16),
              ("b2.0.att", 14), ("b2.0.n2", 2), ("b2.1.n1", 2), ("b2.1.nm", 2), ("b2.1.heads", 10), ("b2.1.att", 0)]
MODS = {}
for place, n_mods in MOD_PLACES:
    done = sum(len(m) for m in MODS.values())
    MODS[place] = [divmod(c, MT // 2) for c in range(done, done + n_mods)]
assert sum(n for _, n in MOD_PLACES) == MT
MODS_EVERY = {"b2.0.heads": 1, "b2.1.heads": 1}

def fillers(nm):
    steps = UNITS[nm] + 3
    out = [[] for _ in range(steps)]

    def spread(kind, l, a, b):
        for c in range(a, b):
            out[(c - a) * steps // (b - a)].append((kind, l, c))

    for i, (l, c) in enumerate(MODS[nm]):
        out[i * steps // max(1, len(MODS[nm]))].append(("mod", l, c))
    if nm.startswith("b1"):
        l = int(nm[3])
        for j in range(12):
            out[2 * j + 1].append(("merge", l, j))
    elif nm == "b2.0.att":
        spread("tap", 0, 0, DVE_CONV * TAPS)
    return out


def weight_plan():
    plan = []

    def mods(place):
        plan.extend((f"mod{l}", 1, KD * 256) for l, _ in MODS[place])

    def fill(nm):
        for kind, l, _ in sum(fillers(nm), []):
            if kind == "mod":
                plan.append((f"mod{l}", 1, KD * 256))
            if kind == "merge":
                plan.append((f"b1.{l}.merge", 1, KD * 256))

    def ffn(nm):
        for half in range(2):
            plan.extend([(f"{nm}_in{half}", KH, KD * 256), (f"{nm}_out{half}", KD, KH * P)])

    for l in range(2):
        if l == 1:
            mods("b1.1")
        for br in range(2):
            for part in "qkvg":
                plan.append((f"b1.{l}.{part}{br}", 2, KD * 256))
        plan += [(f"b1.{l}.qi", 2, KD * 256), (f"b1.{l}.misc", 1, KD * 144)]
        for part in "qkvg":
            plan.append((f"b1.{l}.{part}2", 2, KD * 256))
        fill(f"b1.{l}.att")
        plan += [(f"b1.{l}.branch", 6, KW * 512), (f"b1.{l}.out", 4, KD * 256)]
    for l in range(2):
        mods(f"b2.{l}.n1")
        ffn(f"b2.{l}.ffn1")
        mods(f"b2.{l}.nm")
        if l == 0:
            plan += [("b2.0.in", 7, KD * 256), ("b2.0.uq", 2, 3 * 384), ("b2.0.ukv", 1, 2 * 1024)]
        else:
            plan += [("b2.1.in", 9, KD * 256)]
        mods(f"b2.{l}.heads")
        fill(f"b2.{l}.att")
        plan += [(f"b2.{l}.out", 4, KD * 256)]
        if l == 0:
            mods("b2.0.n2")
        ffn(f"b2.{l}.ffn2")
    return plan


LOOPED = {s: (n % SLOTS, n // SLOTS) for s, n, _ in weight_plan() if "_in" in s}



def columns(items):
    at, out = 0, {}
    for name, n in items:
        out[name] = (at, n)
        at += n
    return out, at


CONST, N_CONST = columns([
    ("ident", P), ("ones", P), ("sum64", P), ("sum32", P), ("rot_half", P), ("rot_pair", P), ("rot_q", P), ("sum96", P),
    ("cos_part", 512), ("sin_part", 512), ("cos64", 256), ("sin64", 256), ("cos96", 256), ("sin96", 256),
    ("causal", 512), ("window", 512), ("upto", 512), ("eps", 1), ("one", 1)])
PARAM, N_PARAM = columns(
    [(f"b1.{l}.gain", KD) for l in range(2)] + [(f"b1.{l}.fbias", 16) for l in range(2)] + [("final", KD)]
    + [(f"b2.{l}.mod_b", 2 * MT) for l in range(2)]
    + [(f"b2.{l}.{n}", 2 * KD) for l in range(2) for n in ("ffn1_norm", "mix_norm", "ffn2_norm")]
    + [("q_norm", 3), ("kv_norm", 2), ("q_gain", 1), ("k_gain", 1),
       ("glu_b", 8), ("dw_w", 4 * TAPS), ("dw_b", 4), ("ln_g", 4), ("ln_b", 4),
       ("gq_gain", 1), ("gk_gain", 1), ("nq_gain", 1), ("nk_gain", 1), ("cond", 2 * KD)])


SEMAPHORES = (
    "attended", "combined", "copied", "exponentiated", "piece_multiplied", "gated",
    "hidden_written", "weights_rounded", "weights_split", "ffn_added", "mixer_added", "modulation_copied", "modulation_multiplied", "modulation_turned", "multiplied", "normed",
    "partnered", "probs_ready", "projected", "rooted", "roped", "scales_prepared",
    "shifted", "squared", "summed", "tap_added", "tap_multiplied", "pool_tap_added", "diagonal_built")


class Book:

    def __init__(self, before=None):
        self.before = before
        self.labels, self.strides, self.turns, self.banks = {}, {}, {}, {}


class Engine:

    def __init__(self, book, sems):
        self.book, self.sems = book, sems
        self.count = {}
        self.loop_name = self.turn = self.last = self.next_label = None
        self.seen = {}

    def step(self, sem, label=None):
        n = self.count[sem.name] = self.count.get(sem.name, 0) + 1
        self.last = (sem.name, n, self.loop_name)
        for name in (label, self.next_label):
            if name is not None:
                assert name not in self.book.labels, name
                self.book.labels[name] = self.last
        self.next_label = None
        if self.loop_name is None:
            return n
        return self.turn * self.stride(self.loop_name, sem.name) + n

    def name_last(self, label):
        self.book.labels[label] = self.last

    def name_next(self, label):
        self.next_label = label

    def stride(self, loop, sem):
        return self.book.before.strides[loop, sem] if self.book.before else 1

    def at(self, label, shift=0, it=None):
        sem, n, loop = self.book.before.labels[label]
        if loop is None:
            return self.sems[sem], n
        stride = self.stride(loop, sem)
        if it is None and loop == self.loop_name:
            return self.sems[sem], self.turn * stride + (n + shift * stride)
        return self.sems[sem], n + (self.book.before.turns[loop] - 1 if it is None else it) * stride

    def new(self, label, shift=0, it=None):
        if self.book.before is None:
            return False
        sem, n, loop = self.book.before.labels[label]
        if self.loop_name is not None:
            return loop == self.loop_name or self.seen.get(sem, 0) < n
        value = self.at(label, shift, it)[1]
        if self.seen.get(sem, 0) >= value:
            return False
        self.seen[sem] = value
        return True

    @contextmanager
    def loop(self, engine, name, turns, first=0):
        before = dict(self.count)
        with engine.Fori(first, turns) as self.turn:
            self.loop_name = name
            yield self.turn
        self.loop_name = None
        self.book.turns[name] = turns
        for sem, n in self.count.items():
            stride = n - before.get(sem, 0)
            self.book.strides[name, sem] = stride
            self.count[sem] = before.get(sem, 0) + stride * (turns - first)

    def bank(self, label):
        return self.book.before.banks[label] if self.book.before else 0


def program(nc, book, weights, d_const, d_param, d_onehot, d_x, d_ctx, d_bias, d_out):
    plan = weight_plan()
    stage_of, start = [], {}
    for s, n, w in plan:
        start.setdefault(s, []).append(len(stage_of))
        stage_of += [s] * n
    width = {s: w for s, _, w in plan}

    with ExitStack() as ctx:
        def sb(name, shape):
            return ctx.enter_context(nc.sbuf_tensor(name, shape, F32))

        SLAB = 31880
        slab_at = (nc.sbuf_base + 63) // 64 * 64
        slab = sb("slab", [P, SLAB])
        slab_used = [0, 0]

        def mixer_part(*shape):
            n = int(np.prod(shape))
            a = slab_used[0]
            slab_used[0] += n
            assert slab_used[0] <= SLAB
            v = slab[:, a:a + n]
            return v.rearrange("p (a b) -> p a b", a=shape[0]) if len(shape) == 2 else v

        def ffn_part(name, *shape):
            t = nc.alloc_sbuf_tensor_at(name, [P] + list(shape), F32R, offset=slab_at + 4 * slab_used[1])
            slab_used[1] += int(np.prod(shape))
            assert slab_used[1] <= SLAB
            return t

        h_hi, h_lo = (ffn_part(f"h_{n}", KD, TOK) for n in ("hi", "lo"))
        hidden_hi, hidden_lo = (ffn_part(f"hidden_{n}", KH, TOK) for n in ("hi", "lo"))
        w_hi, w_lo = (ffn_part(f"w_{n}", PARTS, KH * P) for n in ("hi", "lo"))
        wring = sb("wring", [P, SLOTS, SLOT])
        cst = sb("cst", [P, N_CONST])
        prm = sb("prm", [P, N_PARAM])
        x = sb("x", [P, KD, TOK])
        h = mixer_part(KD, TOK)
        squares = sb("squares", [P, 4, BANK])
        rs = sb("rs", [P, BANK])
        work = mixer_part(2, BANK)
        probs = mixer_part(3, BANK)
        probsT = mixer_part(2, BANK)
        more_gates = mixer_part(12, SEQ)
        stat = sb("stat", [P, 4, 8])
        csil = sb("csil", [P, KD, 2])
        mods = sb("mods", [P, 2, MT, 2])
        mscale = sb("mscale", [P, KD, 2])
        mod_rows = sb("mod_rows", [P, 2, 256])
        ARENA = 21112
        arena = mixer_part(ARENA)
        psum = ctx.enter_context(nc.psum_tensor("psum", [P, BANKS, BANK], F32))
        sems = {n: ctx.enter_context(nc.semaphore(n)) for n in SEMAPHORES}
        (attended, combined, copied, exponentiated, piece_multiplied, gated,
         hidden_written, weights_rounded, weights_split, ffn_added, mixer_added, modulation_copied, modulation_multiplied, modulation_turned, multiplied, normed,
         partnered, probs_ready, projected, rooted, roped, scales_prepared,
         shifted, squared, summed, tap_added, tap_multiplied, pool_tap_added, diagonal_built) = sems.values()
        landed = [ctx.enter_context(nc.semaphore(f"weights_landed{i}")) for i in range(SLOTS)]
        s_const = ctx.enter_context(nc.semaphore("constants_landed"))
        s_x = ctx.enter_context(nc.semaphore("x_landed"))
        s_ctx = ctx.enter_context(nc.semaphore("context_landed"))
        s_onehot = ctx.enter_context(nc.semaphore("onehot_landed"))
        s_bias = ctx.enter_context(nc.semaphore("bias_landed"))
        s_out = ctx.enter_context(nc.semaphore("output_written"))

        def C(name):
            at, n = CONST[name]
            return cst[:, at:at + n]

        def R(name, i=0, n=None):
            at, m = PARAM[name]
            return prm[:, at + i:at + (m if n is None else i + n)]

        class Space:

            def __init__(self):
                self.at = 0

            def take(self, *shape):
                n = int(np.prod(shape))
                v = arena[:, self.at:self.at + n]
                self.at += n
                assert self.at <= ARENA, self.at
                if len(shape) == 2:
                    v = v.rearrange("p (a b) -> p a b", a=shape[0])
                if len(shape) == 3:
                    v = v.rearrange("p (a b c) -> p a b c", a=shape[0], b=shape[1])
                return v

        s1 = Space()
        qT = [s1.take(KW, SEQ) for _ in range(3)]
        kT = [s1.take(KW, SEQ) for _ in range(3)]
        vv = [s1.take(QT, WIDTH) for _ in range(3)]
        gg = [s1.take(KW, SEQ) for _ in range(3)]
        qiT = s1.take(KW, SEQ)
        kiT = s1.take(SEQ)
        onehot = s1.take(1024)
        merged = s1.take(KD, SEQ)
        oT = [s1.take(KW, SEQ) for _ in range(3)]
        isc = s1.take(QT, SEQ)
        dsa_mask = s1.take(QT, SEQ)
        wl = s1.take(QT, 16)
        fz = s1.take(4, 16)
        csT = s1.take(SEQ)
        cq = s1.take(QT, 8)
        top8 = s1.take(8)

        def gates(j):
            if j < 6:
                return more_gates[:, 2 * j:2 * j + 2, :]
            return (qT[0], kT[0], qT[1])[(j - 6) // 2][:, 2 * (j % 2):2 * (j % 2) + 2, :]

        s2 = Space()
        m_ckv = s2.take(2, TOK)
        m_cq = s2.take(3, TOK)
        m_q = s2.take(HEADS, TOK)
        m_k = s2.take(HEADS, TOK)
        m_kr = s2.take(TOK)
        m_v = s2.take(4, WIDTH)
        m_ca = s2.take(4, TOK)
        m_y = s2.take(4, 2, YW)
        m_yc = m_ca
        m_diag = s2.take(4, P)
        m_o = h

        s3 = Space()
        g_ck = s3.take(TOK)
        g_cv = s3.take(4, P)
        g_nk = s3.take(4, TOK)
        g_nv = s3.take(4, WIDTH)
        g_cq = s3.take(4, SEQ)
        g_nq = s3.take(4, SEQ)
        g_o = h[:, :, 0:SEQ]
        g_bias = s3.take(2 * HEADS, SEQ)

        def flat(v):
            return v.rearrange("p a b -> p (a b)")

        def slot_of(c):
            return wring[:, c % SLOTS, :]

        def used(c):
            s = stage_of[c]
            k = c - max(a for a in start[s] if a <= c)
            if s in LOOPED and k >= LOOPED[s][0]:
                k -= LOOPED[s][0]
                return f"w{c - k + k % SLOTS}", k // SLOTS
            return f"w{c}", None

        def units_of(kind, l=0):
            out = []
            if kind in ("moba", "dsa", "fox"):
                br = ("moba", "dsa", "fox").index(kind)
                for hh in range(HEADS):
                    rows = slice(HD * (hh % 2), HD * (hh % 2) + HD)
                    mms = [(qT[br][rows, hh // 2, P * g:P * g + P], kT[br][rows, hh // 2, :]) for g in range(QT)]
                    out.append(dict(
                        G=QT, K=SEQ, mms=mms, kind=kind, head=hh, scale=HD ** -0.5 if kind != "fox" else 1.0,
                        v=[vv[br][:, t, HD * hh:HD * hh + HD] for t in range(2)], half=hh % 2,
                        cols=(0, SEQ), last=hh % 2 == 1, dst=oT[br][:, hh // 2, :], gate=gg[br][:, hh // 2, :]))
            if kind == "mla_lat":
                for hh in range(HEADS):
                    for q in range(QT):
                        out.append(dict(
                            G=1, K=TOK, kind="none", scale=96 ** -0.5, half=hh % 2, head=hh,
                            mms=[(m_q[0:96, hh, P * q:P * q + P], m_k[0:96, hh, :])],
                            v=[m_v[:, t, HD * hh:HD * hh + HD] for t in range(4)], cols=(P * q, P),
                            last=hh % 2 == 1 and q == 1, dst=m_o[:, hh // 2, 0:SEQ], gate=None))
            if kind == "mla_ctx":
                for hh in range(HEADS):
                    out.append(dict(
                        G=2, K=CTX, kind="none", scale=96 ** -0.5, half=hh % 2, head=hh,
                        mms=[(m_q[0:96, hh, SEQ + P * q:SEQ + P * q + P], m_k[0:96, hh, SEQ:TOK]) for q in range(2)],
                        v=[m_v[:, t, HD * hh:HD * hh + HD] for t in (2, 3)], cols=(0, CTX),
                        last=hh % 2 == 1, dst=m_o[:, hh // 2, SEQ:TOK], gate=None))
            if kind == "gqa":
                for j in range(4):
                    for kv in range(2):
                        rows = slice(HD * kv, HD * kv + HD)
                        for q in range(QT):
                            out.append(dict(
                                G=1, K=TOK, kind="none", scale=HD ** -0.5, half=kv, head=j,
                                mms=[(g_cq[rows, j, P * q:P * q + P], g_ck[rows, :])],
                                v=[g_cv[:, t, HD * kv:HD * kv + HD] for t in range(4)], cols=(P * q, P),
                                last=kv == 1 and q == 1, dst=g_o[:, j, :], gate=None))
            if kind == "na":
                for hh in range(HEADS):
                    rows = slice(HD * (hh % 2), HD * (hh % 2) + HD)
                    for q in range(QT):
                        out.append(dict(
                            G=1, K=TOK, kind="na", scale=1.0, half=hh % 2, head=hh, q=q,
                            mms=[(g_nq[rows, hh // 2, P * q:P * q + P], g_nk[rows, hh // 2, :])],
                            v=[g_nv[:, t, HD * hh:HD * hh + HD] for t in range(4)], cols=(P * q, P),
                            last=hh % 2 == 1 and q == 1, dst=g_o[:, 4 + hh // 2, :], gate=None))
            return out

        ATT = {}
        for l in range(2):
            ATT[f"b1.{l}.att"] = [u for k in ("moba", "dsa", "fox") for u in units_of(k)]
        ATT["b2.0.att"] = units_of("mla_lat") + units_of("mla_ctx")
        ATT["b2.1.att"] = units_of("gqa") + units_of("na")
        assert all(len(ATT[n]) == UNITS[n] for n in UNITS)

        BEFORE = {"b1.0": None, "b1.1": "b1.0.out.x", "final": "b1.1.out.x",
                  "b2.0.n1": "final.h", "b2.0.nm": "b2.0.ffn1_out.x", "b2.0.n2": "b2.0.out.x",
                  "b2.1.n1": "b2.0.ffn2_out.x", "b2.1.nm": "b2.1.ffn1_out.x", "b2.1.n2": "b2.1.out.x"}
        NORM_N = {nm: SEQ if nm in ("b1.0", "b1.1", "final", "b2.1.n2") else TOK for nm in BEFORE}

        def heads_ready(nm, u):
            if nm.startswith("b1"):
                return nm.replace("att", "cs'") if u["kind"] == "fox" else nm.replace("att", "rki'")
            return "b2.0.heads.kr_copied" if nm == "b2.0.att" else "b2.1.heads.nqh.n3"

        def mixed_ready(nm, k):
            if nm == "b2.0":
                return f"b2.0.att.o{16 + 2 * k + 1}" if k < 4 else f"b2.0.conv.o{k - 4}"
            return f"b2.1.att.o{4 * k + 3}"

        def head_norms(nm):
            out = []

            def one(name, tiles, total, mat, count, gains, ready, rope=None):
                out.append(dict(name=f"{nm}.{name}", tiles=tiles, total=total, mat=mat, count=count, gains=gains,
                                ready=ready, rope=rope))
            if nm == "b2.0.lora":
                one("ckv", [m_ckv[:, t, :] for t in range(2)], True, "ones", 256, [R("kv_norm", t, 1) for t in range(2)],
                    ["b2.0.in.e0", "b2.0.in.e1"])
                one("kr", [m_kr], False, "sum32", 32, [R("k_gain")], ["b2.0.in.e2"], ("cos96", "sin96"))
                one("cq", [m_cq[:, t, :] for t in range(3)], True, "ones", 384, [R("q_norm", t, 1) for t in range(3)],
                    ["b2.0.in.e3", "b2.0.in.e4", "b2.0.in.e5"])
            if nm == "b2.0.heads":
                one("q", [m_q[0:96, t, :] for t in range(HEADS)], False, "sum96", 1, [R("q_gain")[0:96, :]] * HEADS,
                    [f"b2.0.uq.{t}'" for t in range(HEADS)], ("cos96", "sin96"))
                one("k", [m_k[0:64, t, :] for t in range(HEADS)], False, "sum96", 1, [R("k_gain")[0:64, :]] * HEADS,
                    [f"b2.0.ukv.{t}'" for t in range(HEADS)])
            if nm == "b2.1.heads":
                one("ck", [g_ck], False, "sum64", 64, [R("gk_gain")], ["b2.1.in.e0"], ("cos64", "sin64"))
                one("nk", [g_nk[:, t, :] for t in range(4)], False, "sum64", 64, [R("nk_gain")] * 4,
                    [f"b2.1.in.e{1 + t}" for t in range(4)])
                one("cqh", [g_cq[:, t, :] for t in range(4)], False, "sum64", 64, [R("gq_gain")] * 4,
                    [f"b2.1.cq.e{t // 2}" for t in range(4)], ("cos64", "sin64"))
                one("nqh", [g_nq[:, t, :] for t in range(4)], False, "sum64", 64, [R("nq_gain")] * 4,
                    [f"b2.1.nq.e{t // 2}" for t in range(4)])
            return out

        FFNS = ["b2.0.ffn1", "b2.0.ffn2", "b2.1.ffn1", "b2.1.ffn2"]
        VACATED = {"b2.0.ffn1": "b1.1.out3.0", "b2.0.ffn2": "b2.0.out.0", "b2.1.ffn1": None, "b2.1.ffn2": "b2.1.out.0"}

        def piece_number(nm, half, i=0):
            return (2 * FFNS.index(nm) + half) * PIECES + i

        def tile_number(nm, half, t=0):
            return (2 * FFNS.index(nm) + half) * KH + t

        def piece_chunk(nm, half, i):
            if i < 2 * KH:
                return start[f"{nm}_in{half}"][0] + i // 2
            return start[f"{nm}_out{half}"][0] + i - 2 * KH

        def raw_piece(c, i):
            if i < 2 * KH:
                return slot_of(c)[:, 0:KD * 256].rearrange("p (k n) -> p k n", n=256)[:, :, P * (i % 2):P * (i % 2) + P]
            return slot_of(c)[:, 0:KH * P].rearrange("p (k n) -> p k n", n=P)

        def part_piece(parts, q, i):
            n = KD if i < 2 * KH else KH
            return parts[:, q % PARTS, 0:n * P].rearrange("p (k n) -> p k n", n=P)

        block = ctx.enter_context(nc.Block())

        @block.sync
        def _(sp):
            E = Engine(book, sems)
            sp.dma_start(cst[:, :], d_const).then_inc(s_const, 16)
            sp.dma_start(prm[:, :], d_param).then_inc(s_const, 16)
            sp.dma_start(x[:, :, 0:SEQ], d_x).then_inc(s_x, 16)
            sp.dma_start(onehot, d_onehot).then_inc(s_onehot, 16)
            for c, s in enumerate(stage_of):
                first = max(a for a in start[s] if a <= c)
                k = c - first
                w = width[s]
                n_chunks = len(stage_of)
                base = k + sum(n for (s2_, n, _), a in zip(plan, np.cumsum([0] + [n for _, n, _ in plan])[:-1])
                               if s2_ == s and a < first)
                lead, turns = LOOPED.get(s, (n_chunks, 0))
                if k >= lead + SLOTS:
                    if k > lead + SLOTS:
                        continue
                    with E.loop(sp, s, turns, first=1) as it:
                        for u in range(SLOTS):
                            if E.new(f"w{first + lead + u}", shift=-1):
                                sp.wait_ge(*E.at(f"w{first + lead + u}", shift=-1))
                            sp.dma_start(slot_of(first + lead + u)[:, 0:w],
                                         weights[s][bass.ds(it * SLOTS + (lead + u), 1), :, :].rearrange("a p w -> (a p) w"))\
                              .then_inc(landed[(first + lead + u) % SLOTS], 16)
                    continue
                if c >= SLOTS:
                    label, turn = used(c - SLOTS)
                    if E.new(label, it=turn):
                        sp.wait_ge(*E.at(label, it=turn))
                sp.dma_start(slot_of(c)[:, 0:w], weights[s][base, :, :]).then_inc(landed[c % SLOTS], 16)
                if s == "b1.0.q0" and k == 1:
                    sp.dma_start(x[:, :, SEQ:TOK], d_ctx).then_inc(s_ctx, 16)
                if s == "b2.1.in" and k == 8:
                    if E.new("b2.1.ffn1_out.x7"):
                        sp.wait_ge(*E.at("b2.1.ffn1_out.x7"))
                    for r in range(4):
                        for hh in range(HEADS):
                            q, part = divmod(r, 2)
                            sp.dma_start(
                                g_bias[HD * part:HD * part + HD, 2 * hh + q, :].rearrange("c (j k) -> c j k", j=4),
                                d_bias[hh, 7 - r:11 - r, :, :].rearrange("j c k -> c j k")).then_inc(s_bias, 16)
            if E.new("last.h7"):
                sp.wait_ge(*E.at("last.h7"))
            sp.dma_start(d_out, x[:, :, 0:SEQ]).then_inc(s_out, 16)
            sp.wait_ge(s_out, 16)

        @block.tensor
        def _(pe):
            E = Engine(book, sems)
            state = dict(c=0, bank=0, o=0)
            occupant = {}

            def take(label, rotating=BANKS, fixed=None):
                b = state["bank"] % rotating if fixed is None else fixed
                if fixed is None:
                    state["bank"] = (b + 1) % rotating
                if b in occupant:
                    if E.new(occupant[b] + "'"):
                        pe.wait_ge(*E.at(occupant[b] + "'"))
                occupant[b] = label
                book.banks[label] = b
                return psum[:, b, :]

            def next_chunk():
                c = state["c"]
                state["c"] += 1
                pe.wait_ge(landed[c % SLOTS], 16 * (c // SLOTS + 1))
                return c, slot_of(c)

            def product(out, lhsT, rhs, k, n):
                return nc.tensor.matmul(out, lhsT, rhs, start=(k == 0), stop=(k == n - 1))

            def features(nm, c, w, cols, rhs, N, tiles, first=0, rotating=BANKS):
                per = BANK // N
                wv = w[:, 0:len(rhs) * cols].rearrange("p (k n) -> p k n", n=cols)
                for t in range(tiles):
                    if t % per == 0:
                        label = f"{nm}.{first + t // per}"
                        acc = take(label, rotating)
                    for k, (r, lab) in enumerate(rhs):
                        if t == 0 and lab:
                            if E.new(lab):
                                pe.wait_ge(*E.at(lab))
                        mm = product(acc[:, N * (t % per):N * (t % per) + N], wv[:, k, P * t:P * t + P], r, k, len(rhs))
                    if t % per == per - 1 or t == tiles - 1:
                        if t == tiles - 1 and c is not None:
                            E.name_next(f"w{c}")
                        mm.then_inc(projected, 1)
                        E.step(projected, label)

            def tokens(nm, c, w, cols, a, b, lhs, ntok, first=0, close=True):
                n = b - a
                per = BANK // n
                wv = w[:, 0:len(lhs) * cols].rearrange("p (k n) -> p k n", n=cols)
                for t in range(ntok):
                    if t % per == 0:
                        label = f"{nm}.{first + t // per}"
                        acc = take(label)
                    for k, (r, lab) in enumerate(lhs):
                        if lab:
                            if E.new(lab):
                                pe.wait_ge(*E.at(lab))
                        mm = product(acc[:, n * (t % per):n * (t % per) + n], r[:, P * t:P * t + P], wv[:, k, a:b], k, len(lhs))
                    if t % per == per - 1 or t == ntok - 1:
                        if t == ntok - 1 and close:
                            E.name_next(f"w{c}")
                        mm.then_inc(projected, 1)
                        E.step(projected, label)

            def normed(nm, N):
                return [(h[:, k, 0:N], f"{nm}.h{k}") for k in range(KD)]

            def norm(nm):
                acc = take(f"{nm}.sum")
                for k in range(KD):
                    if E.new(f"{nm}.sq{k}"):
                        pe.wait_ge(*E.at(f"{nm}.sq{k}"))
                    mm = product(acc[:, 0:NORM_N[nm]], C("ones"), squares[:, k % 4, 0:NORM_N[nm]], k, KD)
                    mm.then_inc(summed, 1)
                    E.step(summed, f"{nm}.c{k}")
                if MODS.get(nm):
                    after = nm.replace(".n", ".ffn")
                    bank = ((piece_number(after, 0) if after in FFNS else state["bank"]) + 6) % BANKS
                    modulation_beside(nm, bank)

            def rotate(nm, view, mat, ready, N):
                acc = take(nm)
                if E.new(ready):
                    pe.wait_ge(*E.at(ready))
                rows = view.shape[0]
                product(acc[0:rows, 0:N], C(mat)[0:rows, 0:rows], view, 0, 1).then_inc(partnered, 1)
                E.step(partnered, nm)

            def attention(nm):
                units, fill = ATT[nm], fillers(nm)
                n = len(units)
                for t in range(n + 3):
                    if t < n:
                        u = units[t]
                        if E.new(heads_ready(nm, u)):
                            pe.wait_ge(*E.at(heads_ready(nm, u)))
                        if u["kind"] == "fox":
                            hh = u["head"]
                            acc = take(f"{nm}.B{t}", ROTATING)
                            for g in range(2):
                                out = acc[:, SEQ * g:SEQ * g + SEQ]
                                product(out, onehot[:, P * hh:P * hh + P], csT, 0, 2)
                                mm = product(out, C("ident"), C("causal")[:, SEQ * g:SEQ * g + SEQ], 1, 2)
                            mm.then_inc(attended, 1)
                            E.step(attended, f"{nm}.B{t}")
                        acc = take(f"{nm}.S{t}", ROTATING)
                        for g, (lh, rh) in enumerate(u["mms"]):
                            mm = product(acc[:, g * u["K"]:(g + 1) * u["K"]], lh, rh, 0, 1)
                        mm.then_inc(attended, 1)
                        E.step(attended, f"{nm}.S{t}")
                    for kind, l, c in fill[t]:
                        if kind == "mod":
                            modulation(l, c)
                        if kind == "merge":
                            chunk, w = next_chunk()
                            features(f"b1.{l}.m{c}", chunk, w, 256, normed(f"b1.{l}", SEQ), SEQ, 2, rotating=ROTATING)
                    if 2 <= t < n + 2:
                        v = t - 2
                        acc = take(f"{nm}.T{v}", ROTATING)
                        if E.new(f"{nm}.p{v}"):
                            pe.wait_ge(*E.at(f"{nm}.p{v}"))
                        for b in range(4):
                            mm = nc.tensor.transpose(acc[:, P * b:P * b + P], probs[:, v % 3, P * b:P * b + P], C("ident"))
                        mm.then_inc(attended, 1)
                        E.step(attended, f"{nm}.T{v}")
                    if t >= 3:
                        v = t - 3
                        u = units[v]
                        if v == 0 or units[v - 1]["last"]:
                            state["o"] ^= 1
                            state["acc"] = take(f"{nm}.O{v}", fixed=ROTATING + state["o"])
                            state["ol"] = f"{nm}.O{v}"
                        acc = state["acc"]
                        if E.new(f"{nm}.pT{v}"):
                            pe.wait_ge(*E.at(f"{nm}.pT{v}"))
                        a, w = u["cols"]
                        out = acc[HD * u["half"]:HD * u["half"] + HD, a:a + w]
                        for i, vt in enumerate(u["v"]):
                            if u["G"] == 2:
                                rh = probsT[:, v % 2, :].rearrange("p (g k q) -> p g k q", g=2, k=2)[:, :, i, :]
                                oo = out.rearrange("p (g q) -> p g q", g=2)
                            else:
                                rh, oo = probsT[:, v % 2, P * i:P * i + P], out
                            mm = product(oo, vt, rh, i, len(u["v"]))
                        mm.then_inc(attended, 1)
                        E.step(attended, state["ol"] if u["last"] else None)
                while waiting:
                    finish_modulation()

            waiting = []

            def multiply_modulation(acc, at):
                c, w = next_chunk()
                if E.new("cond"):
                    pe.wait_ge(*E.at("cond"))
                wv = w[:, 0:KD * 256].rearrange("p (k n) -> p k n", n=256)
                for k in range(KD):
                    mm = product(acc[0:2, at:at + 256], csil[:, k, :], wv[:, k, :], k, KD)
                E.name_next(f"w{c}")
                return mm

            def turn_modulation(l, m, acc, at):
                if E.new(f"modrow{l}.{m}'"):
                    pe.wait_ge(*E.at(f"modrow{l}.{m}'"))
                for t in range(2):
                    mm = nc.tensor.transpose(acc[:, at + 2 * t:at + 2 * t + 2], mod_rows[0:2, m % 2, P * t:P * t + P], C("ident")[0:2, 0:2])
                mm.then_inc(modulation_turned, 1)
                E.step(modulation_turned, f"mod{l}.{m}")

            def modulation(l, m):
                acc = take(f"modrow{l}.{m}", ROTATING)
                multiply_modulation(acc, 0).then_inc(modulation_multiplied, 1)
                E.step(modulation_multiplied, f"modrow{l}.{m}")
                waiting.append((l, m))
                if len(waiting) == 2:
                    finish_modulation()

            def finish_modulation():
                l, m = waiting.pop(0)
                turn_modulation(l, m, take(f"mod{l}.{m}", ROTATING), 0)

            def modulation_beside(place, bank):
                acc = take(f"modrows.{place}", fixed=bank)
                for i, (l, m) in enumerate(MODS[place]):
                    multiply_modulation(acc, 256 * i).then_inc(modulation_multiplied, 1)
                    E.step(modulation_multiplied, f"modrow{l}.{m}")
                    E.name_last(f"modrows.{place}")

            def turn_beside(place, bank):
                acc = take(f"mods.{place}", fixed=bank)
                for i, (l, m) in enumerate(MODS[place]):
                    turn_modulation(l, m, acc, 4 * i)
                E.name_last(f"mods.{place}")

            def ffn(nm, nn, N):
                q0 = piece_number(nm, 0)

                def vacated(i):
                    b = (q0 + i) % BANKS
                    if b in occupant:
                        if E.new(occupant[b] + "'"):
                            pe.wait_ge(*E.at(occupant[b] + "'"))

                def passes(q, i, k, n, rhs_hi, rhs_lo):
                    wh, wl = part_piece(w_hi, q, i), part_piece(w_lo, q, i)
                    acc = psum[:, q % BANKS, 0:N]
                    nc.tensor.matmul(acc, wh[:, k, :], rhs_hi[k], start=(k == 0), stop=False)
                    nc.tensor.matmul(acc, wh[:, k, :], rhs_lo[k], start=False, stop=False)
                    return nc.tensor.matmul(acc, wl[:, k, :], rhs_hi[k], start=False, stop=(k == n - 1))

                def piece(half, i, rhs_hi, rhs_lo, ready=None, turn=None):
                    q = piece_number(nm, half, i)
                    if turn is None:
                        pe.wait_ge(weights_split, q + 1)
                    else:
                        pe.wait_ge(weights_split, turn * 8 + (q + 1))
                    n = len(rhs_hi)
                    for k in range(n):
                        if ready:
                            pe.wait_ge(hidden_written, ready[k])
                        mm = passes(q, i, k, n, rhs_hi, rhs_lo)
                    mm.then_inc(piece_multiplied, 1)

                def first_pieces():
                    for i in range(PARTS):
                        vacated(i)
                    pe.wait_ge(weights_split, piece_number(nm, 0, PARTS))
                    for k in range(KD):
                        if E.new(f"{nn}.h{k}"):
                            pe.wait_ge(*E.at(f"{nn}.h{k}"))
                        for i in range(PARTS):
                            mm = passes(piece_number(nm, 0, i), i, k, KD, x_hi, x_lo)
                            if k == KD - 1:
                                mm.then_inc(piece_multiplied, 1)

                x_hi, x_lo = [h_hi[:, k, 0:N] for k in range(KD)], [h_lo[:, k, 0:N] for k in range(KD)]
                u_hi, u_lo = [hidden_hi[:, k, 0:N] for k in range(KH)], [hidden_lo[:, k, 0:N] for k in range(KH)]
                for half in range(2):
                    lead, turns = LOOPED[f"{nm}_in{half}"]
                    tile = tile_number(nm, half)
                    if half == 0:
                        first_pieces()
                        if MODS.get(nn):
                            turn_beside(nn, (q0 + 7) % BANKS)
                    for i in range(0 if half else PARTS, 2 * lead):
                        if half:
                            if E.new(f"{nm}_o0.{i}'"):
                                pe.wait_ge(*E.at(f"{nm}_o0.{i}'"))
                        else:
                            vacated(i)
                        piece(half, i, x_hi, x_lo)
                    if half == 0:
                        vacated(6)
                        vacated(7)
                    else:
                        if E.new(f"{nm}_o0.7'"):
                            pe.wait_ge(*E.at(f"{nm}_o0.7'"))
                    with E.loop(pe, f"{nm}_in{half}", turns) as it:
                        for u in range(SLOTS):
                            m = tile + lead + u
                            pe.wait_ge(gated, it * SLOTS + (m - 2))
                            piece(half, 2 * (lead + u), x_hi, x_lo, turn=it)
                            pe.wait_ge(hidden_written, it * (3 * SLOTS) + (3 * (m - 3) + 1))
                            piece(half, 2 * (lead + u) + 1, x_hi, x_lo, turn=it)
                    for o in range(KD):
                        m = tile + KH - 4 + o // 2
                        if o % 2 == 0:
                            pe.wait_ge(gated, m + 1)
                        else:
                            pe.wait_ge(hidden_written, 3 * m + 1)
                        ready = [3 * (tile + k + 1) for k in range(KH)] if o == 0 else None
                        piece(half, 2 * KH + o, u_hi, u_lo, ready)
                for o in range(KD):
                    q = piece_number(nm, 1, 2 * KH + o)
                    occupant[q % BANKS] = f"{nm}_o1.{o}"
                state["c"] += 2 * (KH + KD)

            def head_norm(nm, mods=(), every=1):
                mods, count = list(mods), 0
                for H in head_norms(nm):
                    T = H["tiles"]
                    N = T[0].shape[-1]
                    if H["total"]:
                        acc = take(f"{H['name']}.sum0")
                    for t in range(len(T)):
                        if not H["total"]:
                            acc = take(f"{H['name']}.sum{t}")
                        if E.new(f"{H['name']}.sq{t}"):
                            pe.wait_ge(*E.at(f"{H['name']}.sq{t}"))
                        rows = T[t].shape[0]
                        mm = product(acc[0:rows, 0:N], C(H["mat"])[0:rows, 0:rows], squares[0:rows, t % 4, 0:N],
                                     t if H["total"] else 0, len(T) if H["total"] else 1)
                        mm.then_inc(summed, 1)
                        E.step(summed, f"{H['name']}.c{t}")
                        if not H["total"]:
                            E.name_last(f"{H['name']}.sum{t}")
                        count += 1
                        if mods and count % every == 0:
                            modulation(*mods.pop(0))
                    if H["total"]:
                        E.name_last(f"{H['name']}.sum0")
                    if H["rope"]:
                        for t in range(len(T)):
                            rotate(f"{H['name']}.r{t}", T[t][:, 0:SEQ], "rot_q" if rows == 96 else "rot_pair", f"{H['name']}.n{t}", SEQ)
                for m in mods:
                    modulation(*m)

            pe.wait_ge(s_const, 32)
            for l in range(2):
                nm = f"b1.{l}"
                norm(nm)
                rhs = normed(nm, SEQ)
                def branch_projections(br):
                    for part in "qkvg":
                        for j in range(2):
                            c, w = next_chunk()
                            if part == "v":
                                tokens(f"{nm}.v{br}{j}", c, w, 256, 0, 256, rhs, QT)
                            else:
                                features(f"{nm}.{part}{br}{j}", c, w, 256, rhs, SEQ, 2)
                            if l == 1 and (br, part, j) == (0, "q", 0):
                                turn_beside("b1.1", (state["bank"] + 6) % BANKS)
                for br in range(2):
                    branch_projections(br)
                    if br < 2:
                        for part, buf in (("q", qT[br]), ("k", kT[br])):
                            for j in range(2):
                                rotate(f"{nm}.r{part}{br}{j}", flat(buf[:, 2 * j:2 * j + 2, :]), "rot_half",
                                       f"{nm}.{part}{br}{j}.0'", 512)
                for j in range(2):
                    c, w = next_chunk()
                    features(f"{nm}.qi{j}", c, w, 256, rhs, SEQ, 2)
                c, w = next_chunk()
                features(f"{nm}.ki", None, w, 144, rhs, SEQ, 1)
                tokens(f"{nm}.wl", c, w, 144, 128, 144, rhs, QT)
                for j in range(2):
                    rotate(f"{nm}.rqi{j}", flat(qiT[:, 2 * j:2 * j + 2, :]), "rot_half", f"{nm}.qi{j}.0'", 512)
                rotate(f"{nm}.rki", kiT, "rot_half", f"{nm}.ki.0'", SEQ)
                for hh in range(HEADS):
                    acc = take(f"{nm}.ix{hh}")
                    rows = slice(HD * (hh % 2), HD * (hh % 2) + HD)
                    if E.new(f"{nm}.rqi{hh // 4}'"):
                        pe.wait_ge(*E.at(f"{nm}.rqi{hh // 4}'"))
                    if E.new(f"{nm}.rki'"):
                        pe.wait_ge(*E.at(f"{nm}.rki'"))
                    for q in range(QT):
                        mm = product(acc[:, SEQ * q:SEQ * q + SEQ], qiT[rows, hh // 2, P * q:P * q + P], kiT[rows, :], 0, 1)
                    mm.then_inc(multiplied, 1)
                    E.step(multiplied, f"{nm}.ix{hh}")
                branch_projections(2)
                acc = take(f"{nm}.cs")
                if E.new(f"{nm}.logf"):
                    pe.wait_ge(*E.at(f"{nm}.logf"))
                for t in range(QT):
                    mm = product(acc[0:8, 0:SEQ], fz[:, t, 0:8], C("upto")[:, SEQ * t:SEQ * t + SEQ], t, QT)
                for q in range(QT):
                    for t in range(QT):
                        mm = product(acc[:, SEQ + 8 * q:SEQ + 8 * q + 8],
                                     C("upto")[:, SEQ * t + P * q:SEQ * t + P * q + P], fz[:, t, 0:8], t, QT)
                mm.then_inc(multiplied, 1)
                E.step(multiplied, f"{nm}.cs")
                if l == 0:
                    pe.wait_ge(s_onehot, 16)
                attention(f"{nm}.att")
                for n in range(3):
                    for j in range(2):
                        c, w = next_chunk()
                        features(f"{nm}.y{n}{j}", c, w, 512, [(oT[n][:, k, :], f"{nm}.att.o{8 * n + 2 * k + 1}") for k in range(KW)],
                                 SEQ, 4)
                for j in range(4):
                    c, w = next_chunk()
                    features(f"{nm}.out{j}", c, w, 256, [(merged[:, k, :], f"{nm}.mg{k // 2}") for k in range(KD)], SEQ, 2)
            norm("final")
            norm("b2.0.n1")
            ffn("b2.0.ffn1", "b2.0.n1", TOK)
            norm("b2.0.nm")
            rhs = normed("b2.0.nm", TOK)
            for j in range(7):
                c, w = next_chunk()
                features("b2.0.in", c, w, 256, rhs, TOK, 2, first=2 * j)
                if j == 0:
                    turn_beside("b2.0.nm", (state["bank"] + 5) % BANKS)
            head_norm("b2.0.lora")
            for i in PE_CONV:
                acc = take(f"b2.0.conv.pe{i}")
                for k in range(TAPS):
                    n = TAPS * (i - PE_CONV[0]) + k
                    if E.new(f"b2.0.conv.glu{i}"):
                        pe.wait_ge(*E.at(f"b2.0.conv.glu{i}"))
                    if E.new(f"b2.0.conv.diag{n}"):
                        pe.wait_ge(*E.at(f"b2.0.conv.diag{n}"))
                    product(acc.rearrange("p (g s) -> p g s", g=2), m_diag[:, n % 4, :], m_y[:, i, :, k:k + SEQ], k, TAPS)\
                        .then_inc(tap_multiplied, 1)
                    E.step(tap_multiplied, f"b2.0.conv.tap{n}")
                E.name_last(f"b2.0.conv.pe{i}")
            for t in range(HEADS):
                if t % 4 == 0:
                    c, w = next_chunk()
                    wv = w[:, 0:3 * 384].rearrange("p (k n) -> p k n", n=384)
                acc = take(f"b2.0.uq.{t}")
                for k in range(3):
                    if E.new(f"b2.0.lora.cq.n{k}"):
                        pe.wait_ge(*E.at(f"b2.0.lora.cq.n{k}"))
                    mm = product(acc[0:96, :], wv[:, k, 96 * (t % 4):96 * (t % 4) + 96], m_cq[:, k, :], k, 3)
                if t % 4 == 3:
                    E.name_next(f"w{c}")
                mm.then_inc(multiplied, 1)
                E.step(multiplied, f"b2.0.uq.{t}")
            c, w = next_chunk()
            kv = [(m_ckv[:, k, :], f"b2.0.lora.ckv.n{k}") for k in range(2)]
            wv = w[:, 0:2048].rearrange("p (k n) -> p k n", n=1024)
            for t in range(HEADS):
                acc = take(f"b2.0.ukv.{t}")
                for k in range(2):
                    if E.new(kv[k][1]):
                        pe.wait_ge(*E.at(kv[k][1]))
                    mm = product(acc[0:64, :], wv[:, k, HD * t:HD * t + HD], kv[k][0], k, 2)
                mm.then_inc(multiplied, 1)
                E.step(multiplied, f"b2.0.ukv.{t}")
            tokens("b2.0.mv", c, w, 1024, 512, 1024, kv, 4)
            head_norm("b2.0.heads", MODS["b2.0.heads"], MODS_EVERY["b2.0.heads"])
            attention("b2.0.att")
            for what in ("mean", "var"):
                acc = take(f"b2.0.conv.{what}")
                for t in range(4):
                    if E.new(f"b2.0.conv.{'y' if what == 'mean' else 'sq'}{t}"):
                        pe.wait_ge(*E.at(f"b2.0.conv.{'y' if what == 'mean' else 'sq'}{t}"))
                    mm = product(acc, C("ones"), m_yc[:, t, :] if what == "mean" else squares[:, t, :], t, 4)
                mm.then_inc(multiplied, 1)
                E.step(multiplied, f"b2.0.conv.{what}")
            for j in range(4):
                c, w = next_chunk()
                features(f"b2.0.out", c, w, 256,
                         [(m_o[:, k, :], mixed_ready("b2.0", k)) for k in range(KD)], TOK, 2, first=2 * j)
            norm("b2.0.n2")
            ffn("b2.0.ffn2", "b2.0.n2", TOK)
            norm("b2.1.n1")
            ffn("b2.1.ffn1", "b2.1.n1", TOK)
            norm("b2.1.nm")
            rhs = normed("b2.1.nm", TOK)
            for j in range(2):
                c, w = next_chunk()
                features("b2.1.in", c, w, 256, rhs, TOK, 2, first=2 * j)
                if j == 0:
                    turn_beside("b2.1.nm", (state["bank"] + 5) % BANKS)
            c, w = next_chunk()
            features("b2.1.in", None, w, 256, rhs, TOK, 1, first=4)
            tokens("b2.1.cv", c, w, 256, 128, 256, rhs, 4)
            for j in range(2):
                c, w = next_chunk()
                tokens("b2.1.nv", c, w, 256, 0, 256, rhs, 4, first=2 * j)
            rhs = normed("b2.1.nm", SEQ)
            for part in ("cq", "nq"):
                for j in range(2):
                    c, w = next_chunk()
                    features(f"b2.1.{part}", c, w, 256, rhs, SEQ, 2, first=j)
            head_norm("b2.1.heads", MODS["b2.1.heads"], MODS_EVERY["b2.1.heads"])
            attention("b2.1.att")
            for j in range(4):
                c, w = next_chunk()
                features(f"b2.1.out", c, w, 256, [(g_o[:, k, :], mixed_ready("b2.1", k)) for k in range(KD)], SEQ, 2, first=j)
            norm("b2.1.n2")
            ffn("b2.1.ffn2", "b2.1.n2", SEQ)
            assert state["c"] == len(stage_of), (state["c"], len(stage_of))

        @block.scalar
        def _(act):
            E = Engine(book, sems)
            A = nc.scalar.activation

            def bank(label, N=BANK):
                if E.new(label):
                    act.wait_ge(*E.at(label))
                return psum[:, E.bank(label), 0:N]

            def norm(nm):
                N = NORM_N[nm]
                for k in range(KD):
                    if BEFORE[nm] and E.new(f"{BEFORE[nm]}{k}"):
                        act.wait_ge(*E.at(f"{BEFORE[nm]}{k}"))
                    if k >= 4:
                        if E.new(f"{nm}.c{k - 4}"):
                            act.wait_ge(*E.at(f"{nm}.c{k - 4}"))
                    A(squares[:, k % 4, 0:N], x[:, k, 0:N], ACT.Square).then_inc(rooted, 1)
                    act.wait_ge(rooted, E.step(rooted, f"{nm}.sq{k}"))
                A(rs[:, 0:N], sum_bank(nm, N), ACT.Sqrt, scale=1.0 / D,
                  bias=C("eps")).then_inc(rooted, 1)
                act.wait_ge(rooted, E.step(rooted, f"{nm}.sum'"))

            def sum_bank(nm, N):
                if E.new(f"{nm}.c7"):
                    act.wait_ge(*E.at(f"{nm}.c7"))
                return psum[:, E.bank(f"{nm}.sum"), 0:N]

            def modulate(nm, l, which, N):
                if E.new(f"{nm}.mscale"):
                    act.wait_ge(*E.at(f"{nm}.mscale"))
                for k in range(KD):
                    if E.new(f"{nm}.t{k}"):
                        act.wait_ge(*E.at(f"{nm}.t{k}"))
                    for g in range(N // SEQ):
                        v = (h[:, k, :] if which == 1 else squares[:, k % 4, :])[:, SEQ * g:SEQ * g + SEQ]
                        last = g == N // SEQ - 1
                        A(v, v, ACT.Identity, scale=mscale[:, k, g:g + 1],
                          bias=mods[:, l, 24 * which + k, g:g + 1]).then_inc(shifted, 1)
                        act.wait_ge(shifted, E.step(shifted, f"{nm}.h{k}" if last and which == 1 else None))
                    if which != 1:
                        A(h_hi[:, k, 0:N], squares[:, k % 4, 0:N], ACT.Copy).then_inc(shifted, 1)
                        act.wait_ge(shifted, E.step(shifted, f"{nm}.hi{k}"))

            def attention(nm):
                units, fill = ATT[nm], fillers(nm)
                n = len(units)
                for t in range(n + 3):
                    if t < n:
                        u = units[t]
                        if u["kind"] == "fox":
                            A(work[:, t % 2, :], bank(f"{nm}.B{t}"), ACT.Copy).then_inc(exponentiated, 1)
                            act.wait_ge(exponentiated, E.step(exponentiated, f"{nm}.B{t}'"))
                        if E.new(f"{nm}.mx{t}"):
                            act.wait_ge(*E.at(f"{nm}.mx{t}"))
                        K = u["K"]
                        src = psum[:, E.bank(f"{nm}.S{t}"), :]
                        for g in range(u["G"]):
                            last = g == u["G"] - 1
                            A(probs[:, t % 3, K * g:K * g + K], src[:, K * g:K * g + K], ACT.Exp,
                              scale=u["scale"], bias=stat[:, t % 4, 2 + g:3 + g],
                              accum_out=stat[:, t % 4, 4 + g:5 + g]).then_inc(exponentiated, 1)
                            act.wait_ge(exponentiated, E.step(exponentiated, f"{nm}.S{t}'" if last else None))
                    for kind, l, c in fill[t]:
                        if kind == "mod":
                            modulation(l, c)
                        if kind == "merge":
                            lab = f"b1.{l}.m{c}.0"
                            A(flat(gates(c)), bank(lab), ACT.Tanh, scale=0.5).then_inc(exponentiated, 1)
                            act.wait_ge(exponentiated, E.step(exponentiated, lab + "'"))
                    if 2 <= t < n + 2:
                        v = t - 2
                        A(probsT[:, v % 2, :], bank(f"{nm}.T{v}"), ACT.Copy).then_inc(exponentiated, 1)
                        act.wait_ge(exponentiated, E.step(exponentiated, f"{nm}.T{v}'"))
                        E.name_last(f"{nm}.pT{v}")
                while waiting:
                    finish_modulation()

            order = [m for chunks in MODS.values() for m in chunks]
            waiting = []

            def copy_row(l, m, label, at=0):
                src = bank(label)[0:2, at:at + 256]
                n = order.index((l, m))
                if n >= 2:
                    before = "mod{}.{}".format(*order[n - 2])
                    if E.new(before):
                        act.wait_ge(*E.at(before))
                A(mod_rows[0:2, m % 2, :], src, ACT.Copy).then_inc(modulation_copied, 1)
                act.wait_ge(modulation_copied, E.step(modulation_copied, f"modrow{l}.{m}'"))

            def copy_turned(l, m, label, at=0):
                src = bank(label)[:, at:at + 4]
                A(mods[:, l, 2 * m:2 * m + 2, :].rearrange("p a b -> p (a b)"), src, ACT.Copy).then_inc(modulation_copied, 1)
                act.wait_ge(modulation_copied, E.step(modulation_copied, f"mod{l}.{m}'"))

            def modulation(l, m):
                copy_row(l, m, f"modrow{l}.{m}")
                waiting.append((l, m))
                if len(waiting) == 2:
                    finish_modulation()

            def finish_modulation():
                l, m = waiting.pop(0)
                copy_turned(l, m, f"mod{l}.{m}")

            def rows_beside(place):
                for i, (l, m) in enumerate(MODS[place]):
                    copy_row(l, m, f"modrows.{place}", 256 * i)
                E.name_last(f"modrows.{place}'")

            def turned_beside(place):
                for i, (l, m) in enumerate(MODS[place]):
                    copy_turned(l, m, f"mods.{place}", 4 * i)
                E.name_last(f"mods.{place}'")

            def round_weights(nm, half, i, turn=None):
                q, c = piece_number(nm, half, i), piece_chunk(nm, half, i)
                if turn is None:
                    act.wait_ge(landed[c % SLOTS], 16 * (c // SLOTS + 1))
                    if q >= PARTS:
                        act.wait_ge(piece_multiplied, q - PARTS + 1)
                else:
                    act.wait_ge(landed[c % SLOTS], 16 * (c // SLOTS + 1) + turn * 16)
                    act.wait_ge(piece_multiplied, turn * 8 + (q - PARTS + 1))
                A(part_piece(w_hi, q, i), raw_piece(c, i), ACT.Copy).then_inc(weights_rounded, 1)

            def ffn_weights(nm):
                if VACATED[nm] and E.new(VACATED[nm]):
                    act.wait_ge(*E.at(VACATED[nm]))
                for i in range(PARTS):
                    round_weights(nm, 0, i)

            def ffn(nm, N, beside=None):
                def gate(half, i, turn=None):
                    if i < 0 or i >= 2 * KH or i % 2:
                        return
                    q, m = piece_number(nm, half, i), tile_number(nm, half, i // 2)
                    if turn is None:
                        act.wait_ge(piece_multiplied, q + 1)
                        if m >= 4:
                            act.wait_ge(hidden_written, 3 * (m - 3))
                    else:
                        act.wait_ge(piece_multiplied, turn * 8 + (q + 1))
                        act.wait_ge(hidden_written, turn * (3 * SLOTS) + max(3 * (m - 3), 1))
                    A(squares[:, m % 4, 0:N], psum[:, q % BANKS, 0:N], ACT.Silu).then_inc(gated, 1)

                for half in range(2):
                    lead, turns = LOOPED[f"{nm}_in{half}"]
                    for i in range(2 * lead):
                        if half or i >= PARTS:
                            round_weights(nm, half, i)
                        gate(half, i - LAG)
                    if half == 0 and beside:
                        turned_beside(beside)
                    with E.loop(act, f"{nm}_in{half}", turns) as it:
                        for i in range(2 * lead, 2 * (lead + SLOTS)):
                            round_weights(nm, half, i, it)
                            gate(half, i - LAG, it)
                    for i in range(2 * KH, PIECES):
                        round_weights(nm, half, i)
                        gate(half, i - LAG)

            def head_norm(nm, mods=(), every=1):
                mods, count = list(mods), 0
                for H in head_norms(nm):
                    T = H["tiles"]
                    N = T[0].shape[-1]
                    rows = T[0].shape[0]

                    def square(t):
                        if E.new(H["ready"][t]):
                            act.wait_ge(*E.at(H["ready"][t]))
                        if t >= 4:
                            if E.new(f"{H['name']}.c{t - 4}"):
                                act.wait_ge(*E.at(f"{H['name']}.c{t - 4}"))
                        A(squares[0:rows, t % 4, 0:N], T[t], ACT.Square).then_inc(squared, 1)
                        act.wait_ge(squared, E.step(squared, f"{H['name']}.sq{t}"))

                    def root(t, s):
                        src = psum[0:rows, E.bank(f"{H['name']}.sum{s}"), 0:N]
                        if E.new(f"{H['name']}.sum{s}"):
                            act.wait_ge(*E.at(f"{H['name']}.sum{s}"))
                        A(work[0:rows, t % 2, 0:N], src, ACT.Sqrt, scale=1.0 / H["count"], bias=C("eps")[0:rows, :]).then_inc(rooted, 1)
                        act.wait_ge(rooted, E.step(rooted, f"{H['name']}.sum{s}'"))
                    for t in range(min(4, len(T))):
                        square(t)
                    if H["total"]:
                        root(0, 0)
                    else:
                        for t in range(len(T)):
                            if t >= 2:
                                if E.new(f"{H['name']}.n{t - 2}"):
                                    act.wait_ge(*E.at(f"{H['name']}.n{t - 2}"))
                            root(t, t)
                            if t + 4 < len(T):
                                square(t + 4)
                            count += 1
                            if mods and count % every == 0:
                                modulation(*mods.pop(0))
                    if E.new(f"{H['name']}.n{len(T) - 1}"):
                        act.wait_ge(*E.at(f"{H['name']}.n{len(T) - 1}"))
                for m in mods:
                    modulation(*m)

            act.wait_ge(s_const, 32)
            act.wait_ge(s_x, 16)
            A(csil[:, :, :].rearrange("p a b -> p (a b)"), R("cond"), ACT.Silu).then_inc(copied, 1)
            act.wait_ge(copied, E.step(copied, "cond"))
            for l in range(2):
                nm = f"b1.{l}"
                norm(nm)
                if l == 1:
                    rows_beside("b1.1")
                def copy_branch(br):
                    for part in "qkvg":
                        for j in range(2):
                            lab = f"{nm}.{part}{br}{j}.0"
                            if l == 1 and (br, part, j) == (0, "q", 1):
                                turned_beside("b1.1")
                            src = bank(lab)
                            if part == "v":
                                A(vv[br][:, :, 256 * j:256 * j + 256], src.rearrange("p (a b) -> p a b", a=2), ACT.Copy).then_inc(copied, 1)
                                act.wait_ge(copied, E.step(copied, lab + "'"))
                            else:
                                buf = {"q": qT, "k": kT, "g": gg}[part][br]
                                sc = HD ** -0.5 if (part == "q" and br == 2) else 1.0
                                A(flat(buf[:, 2 * j:2 * j + 2, :]), src, ACT.Silu if part == "g" else ACT.Copy,
                                  scale=sc).then_inc(copied, 1)
                                act.wait_ge(copied, E.step(copied, lab + "'"))
                for br in range(2):
                    copy_branch(br)
                for j in range(2):
                    lab = f"{nm}.qi{j}.0"
                    A(flat(qiT[:, 2 * j:2 * j + 2, :]), bank(lab), ACT.Copy).then_inc(copied, 1)
                    act.wait_ge(copied, E.step(copied, lab + "'"))
                lab = f"{nm}.ki.0"
                A(kiT, bank(lab, SEQ), ACT.Copy).then_inc(copied, 1)
                act.wait_ge(copied, E.step(copied, lab + "'"))
                lab = f"{nm}.wl.0"
                A(flat(wl), bank(lab, 32), ACT.Copy).then_inc(copied, 1)
                act.wait_ge(copied, E.step(copied, lab + "'"))
                for hh in range(HEADS):
                    if hh >= 2:
                        if E.new(f"{nm}.isc{hh - 2}"):
                            act.wait_ge(*E.at(f"{nm}.isc{hh - 2}"))
                    lab = f"{nm}.ix{hh}"
                    A(work[:, hh % 2, :], bank(lab), ACT.Relu).then_inc(copied, 1)
                    act.wait_ge(copied, E.step(copied, lab + "'"))
                copy_branch(2)
                if E.new(f"{nm}.z"):
                    act.wait_ge(*E.at(f"{nm}.z"))
                A(fz[:, 2, :], fz[:, 1, :], ACT.Exp, scale=-1.0).then_inc(copied, 1)
                act.wait_ge(copied, E.step(copied))
                A(fz[:, 3, :], fz[:, 2, :], ACT.Ln, bias=C("one")).then_inc(copied, 1)
                act.wait_ge(copied, E.step(copied, f"{nm}.ln"))
                attention(f"{nm}.att")
            norm("final")
            act.wait_ge(s_ctx, 16)
            ffn_weights("b2.0.ffn1")
            norm("b2.0.n1")
            modulate("b2.0.n1", 0, 0, TOK)
            rows_beside("b2.0.n1")
            ffn("b2.0.ffn1", TOK, "b2.0.n1")
            norm("b2.0.nm")
            modulate("b2.0.nm", 0, 1, TOK)
            rows_beside("b2.0.nm")
            dst = [m_ckv[:, 0, :], m_ckv[:, 1, :], m_kr, m_cq[:, 0, :], m_cq[:, 1, :], m_cq[:, 2, :]]
            for i in range(6):
                lab = f"b2.0.in.{i}"
                A(dst[i], bank(lab), ACT.Copy).then_inc(copied, 1)
                act.wait_ge(copied, E.step(copied, lab + "'"))
                E.name_last(f"b2.0.in.e{i}")
                if i == 1:
                    turned_beside("b2.0.nm")
            for i in range(4):
                lab = f"b2.0.in.{6 + i}"
                A(m_ca[:, i, :], bank(lab), ACT.Identity, bias=R("glu_b", i, 1)).then_inc(copied, 1)
                act.wait_ge(copied, E.step(copied, lab + "'"))
            for i in range(4):
                lab = f"b2.0.in.{10 + i}"
                A(squares[:, i, :], bank(lab), ACT.Sigmoid, bias=R("glu_b", 4 + i, 1)).then_inc(copied, 1)
                act.wait_ge(copied, E.step(copied, lab + "'"))
            if E.new("b2.0.conv.glu3"):
                act.wait_ge(*E.at("b2.0.conv.glu3"))
            head_norm("b2.0.lora")
            for i in PE_CONV:
                lab = f"b2.0.conv.pe{i}"
                A(m_yc[:, i, :], bank(lab), ACT.Identity, bias=R("dw_b", i, 1)).then_inc(copied, 1)
                act.wait_ge(copied, E.step(copied, lab + "'"))
                E.name_last(f"b2.0.conv.y{i}")
            for i in range(HEADS):
                lab = f"b2.0.uq.{i}"
                A(m_q[0:96, i, :], bank(lab)[0:96, :], ACT.Copy).then_inc(copied, 1)
                act.wait_ge(copied, E.step(copied, lab + "'"))
            for i in range(HEADS):
                lab = f"b2.0.ukv.{i}"
                A(m_k[0:64, i, :], bank(lab)[0:64, :], ACT.Copy).then_inc(copied, 1)
                act.wait_ge(copied, E.step(copied, lab + "'"))
            for i in range(4):
                lab = f"b2.0.mv.{i}"
                A(m_v[:, i, :], bank(lab), ACT.Copy).then_inc(copied, 1)
                act.wait_ge(copied, E.step(copied, lab + "'"))
            head_norm("b2.0.heads", MODS["b2.0.heads"], MODS_EVERY["b2.0.heads"])
            for i in range(HEADS):
                A(m_k[64:96, i, :], m_kr[64:96, :], ACT.Copy).then_inc(copied, 1)
                act.wait_ge(copied, E.step(copied, "b2.0.heads.kr_copied" if i == HEADS - 1 else None))
            attention("b2.0.att")
            for t in range(4):
                if E.new(f"b2.0.conv.c{t}"):
                    act.wait_ge(*E.at(f"b2.0.conv.c{t}"))
                A(squares[:, t, :], m_yc[:, t, :], ACT.Square).then_inc(copied, 1)
                act.wait_ge(copied, E.step(copied, f"b2.0.conv.sq{t}"))
            A(rs[:, :], bank("b2.0.conv.var"), ACT.Sqrt, scale=1.0 / 512, bias=C("eps")).then_inc(copied, 1)
            act.wait_ge(copied, E.step(copied, "b2.0.conv.var'"))
            for t in range(4):
                if E.new(f"b2.0.conv.n{t}"):
                    act.wait_ge(*E.at(f"b2.0.conv.n{t}"))
                A(m_o[:, 4 + t, :], m_yc[:, t, :], ACT.Silu, scale=R("ln_g", t, 1), bias=R("ln_b", t, 1)).then_inc(copied, 1)
                act.wait_ge(copied, E.step(copied, f"b2.0.conv.o{t}"))
            ffn_weights("b2.0.ffn2")
            norm("b2.0.n2")
            modulate("b2.0.n2", 0, 2, TOK)
            rows_beside("b2.0.n2")
            ffn("b2.0.ffn2", TOK, "b2.0.n2")
            ffn_weights("b2.1.ffn1")
            norm("b2.1.n1")
            modulate("b2.1.n1", 1, 0, TOK)
            rows_beside("b2.1.n1")
            ffn("b2.1.ffn1", TOK, "b2.1.n1")
            norm("b2.1.nm")
            modulate("b2.1.nm", 1, 1, TOK)
            rows_beside("b2.1.nm")
            dst = [g_ck] + [g_nk[:, t, :] for t in range(4)]
            for i in range(5):
                lab = f"b2.1.in.{i}"
                A(dst[i], bank(lab), ACT.Copy).then_inc(copied, 1)
                act.wait_ge(copied, E.step(copied, lab + "'"))
                E.name_last(f"b2.1.in.e{i}")
                if i == 1:
                    turned_beside("b2.1.nm")
            A(flat(g_cv), bank("b2.1.cv.0"), ACT.Copy).then_inc(copied, 1)
            act.wait_ge(copied, E.step(copied, "b2.1.cv.0'"))
            for j in range(2):
                for i in range(2):
                    lab = f"b2.1.nv.{2 * j + i}"
                    A(g_nv[:, 2 * i:2 * i + 2, 256 * j:256 * j + 256],
                      bank(lab).rearrange("p (a b) -> p a b", a=2), ACT.Copy).then_inc(copied, 1)
                    act.wait_ge(copied, E.step(copied, lab + "'"))
            for part, buf in (("cq", g_cq), ("nq", g_nq)):
                for j in range(2):
                    lab = f"b2.1.{part}.{j}"
                    A(flat(buf[:, 2 * j:2 * j + 2, :]), bank(lab), ACT.Copy).then_inc(copied, 1)
                    act.wait_ge(copied, E.step(copied, lab + "'"))
                    E.name_last(f"b2.1.{part}.e{j}")
            head_norm("b2.1.heads", MODS["b2.1.heads"], MODS_EVERY["b2.1.heads"])
            attention("b2.1.att")
            ffn_weights("b2.1.ffn2")
            norm("b2.1.n2")
            modulate("b2.1.n2", 1, 2, SEQ)
            ffn("b2.1.ffn2", SEQ)

        @block.gpsimd
        def _(pool):
            E = Engine(book, sems)
            pool.wait_ge(s_const, 32)

            def tap(n):
                i, k = divmod(n, TAPS)
                i += DVE_CONV
                if E.new(f"b2.0.conv.glu{i}"):
                    pool.wait_ge(*E.at(f"b2.0.conv.glu{i}"))
                out, term = (v.rearrange("p (g s) -> p g s", g=2) for v in (m_yc[:, i, :], rs[:, :]))
                src, wk = m_y[:, i, :, k:k + SEQ], R("dw_w", TAPS * i + k, 1)
                if k == 0:
                    nc.gpsimd.tensor_scalar(out, src, wk, R("dw_b", i, 1), ALU.mult, ALU.add).then_inc(pool_tap_added, 1)
                else:
                    nc.gpsimd.tensor_scalar(term, src, wk, 1.0, ALU.mult, ALU.mult).then_inc(pool_tap_added, 1)
                    pool.wait_ge(pool_tap_added, E.step(pool_tap_added))
                    nc.gpsimd.tensor_tensor(out, out, term, ALU.add).then_inc(pool_tap_added, 1)
                pool.wait_ge(pool_tap_added, E.step(pool_tap_added, f"b2.0.conv.y{i}" if k == TAPS - 1 else None))

            if E.new("b2.0.ffn1_out.x7"):
                pool.wait_ge(*E.at("b2.0.ffn1_out.x7"))
            for n in range(len(PE_CONV) * TAPS):
                if n >= 4 and E.new(f"b2.0.conv.tap{n - 4}"):
                    pool.wait_ge(*E.at(f"b2.0.conv.tap{n - 4}"))
                nc.gpsimd.tensor_scalar(m_diag[:, n % 4, :], C("ident"), R("dw_w", PE_CONV[0] * TAPS + n, 1), 1.0,
                                        ALU.mult, ALU.mult).then_inc(diagonal_built, 1)
                E.step(diagonal_built, f"b2.0.conv.diag{n}")
            for n in range(POOL_CONV * TAPS):
                tap(n)

        @block.vector
        def _(dve):
            E = Engine(book, sems)
            V = nc.vector

            def bank(label, N=BANK):
                if E.new(label):
                    dve.wait_ge(*E.at(label))
                return psum[:, E.bank(label), 0:N]

            def norm(nm, gain=None, to=None, split=False):
                N = NORM_N[nm]
                if E.new(f"{nm}.sum'"):
                    dve.wait_ge(*E.at(f"{nm}.sum'"))
                V.reciprocal(rs[:, 0:N], rs[:, 0:N]).then_inc(normed, 1)
                dve.wait_ge(normed, E.step(normed))
                if split:
                    for k in range(KD + 4):
                        if k >= 4:
                            if E.new(f"{nm}.hi{k - 4}"):
                                dve.wait_ge(*E.at(f"{nm}.hi{k - 4}"))
                            V.tensor_tensor(h_lo[:, k - 4, 0:N], squares[:, k % 4, 0:N], h_hi[:, k - 4, 0:N].bitcast(F32),
                                            ALU.subtract).then_inc(normed, 1)
                            dve.wait_ge(normed, E.step(normed, f"{nm}.h{k - 4}"))
                        if k < KD:
                            V.tensor_tensor(squares[:, k % 4, 0:N], x[:, k, 0:N], rs[:, 0:N], ALU.mult).then_inc(normed, 1)
                            dve.wait_ge(normed, E.step(normed, f"{nm}.t{k}"))
                    return
                for k in range(KD):
                    if gain is not None:
                        out = (x if to == "x" else h)[:, k, 0:N]
                        V.scalar_tensor_tensor(out=out, in0=x[:, k, 0:N], scalar=gain[:, k:k + 1], in1=rs[:, 0:N],
                                               op0=ALU.mult, op1=ALU.mult).then_inc(normed, 1)
                        dve.wait_ge(normed, E.step(normed, f"{nm}.h{k}"))
                    else:
                        V.tensor_tensor(h[:, k, 0:N], x[:, k, 0:N], rs[:, 0:N], ALU.mult).then_inc(normed, 1)
                        dve.wait_ge(normed, E.step(normed, f"{nm}.t{k}"))

            def add_mod_bias(l, a, b):
                if E.new(f"mod{l}.{b - 1}'"):
                    dve.wait_ge(*E.at(f"mod{l}.{b - 1}'"))
                md = mods[:, l, 2 * a:2 * b, :].rearrange("p a b -> p (a b)")
                V.tensor_tensor(md, md, R(f"b2.{l}.mod_b", 4 * a, 4 * (b - a)), ALU.add).then_inc(scales_prepared, 1)
                dve.wait_ge(scales_prepared, E.step(scales_prepared))

            def prepare(nm, l, which, gain):
                a = 24 * which + 8
                V.scalar_tensor_tensor(out=mscale[:, :, :].rearrange("p a b -> p (a b)"),
                                       in0=mods[:, l, a:a + 8, :].rearrange("p a b -> p (a b)"), scalar=1.0,
                                       in1=R(gain), op0=ALU.add, op1=ALU.mult).then_inc(scales_prepared, 1)
                dve.wait_ge(scales_prepared, E.step(scales_prepared, f"{nm}.mscale"))

            def rope(nm, view, cos, sin, lab, N):
                rows = view.shape[0]
                b, cos, sin = bank(lab, N)[0:rows, :], cos[0:rows, :], sin[0:rows, :]
                V.tensor_tensor(b, b, sin, ALU.mult).then_inc(roped, 1)
                dve.wait_ge(roped, E.step(roped))
                V.tensor_tensor(view, view, cos, ALU.mult).then_inc(roped, 1)
                dve.wait_ge(roped, E.step(roped))
                V.tensor_tensor(view, view, b, ALU.add).then_inc(roped, 1)
                dve.wait_ge(roped, E.step(roped, lab + "'"))

            def attention(nm):
                units, fill = ATT[nm], fillers(nm)
                n = len(units)
                pair = 0
                for t in range(n + 3):
                    if t < n:
                        u = units[t]
                        G, K = u["G"], u["K"]
                        S = bank(f"{nm}.S{t}", G * K)
                        st = stat[:, t % 4, :]
                        if u["kind"] == "moba":
                            V.tensor_tensor(S, S, C("causal"), ALU.add).then_inc(probs_ready, 1)
                            dve.wait_ge(probs_ready, E.step(probs_ready))
                        if u["kind"] == "dsa":
                            V.tensor_tensor(S, S, flat(dsa_mask), ALU.add).then_inc(probs_ready, 1)
                            dve.wait_ge(probs_ready, E.step(probs_ready))
                        if u["kind"] == "fox":
                            if E.new(f"{nm}.B{t}'"):
                                dve.wait_ge(*E.at(f"{nm}.B{t}'"))
                            for g in range(G):
                                V.scalar_tensor_tensor(
                              out=S[:, K * g:K * g + K], in0=S[:, K * g:K * g + K], scalar=cq[:, g, u["head"]:u["head"] + 1],
                              in1=work[:, t % 2, K * g:K * g + K], op0=ALU.add, op1=ALU.add).then_inc(probs_ready, 1)
                                dve.wait_ge(probs_ready, E.step(probs_ready))
                        if u["kind"] == "na":
                            V.tensor_tensor(S[:, 0:SEQ], S[:, 0:SEQ], g_bias[:, 2 * u["head"] + u["q"], :], ALU.add).then_inc(probs_ready, 1)
                            dve.wait_ge(probs_ready, E.step(probs_ready))
                        V.tensor_reduce(st[:, 0:G], S.rearrange("p (g k) -> p g k", g=G), AX_X, ALU.max).then_inc(probs_ready, 1)
                        dve.wait_ge(probs_ready, E.step(probs_ready))
                        V.tensor_scalar(st[:, 2:2 + G], st[:, 0:G], -u["scale"], None, ALU.mult).then_inc(probs_ready, 1)
                        dve.wait_ge(probs_ready, E.step(probs_ready, f"{nm}.mx{t}"))
                    if 1 <= t <= n:
                        v = t - 1
                        u = units[v]
                        G, K = u["G"], u["K"]
                        st = stat[:, v % 4, :]
                        if E.new(f"{nm}.S{v}'"):
                            dve.wait_ge(*E.at(f"{nm}.S{v}'"))
                        V.reciprocal(st[:, 6:6 + G], st[:, 4:4 + G]).then_inc(probs_ready, 1)
                        dve.wait_ge(probs_ready, E.step(probs_ready))
                        for g in range(G):
                            pv = probs[:, v % 3, K * g:K * g + K]
                            V.tensor_scalar(pv, pv, st[:, 6 + g:7 + g], None, ALU.mult).then_inc(probs_ready, 1)
                            dve.wait_ge(probs_ready, E.step(probs_ready, f"{nm}.p{v}" if g == G - 1 else None))
                    for kind, _, c in fill[t]:
                        if kind == "tap":
                            tap(c)
                    if t >= 3:
                        v = t - 3
                        u = units[v]
                        if v == 0 or units[v - 1]["last"]:
                            state["ol"] = f"{nm}.O{v}"
                        if u["last"]:
                            o = bank(state["ol"], SEQ)
                            if u["gate"] is not None:
                                V.tensor_tensor(u["dst"], o, u["gate"], ALU.mult).then_inc(probs_ready, 1)
                                dve.wait_ge(probs_ready, E.step(probs_ready, state["ol"] + "'"))
                            else:
                                V.tensor_copy(u["dst"], o).then_inc(probs_ready, 1)
                                dve.wait_ge(probs_ready, E.step(probs_ready, state["ol"] + "'"))
                            E.name_last(f"{nm}.o{v}")

            state = {}

            def tap(n):
                i, k = divmod(n, TAPS)
                out = m_yc[:, i, :].rearrange("p (g s) -> p g s", g=2)
                src, wk = m_y[:, i, :, k:k + SEQ], R("dw_w", TAPS * i + k, 1)
                if k == 0:
                    V.tensor_scalar(out, src, wk, R("dw_b", i, 1), ALU.mult, ALU.add).then_inc(tap_added, 1)
                else:
                    V.scalar_tensor_tensor(out=out, in0=src, scalar=wk, in1=out, op0=ALU.mult, op1=ALU.add)\
                        .then_inc(tap_added, 1)
                dve.wait_ge(tap_added, E.step(tap_added, f"b2.0.conv.y{i}" if k == TAPS - 1 else None))

            def split_weights(nm, half, i, turn=None):
                q, c = piece_number(nm, half, i), piece_chunk(nm, half, i)
                if turn is None:
                    dve.wait_ge(weights_rounded, q + 1)
                else:
                    dve.wait_ge(weights_rounded, turn * 8 + (q + 1))
                V.tensor_tensor(part_piece(w_lo, q, i), raw_piece(c, i), part_piece(w_hi, q, i).bitcast(F32),
                                ALU.subtract).then_inc(weights_split, 1)
                E.step(weights_split, f"w{c}" if i >= 2 * KH or i % 2 else None)

            def ffn_weights(nm):
                for i in range(PARTS):
                    split_weights(nm, 0, i)

            def ffn(nm, l, N, which):
                a = 24 * which + 16
                V.tensor_scalar(mscale[:, :, :].rearrange("p a b -> p (a b)"),
                                mods[:, l, a:a + 8, :].rearrange("p a b -> p (a b)"), 0.5, None, ALU.mult).then_inc(scales_prepared, 1)
                dve.wait_ge(scales_prepared, E.step(scales_prepared))

                def hidden(half, i, turn=None):
                    if i < 0 or i >= 2 * KH or i % 2 == 0:
                        return
                    q, m, t = piece_number(nm, half, i), tile_number(nm, half, i // 2), i // 2
                    s_m = squares[:, m % 4, 0:N]
                    if turn is None:
                        dve.wait_ge(gated, m + 1)
                        dve.wait_ge(piece_multiplied, q + 1)
                        hi, lo = hidden_hi[:, t, 0:N], hidden_lo[:, t, 0:N]
                        ahead = 0
                    else:
                        dve.wait_ge(gated, turn * SLOTS + (m + 1))
                        dve.wait_ge(piece_multiplied, turn * 8 + (q + 1))
                        hi, lo = (v[:, bass.ds(turn * SLOTS + t, 1), 0:N].rearrange("p a b -> p (a b)")
                                  for v in (hidden_hi, hidden_lo))
                        ahead = turn * (3 * SLOTS)
                    V.tensor_tensor(s_m, s_m, psum[:, q % BANKS, 0:N], ALU.mult).then_inc(hidden_written, 1)
                    dve.wait_ge(hidden_written, ahead + (3 * m + 1))
                    V.tensor_copy(hi, s_m).then_inc(hidden_written, 1)
                    dve.wait_ge(hidden_written, ahead + (3 * m + 2))
                    V.tensor_tensor(lo, s_m, hi.bitcast(F32), ALU.subtract).then_inc(hidden_written, 1)

                def add(half, o):
                    q = piece_number(nm, half, 2 * KH + o)
                    dve.wait_ge(piece_multiplied, q + 1)
                    for g in range(N // SEQ):
                        xv = x[:, o, SEQ * g:SEQ * g + SEQ]
                        V.scalar_tensor_tensor(out=xv, in0=psum[:, q % BANKS, SEQ * g:SEQ * g + SEQ], scalar=mscale[:, o, g:g + 1],
                                               in1=xv, op0=ALU.mult, op1=ALU.add).then_inc(ffn_added, 1)
                        dve.wait_ge(ffn_added, E.step(ffn_added))
                    E.name_last(f"{nm}_o{half}.{o}'")
                    if half:
                        E.name_last(f"{nm}_out.x{o}")

                for half in range(2):
                    lead, turns = LOOPED[f"{nm}_in{half}"]
                    for i in range(2 * lead):
                        if half or i >= PARTS:
                            split_weights(nm, half, i)
                        if half and i < LAG:
                            add(0, KD - LAG + i)
                        hidden(half, i - LAG)
                    with E.loop(dve, f"{nm}_in{half}", turns) as it:
                        for i in range(2 * lead, 2 * (lead + SLOTS)):
                            split_weights(nm, half, i, it)
                            hidden(half, i - LAG, it)
                    for i in range(2 * KH, PIECES):
                        split_weights(nm, half, i)
                        hidden(half, i - LAG)
                        if i - 2 * KH >= LAG:
                            add(half, i - 2 * KH - LAG)
                for o in range(KD - LAG, KD):
                    add(1, o)

            def head_norm(nm):
                for H in head_norms(nm):
                    T = H["tiles"]
                    N = T[0].shape[-1]
                    for t in range(len(T)):
                        if E.new(f"{H['name']}.sum{0 if H['total'] else t}'"):
                            dve.wait_ge(*E.at(f"{H['name']}.sum{0 if H['total'] else t}'"))
                        w = work[0:T[t].shape[0], 0 if H["total"] else t % 2, 0:N]
                        if t == 0 or not H["total"]:
                            V.reciprocal(w, w).then_inc(normed, 1)
                            dve.wait_ge(normed, E.step(normed))
                        V.scalar_tensor_tensor(out=T[t], in0=T[t], scalar=H["gains"][t], in1=w,
                                               op0=ALU.mult, op1=ALU.mult).then_inc(normed, 1)
                        dve.wait_ge(normed, E.step(normed, f"{H['name']}.n{t}"))
                    if H["rope"]:
                        for t in range(len(T)):
                            rope(H["name"], T[t][:, 0:SEQ], C(H["rope"][0]), C(H["rope"][1]), f"{H['name']}.r{t}", SEQ)
                    E.name_last(f"{H['name']}.done")

            dve.wait_ge(s_const, 32)
            for l in range(2):
                nm = f"b1.{l}"
                norm(nm, gain=R(f"{nm}.gain"))
                for br in range(2):
                    for part, buf in (("q", qT[br]), ("k", kT[br])):
                        for j in range(2):
                            rope(nm, flat(buf[:, 2 * j:2 * j + 2, :]), C("cos_part"), C("sin_part"), f"{nm}.r{part}{br}{j}", 512)
                if E.new(f"{nm}.wl.0'"):
                    dve.wait_ge(*E.at(f"{nm}.wl.0'"))
                zz = fz[:, 0, :].rearrange("p (a b) -> p a b", a=2)
                aa = fz[:, 1, :].rearrange("p (a b) -> p a b", a=2)
                V.tensor_tensor(zz, wl[:, :, 8:16], R(f"{nm}.fbias").rearrange("p (a b) -> p a b", a=2), ALU.add).then_inc(combined, 1)
                dve.wait_ge(combined, E.step(combined))
                V.tensor_scalar(fz[:, 1, :], fz[:, 0, :], -1.0, None, ALU.mult).then_inc(combined, 1)
                dve.wait_ge(combined, E.step(combined))
                V.tensor_tensor(aa, aa, zz, ALU.max).then_inc(combined, 1)
                dve.wait_ge(combined, E.step(combined, f"{nm}.z"))
                V.tensor_scalar(wl[:, :, 0:8], wl[:, :, 0:8], float(HEADS ** -0.5 * HD ** -0.5), None, ALU.mult).then_inc(combined, 1)
                dve.wait_ge(combined, E.step(combined))
                for j in range(2):
                    rope(nm, flat(qiT[:, 2 * j:2 * j + 2, :]), C("cos_part"), C("sin_part"), f"{nm}.rqi{j}", 512)
                rope(nm, kiT, C("cos_part")[:, 0:SEQ], C("sin_part")[:, 0:SEQ], f"{nm}.rki", SEQ)
                for hh in range(HEADS):
                    if E.new(f"{nm}.ix{hh}'"):
                        dve.wait_ge(*E.at(f"{nm}.ix{hh}'"))
                    for q in range(QT):
                        rl = work[:, hh % 2, SEQ * q:SEQ * q + SEQ]
                        wcol = wl[:, q, hh:hh + 1]
                        last = f"{nm}.isc{hh}" if q == 1 else None
                        if hh == 0:
                            V.tensor_scalar(isc[:, q, :], rl, wcol, None, ALU.mult).then_inc(combined, 1)
                            dve.wait_ge(combined, E.step(combined, last))
                        else:
                            V.scalar_tensor_tensor(out=isc[:, q, :], in0=rl, scalar=wcol, in1=isc[:, q, :],
                                                   op0=ALU.mult, op1=ALU.add).then_inc(combined, 1)
                            dve.wait_ge(combined, E.step(combined, last))
                V.tensor_tensor(flat(isc), flat(isc), C("causal"), ALU.add).then_inc(combined, 1)
                dve.wait_ge(combined, E.step(combined))
                for q in range(QT):
                    for r in range(TOP // 8):
                        V.max(top8, isc[:, q, :]).then_inc(combined, 1)
                        dve.wait_ge(combined, E.step(combined))
                        V.match_replace(isc[:, q, :], top8, isc[:, q, :], TAKEN).then_inc(combined, 1)
                        dve.wait_ge(combined, E.step(combined))
                V.tensor_scalar(flat(dsa_mask), flat(isc), TAKEN / 2, -BLOCKED, ALU.is_le, ALU.mult).then_inc(combined, 1)
                dve.wait_ge(combined, E.step(combined))
                V.scalar_tensor_tensor(out=flat(dsa_mask), in0=flat(dsa_mask), scalar=BLOCKED, in1=C("causal"),
                                       op0=ALU.add, op1=ALU.add).then_inc(combined, 1)
                dve.wait_ge(combined, E.step(combined))
                if E.new(f"{nm}.ln"):
                    dve.wait_ge(*E.at(f"{nm}.ln"))
                V.tensor_scalar(fz[:, 2, :], fz[:, 0, :], 0.0, None, ALU.min).then_inc(combined, 1)
                dve.wait_ge(combined, E.step(combined))
                V.tensor_tensor(fz[:, 3, :], fz[:, 2, :], fz[:, 3, :], ALU.subtract).then_inc(combined, 1)
                dve.wait_ge(combined, E.step(combined))
                V.tensor_copy(fz[:, 0:2, 0:8], fz[:, 3, :].rearrange("p (a b) -> p a b", a=2)).then_inc(combined, 1)
                dve.wait_ge(combined, E.step(combined, f"{nm}.logf"))
                b = bank(f"{nm}.cs", SEQ + 16)
                V.memset(csT, 0.0).then_inc(combined, 1)
                dve.wait_ge(combined, E.step(combined))
                V.tensor_copy(csT[0:8, :], b[0:8, 0:SEQ]).then_inc(combined, 1)
                dve.wait_ge(combined, E.step(combined))
                V.tensor_copy(flat(cq), b[:, SEQ:SEQ + 16]).then_inc(combined, 1)
                dve.wait_ge(combined, E.step(combined, f"{nm}.cs'"))
                attention(f"{nm}.att")
                for n in range(3):
                    for j in range(2):
                        for i in range(2):
                            lab = f"{nm}.y{n}{j}.{i}"
                            k = 4 * j + 2 * i
                            if E.new(f"{nm}.m{(KD * n + k) // 2}.0'"):
                                dve.wait_ge(*E.at(f"{nm}.m{(KD * n + k) // 2}.0'"))
                            b = bank(lab)
                            mg, gt = flat(merged[:, k:k + 2, :]), flat(gates((KD * n + k) // 2))
                            V.scalar_tensor_tensor(out=mg if n == 0 else gt, in0=gt, scalar=1.0, in1=b,
                                                   op0=ALU.add, op1=ALU.mult).then_inc(combined, 1)
                            dve.wait_ge(combined, E.step(combined, lab + "'"))
                            if n:
                                V.tensor_tensor(mg, mg, gt, ALU.add).then_inc(combined, 1)
                                dve.wait_ge(combined, E.step(combined, f"{nm}.mg{k // 2}" if n == 2 else None))
                for j in range(4):
                    lab = f"{nm}.out{j}.0"
                    xv = x[:, 2 * j:2 * j + 2, 0:SEQ]
                    V.scalar_tensor_tensor(out=xv, in0=bank(lab).rearrange("p (a b) -> p a b", a=2), scalar=0.5, in1=xv,
                                           op0=ALU.mult, op1=ALU.add).then_inc(combined, 1)
                    dve.wait_ge(combined, E.step(combined, lab + "'"))
                    for k in (2 * j, 2 * j + 1):
                        E.name_last(f"{nm}.out.x{k}")
            norm("final", gain=R("final"), to="x")
            add_mod_bias(0, 0, 12)
            prepare("b2.0.n1", 0, 0, "b2.0.ffn1_norm")
            ffn_weights("b2.0.ffn1")
            norm("b2.0.n1", split=True)
            ffn("b2.0.ffn1", 0, TOK, 0)
            add_mod_bias(0, 12, 24)
            prepare("b2.0.nm", 0, 1, "b2.0.mix_norm")
            norm("b2.0.nm")
            if E.new("b2.0.ffn1_out.x7"):
                dve.wait_ge(*E.at("b2.0.ffn1_out.x7"))
            V.memset(m_y.rearrange("p a b c -> p (a b c)"), 0.0).then_inc(combined, 1)
            dve.wait_ge(combined, E.step(combined))
            for i in range(4):
                if E.new(f"b2.0.in.{10 + i}'"):
                    dve.wait_ge(*E.at(f"b2.0.in.{10 + i}'"))
                V.tensor_tensor(m_y[:, i, :, PAD:PAD + SEQ], m_ca[:, i, :].rearrange("p (g s) -> p g s", g=2),
                                squares[:, i, :].rearrange("p (g s) -> p g s", g=2), ALU.mult).then_inc(combined, 1)
                dve.wait_ge(combined, E.step(combined, f"b2.0.conv.glu{i}"))
            head_norm("b2.0.lora")
            head_norm("b2.0.heads")
            attention("b2.0.att")
            b = bank("b2.0.conv.mean")
            V.tensor_scalar(work[:, 0, :], b, -1.0 / 512, None, ALU.mult).then_inc(combined, 1)
            dve.wait_ge(combined, E.step(combined, "b2.0.conv.mean'"))
            for t in range(4):
                V.tensor_tensor(m_yc[:, t, :], m_yc[:, t, :], work[:, 0, :], ALU.add).then_inc(combined, 1)
                dve.wait_ge(combined, E.step(combined, f"b2.0.conv.c{t}"))
            if E.new("b2.0.conv.var'"):
                dve.wait_ge(*E.at("b2.0.conv.var'"))
            V.reciprocal(rs[:, :], rs[:, :]).then_inc(combined, 1)
            dve.wait_ge(combined, E.step(combined))
            for t in range(4):
                V.tensor_tensor(m_yc[:, t, :], m_yc[:, t, :], rs[:, :], ALU.mult).then_inc(combined, 1)
                dve.wait_ge(combined, E.step(combined, f"b2.0.conv.n{t}"))

            def add_mixer(nm, l, groups, per):
                for i in range(KD):
                    b = psum[:, E.bank(f"{nm}.out.{i // per}"), :]
                    if E.new(f"{nm}.out.{i // per}"):
                        dve.wait_ge(*E.at(f"{nm}.out.{i // per}"))
                    off = (i % per) * SEQ if per > 1 else 0
                    for g in range(groups):
                        xv = x[:, i, SEQ * g:SEQ * g + SEQ]
                        lab = f"{nm}.out.{i // per}'" if g == groups - 1 and i % per == per - 1 else None
                        V.scalar_tensor_tensor(out=xv, in0=b[:, off + SEQ * g:off + SEQ * g + SEQ],
                                               scalar=mods[:, l, 40 + i, g:g + 1], in1=xv,
                                               op0=ALU.mult, op1=ALU.add).then_inc(mixer_added, 1)
                        dve.wait_ge(mixer_added, E.step(mixer_added, lab))
                    E.name_last(f"{nm}.out.x{i}")

            add_mixer("b2.0", 0, 2, 1)
            add_mod_bias(0, 24, 36)
            prepare("b2.0.n2", 0, 2, "b2.0.ffn2_norm")
            ffn_weights("b2.0.ffn2")
            norm("b2.0.n2", split=True)
            ffn("b2.0.ffn2", 0, TOK, 2)
            add_mod_bias(1, 0, 12)
            prepare("b2.1.n1", 1, 0, "b2.1.ffn1_norm")
            ffn_weights("b2.1.ffn1")
            norm("b2.1.n1", split=True)
            ffn("b2.1.ffn1", 1, TOK, 0)
            add_mod_bias(1, 12, 24)
            prepare("b2.1.nm", 1, 1, "b2.1.mix_norm")
            norm("b2.1.nm")
            V.tensor_scalar(R("nq_gain"), R("nq_gain"), HD ** -0.5, None, ALU.mult).then_inc(combined, 1)
            dve.wait_ge(combined, E.step(combined))
            head_norm("b2.1.heads")
            dve.wait_ge(s_bias, 16 * 4 * HEADS)
            for i in range(2 * HEADS):
                q = i % 2
                V.tensor_tensor(g_bias[:, i, :], g_bias[:, i, :], C("window")[:, SEQ * q:SEQ * q + SEQ], ALU.add).then_inc(combined, 1)
                dve.wait_ge(combined, E.step(combined))
            attention("b2.1.att")
            add_mixer("b2.1", 1, 1, 2)
            add_mod_bias(1, 24, 36)
            prepare("b2.1.n2", 1, 2, "b2.1.ffn2_norm")
            ffn_weights("b2.1.ffn2")
            norm("b2.1.n2", split=True)
            ffn("b2.1.ffn2", 1, SEQ, 2)
            E.name_last("last.h7")




def chunked(w, cols):
    k, n = w.shape[0] // P, w.shape[1] // cols
    return np.ascontiguousarray(w.reshape(k, P, n, cols).transpose(2, 1, 0, 3)).reshape(n, P, k * cols)


def by_feature(v):
    return v.reshape(-1, P).T


def constants():
    out = {n: np.zeros((P, w), np.float32) for n, (_, w) in CONST.items()}
    i = np.arange(P)
    out["ident"][:] = np.eye(P)
    out["ones"][:] = 1
    out["sum64"][:] = i[:, None] // 64 == i[None, :] // 64
    out["sum32"][:] = i[:, None] // 32 == i[None, :] // 32
    out["sum96"][0:64, 0:64] = 1 / 64
    out["sum96"][64:96, 64:96] = 1 / 32
    for b in (0, HD):
        for j in range(8):
            out["rot_half"][b + j + 8, b + j] = -1
            out["rot_half"][b + j, b + j + 8] = 1
    for j in range(0, P, 2):
        for name in ("rot_pair",) + (("rot_q",) if 64 <= j < 96 else ()):
            out[name][j + 1, j] = -1
            out[name][j, j + 1] = 1
    pos = np.arange(SEQ, dtype=np.float32)
    inv = np.power(np.float32(500000.0), -np.arange(0, 16, 2, dtype=np.float32) / 16).astype(np.float32)
    ang = (pos[:, None] * inv[None, :]).astype(np.float32)
    c, s = np.ones((P, SEQ), np.float32), np.zeros((P, SEQ), np.float32)
    for b in (0, HD):
        c[b:b + 16] = np.concatenate([np.cos(ang), np.cos(ang)], 1).T
        s[b:b + 16] = np.concatenate([np.sin(ang), np.sin(ang)], 1).T
    out["cos_part"][:], out["sin_part"][:] = np.tile(c, (1, 2)), np.tile(s, (1, 2))
    for dim, name, rows in ((64, "64", slice(0, P)), (32, "96", slice(64, 96))):
        n = dim // 4
        inv = (10000.0 ** (-np.arange(n, dtype=np.float32) / n)).astype(np.float32)
        t = np.arange(SEQ)
        row, col = (t // 64).astype(np.float32), (t % 64).astype(np.float32)
        ang = np.concatenate([row[:, None] * inv, col[:, None] * inv], -1).astype(np.float32)
        out["cos" + name][:] = 1
        out["cos" + name][rows] = np.tile(np.repeat(np.cos(ang).T, 2, 0), (P // dim, 1))[rows]
        out["sin" + name][rows] = np.tile(np.repeat(np.sin(ang).T, 2, 0), (P // dim, 1))[rows]
    q = np.arange(QT)[:, None] * P + i[None, :]
    k = np.arange(SEQ)
    causal = np.where(k[None, None, :] <= q[:, :, None], 0, BLOCKED)
    out["causal"][:] = causal.transpose(1, 0, 2).reshape(P, -1)
    cs = np.clip(q % 64 - 8, 0, 48)
    inside = (k % 64 >= cs[:, :, None]) & (k % 64 < cs[:, :, None] + 16)
    out["window"][:] = np.where(inside, 0, BLOCKED).transpose(1, 0, 2).reshape(P, -1)
    out["upto"][:] = (q[:, :, None] <= k[None, None, :]).astype(np.float32).transpose(1, 0, 2).reshape(P, -1)
    out["eps"][:], out["one"][:] = EPS, 1
    return np.concatenate([out[n] for n in CONST], 1)


def lay_out(I):
    W = {}
    for l in range(2):
        w = I["w_in"][l]
        for br in range(3):
            for i, part in enumerate("qkvg"):
                a = WIDTH * (4 * br + i)
                W[f"b1.{l}.{part}{br}"] = chunked(w[:, a:a + WIDTH], 256)
        W[f"b1.{l}.qi"] = chunked(w[:, 6144:6656], 256)
        ki = w[:, 6656:6720]
        W[f"b1.{l}.misc"] = chunked(np.concatenate([ki, ki, w[:, 6720:6736]], 1), 144)
        W[f"b1.{l}.merge"] = chunked(w[:, 6736:], 256)
        W[f"b1.{l}.branch"] = np.concatenate([chunked(I["w_branch"][l, n], 512) for n in range(3)])
        W[f"b1.{l}.out"] = chunked(I["w_out"][l], 256)
        g = lambda n: I[f"l{l}_{n}_2"]
        W[f"mod{l}"] = chunked(g("mod_w"), 256)
        for f in ("ffn1", "ffn2"):
            w2 = g(f + "_w_in").reshape(D, 2, KF, P).transpose(0, 2, 1, 3).reshape(D, 2 * D_FF)
            W[f"b2.{l}.{f}_in0"], W[f"b2.{l}.{f}_in1"] = np.split(chunked(w2, 256), 2)
            for half in range(2):
                W[f"b2.{l}.{f}_out{half}"] = chunked(g(f + "_w_out")[KH * P * half:KH * P * (half + 1)], P)
    w = I["l0_w_in_2"]
    W["b2.0.in"] = chunked(np.concatenate([w[:, :256]] + [w[:, 256:288]] * 4 + [w[:, 288:]], 1), 256)
    W["b2.0.uq"] = chunked(I["l0_mla_w_uq_2"], 384)
    u = I["l0_mla_w_ukv_2"].reshape(256, HEADS, 2, HD).transpose(0, 2, 1, 3).reshape(256, 1024)
    W["b2.0.ukv"] = chunked(u, 1024)
    W["b2.0.out"] = chunked(I["l0_w_out_2"], 256)
    w = I["l1_w_in_2"]
    pairs = [j for i in range(4) for j in (i, i + 4)]
    cq = w[:, 1280:1792].reshape(D, HEADS, HD)[:, pairs].reshape(D, WIDTH)
    W["b2.1.in"] = chunked(np.concatenate([w[:, 0:128], w[:, 256:768], w[:, 128:256], w[:, 768:1280], cq, w[:, 1792:]], 1), 256)
    wo = I["l1_w_out_2"]
    wo = np.concatenate([wo[:WIDTH].reshape(HEADS, HD, D)[pairs].reshape(WIDTH, D), wo[WIDTH:]])
    W["b2.1.out"] = chunked(wo, 256)

    prm = {}
    for l in range(2):
        prm[f"b1.{l}.gain"] = by_feature(I["norm_gain"][l])
        prm[f"b1.{l}.fbias"] = np.tile(I["forget_bias"][l], (P, 2))
        prm[f"b2.{l}.mod_b"] = np.repeat(by_feature(I[f"l{l}_mod_b_2"]), 2, 1)
        for n in ("ffn1_norm", "mix_norm", "ffn2_norm"):
            prm[f"b2.{l}.{n}"] = np.repeat(by_feature(I[f"l{l}_{n}_2"]), 2, 1)
    prm["final"] = by_feature(I["final_gain"])
    prm["q_norm"] = by_feature(I["l0_mla_q_norm_2"])
    prm["kv_norm"] = by_feature(I["l0_mla_kv_norm_2"])
    for n in "qk":
        v = I[f"l0_mla_{n}_gain_2"]
        prm[f"{n}_gain"] = np.concatenate([v, v[64:96]])[:, None]
    prm["glu_b"] = by_feature(I["l0_conv_glu_b_2"])
    prm["dw_w"] = I["l0_conv_dw_w_2"].reshape(TAPS, 4, P).transpose(2, 1, 0).reshape(P, 4 * TAPS)
    prm["dw_b"] = by_feature(I["l0_conv_dw_b_2"])
    prm["ln_g"] = by_feature(I["l0_conv_ln_g_2"])
    prm["ln_b"] = by_feature(I["l0_conv_ln_b_2"])
    for n, f in (("gq", "gqa_q"), ("gk", "gqa_k"), ("nq", "na_q"), ("nk", "na_k")):
        prm[f"{n}_gain"] = np.tile(I[f"l1_{f}_gain_2"], 2)[:, None]
    prm["cond"] = np.stack([by_feature(I["c_2"][0]), by_feature(I["c_ctx_2"])], 2).reshape(P, 2 * KD)
    for n, (_, w_) in PARAM.items():
        assert prm[n].shape == (P, w_), (n, prm[n].shape)

    onehot = np.zeros((P, 1024), np.float32)
    for hh in range(HEADS):
        onehot[hh, P * hh:P * hh + P] = -1
    wide = np.pad(I["l1_na_rpb_2"], ((0, 0), (0, 0), (48, 48)))
    bias = np.stack([wide[:, :, 63 - c:127 - c] for c in range(64)], 2)
    small = dict(consts=constants(), params=np.concatenate([prm[n] for n in PARAM], 1), onehot=onehot,
                 x=I["x"][0].T.reshape(KD, P, SEQ).transpose(1, 0, 2), ctx=I["ctx_2"][0].T.reshape(KD, P, CTX).transpose(1, 0, 2),
                 bias=bias)
    return W, {n: np.ascontiguousarray(v, np.float32) for n, v in small.items()}


def build(nc, book, shapes):
    t = {n: nc.dram_tensor("in_" + n, s, F32, kind="ExternalInput").ap() for n, s in shapes.items()}
    out = nc.dram_tensor("outT", (P, KD, SEQ), F32, kind="ExternalOutput").ap()
    weights = {s: t["w_" + s.replace(".", "_")] for s, _, _ in weight_plan()}
    program(nc, book, weights, t["consts"], t["params"], t["onehot"], t["x"], t["ctx"], t["bias"], out)


def kernel(**inputs):
    import concourse.bacc as bacc
    from concourse.bass_utils import run_bass_kernel_spmd

    W, arrays = lay_out({n: np.asarray(v) for n, v in inputs.items()})
    for s, v in W.items():
        arrays["w_" + s.replace(".", "_")] = v
    book = None
    for _ in range(2):
        nc = bacc.Bacc("TRN2", target_bir_lowering=False, num_devices=1)
        book = Book(book)
        build(nc, book, {n: v.shape for n, v in arrays.items()})
    r = run_bass_kernel_spmd(nc, [{"in_" + n: v for n, v in arrays.items()}], core_ids=[0])
    y = np.asarray(r.results[0]["outT"])
    return np.ascontiguousarray(y.transpose(1, 0, 2).reshape(D, SEQ).T)[None]
```
